# Optimizing a Trainium2 kernel written in Bass

```python
import math
import jax, jax.numpy as jnp
from jax import lax
import numpy as np

D_MODEL = 1024
BATCH = 1
SEQ = 512
DEPTH = 2

PLE_DIM = 256
N_A_LAYERS = DEPTH // 2
N_B_LAYERS = DEPTH - N_A_LAYERS
GDN_HEADS = 8
GDN_HEAD_DIM = 128
GDN_WIDTH = GDN_HEADS * GDN_HEAD_DIM
CONV_WIDTH = 4
GDN_CHUNK = 64
SB_HEADS = 8
SB_HEAD_DIM = 128
SB_WIDTH = SB_HEADS * SB_HEAD_DIM
SB_BLOCK = 128
FFN_HIDDEN = -(-8 * D_MODEL // (3 * 256)) * 256
EPS = 1e-6


def rms_norm(x, g):
    xf = x.astype(jnp.float32)
    y = xf * lax.rsqrt(jnp.mean(xf * xf, axis=-1, keepdims=True) + EPS)
    return (y * g.astype(jnp.float32)).astype(x.dtype)

def l2_norm(x):
    return x * lax.rsqrt(jnp.sum(x * x, axis=-1, keepdims=True) + EPS)

def causal_conv(x, w):
    k_w, c = w.shape
    return lax.conv_general_dilated(x, w[:, None, :], window_strides=(1,), padding=[(k_w - 1, 0)],
                                    dimension_numbers=('NWC', 'WIO', 'NWC'), feature_group_count=c)

def to_chunks(t):
    b, s, h = t.shape[:3]
    t = t.reshape((b, s // GDN_CHUNK, GDN_CHUNK, h) + t.shape[3:])
    return jnp.swapaxes(t, 2, 3)

def gated_delta_rule(q, k, v, g, beta):
    b_, s_, h_, dk = q.shape
    dv = v.shape[-1]
    c = GDN_CHUNK
    q, k, v, g, beta = to_chunks(q), to_chunks(k), to_chunks(v), to_chunks(g), to_chunks(beta)
    G = jnp.cumsum(g, axis=-1)
    causal = jnp.tril(jnp.ones((c, c), dtype=bool))
    strict = jnp.tril(jnp.ones((c, c), dtype=bool), -1)
    decay_mat = jnp.exp(jnp.where(causal, G[..., :, None] - G[..., None, :], -jnp.inf))
    kk = jnp.einsum('bnhrd,bnhsd->bnhrs', k, k)
    a_low = jnp.where(strict, beta[..., None] * kk * decay_mat, 0.0)
    eye = jnp.eye(c, dtype=q.dtype)
    rhs = jnp.concatenate([v * beta[..., None], k * (beta * jnp.exp(G))[..., None]], axis=-1)
    sol = lax.linalg.triangular_solve(a_low + eye, rhs, left_side=True, lower=True, unit_diagonal=True)
    u, w = sol[..., :dv], sol[..., dv:]
    qk = jnp.einsum('bnhrd,bnhsd->bnhrs', q, k) * decay_mat
    q_dec = q * jnp.exp(G)[..., None]
    k_dec = k * jnp.exp(G[..., -1:] - G)[..., None]
    g_last = jnp.exp(G[..., -1])

    def step(state, xs):
        q_c, k_c, qk_c, u_c, w_c, gl_c = xs
        v_new = u_c - jnp.einsum('bhcd,bhde->bhce', w_c, state)
        o = jnp.einsum('bhcd,bhde->bhce', q_c, state) + jnp.einsum('bhrs,bhse->bhre', qk_c, v_new)
        state = state * gl_c[..., None, None] + jnp.einsum('bhcd,bhce->bhde', k_c, v_new)
        return state, o

    xs = tuple(jnp.moveaxis(t, 1, 0) for t in (q_dec, k_dec, qk, u, w, g_last))
    s0 = jnp.zeros((b_, h_, dk, dv), q.dtype)
    _, o = lax.scan(step, s0, xs)
    return o.transpose(1, 0, 3, 2, 4).reshape(b_, s_, h_, dv)

def gdn_mixer(hn, w_in, w_conv, a_log, dt_bias, norm_g, w_out):
    b_, s_, _ = hn.shape
    proj = hn @ w_in
    qkv = jax.nn.silu(causal_conv(proj[..., :3 * GDN_WIDTH], w_conv))
    gate = proj[..., 3 * GDN_WIDTH:4 * GDN_WIDTH].reshape(b_, s_, GDN_HEADS, GDN_HEAD_DIM)
    a_in = proj[..., 4 * GDN_WIDTH:4 * GDN_WIDTH + GDN_HEADS].astype(jnp.float32)
    b_in = proj[..., 4 * GDN_WIDTH + GDN_HEADS:].astype(jnp.float32)
    qkv = qkv.astype(jnp.float32).reshape(b_, s_, 3, GDN_HEADS, GDN_HEAD_DIM)
    q = l2_norm(qkv[:, :, 0]) * (GDN_HEAD_DIM ** -0.5)
    k = l2_norm(qkv[:, :, 1])
    v = qkv[:, :, 2]
    beta = jax.nn.sigmoid(b_in)
    g = -jnp.exp(a_log.astype(jnp.float32)) * jax.nn.softplus(a_in + dt_bias.astype(jnp.float32))
    o = gated_delta_rule(q, k, v, g, beta).astype(hn.dtype)
    o = rms_norm(o, norm_g) * jax.nn.silu(gate)
    return o.reshape(b_, s_, GDN_WIDTH) @ w_out

def shared_kv(h, kv_norm, w_kv, k_norm):
    b_, s_, _ = h.shape
    kv = (rms_norm(h, kv_norm) @ w_kv).reshape(b_, s_, 2, SB_HEADS, SB_HEAD_DIM)
    k = rms_norm(kv[:, :, 0], k_norm).transpose(0, 2, 1, 3)
    v = kv[:, :, 1].transpose(0, 2, 1, 3)
    return k, v

def stick_breaking(q, k, v):
    s_ = q.shape[2]
    outs = []
    for blk in range(s_ // SB_BLOCK):
        t0, t1 = blk * SB_BLOCK, (blk + 1) * SB_BLOCK
        z = jnp.einsum('bhtd,bhsd->bhts', q[:, :, t0:t1], k[:, :, :t1]).astype(jnp.float32)
        t_idx = t0 + jnp.arange(SB_BLOCK)[:, None]
        s_idx = jnp.arange(t1)[None, :]
        mask = s_idx < t_idx
        log_not = jnp.where(mask, jax.nn.log_sigmoid(-z), 0.0)
        suffix = lax.cumsum(log_not, axis=3, reverse=True) - log_not
        log_w = jnp.where(mask, jax.nn.log_sigmoid(z) + suffix, -jnp.inf)
        wgt = jnp.exp(log_w).astype(v.dtype)
        outs.append(jnp.einsum('bhts,bhsd->bhtd', wgt, v[:, :, :t1]))
    return jnp.concatenate(outs, axis=2)

def sb_mixer(hn, k_sh, v_sh, w_q, q_norm, w_out):
    b_, s_, _ = hn.shape
    q = (hn @ w_q).reshape(b_, s_, SB_HEADS, SB_HEAD_DIM)
    q = (rms_norm(q, q_norm) * (SB_HEAD_DIM ** -0.5)).transpose(0, 2, 1, 3)
    o = stick_breaking(q, k_sh, v_sh)
    return o.transpose(0, 2, 1, 3).reshape(b_, s_, SB_WIDTH) @ w_out

def swiglu(hn, w_in, w_out):
    gu = hn @ w_in
    return (jax.nn.silu(gu[..., :FFN_HIDDEN]) * gu[..., FFN_HIDDEN:]) @ w_out

def first_inputs(seed: int = 0) -> dict:
    key = jax.random.key(seed)
    ks = jax.random.split(key, 24)
    f32 = jnp.float32

    def nrm(k, shape, fan_in):
        return jax.random.normal(k, shape, f32) * (fan_in ** -0.5)

    def gain(k, shape):
        return 1.0 + 0.02 * jax.random.normal(k, shape, f32)

    dt = jnp.exp(jax.random.uniform(ks[8], (N_A_LAYERS, GDN_HEADS), f32, math.log(1e-3), math.log(1e-1)))
    return {
        "x": jax.random.normal(ks[0], (BATCH, SEQ, D_MODEL), f32),
        "p": jax.random.normal(ks[1], (DEPTH, BATCH, SEQ, PLE_DIM), f32),
        "ln_mix": gain(ks[2], (DEPTH, D_MODEL)),
        "ln_ffn": gain(ks[3], (DEPTH, D_MODEL)),
        "ln_ple": gain(ks[4], (DEPTH, D_MODEL)),
        "gdn_w_in": nrm(ks[5], (N_A_LAYERS, D_MODEL, 4 * GDN_WIDTH + 2 * GDN_HEADS), D_MODEL),
        "gdn_conv": nrm(ks[6], (N_A_LAYERS, CONV_WIDTH, 3 * GDN_WIDTH), CONV_WIDTH),
        "gdn_a_log": jnp.log(jax.random.uniform(ks[7], (N_A_LAYERS, GDN_HEADS), f32, 1.0, 16.0)),
        "gdn_dt_bias": dt + jnp.log(-jnp.expm1(-dt)),
        "gdn_norm": gain(ks[9], (N_A_LAYERS, GDN_HEAD_DIM)),
        "gdn_w_out": nrm(ks[10], (N_A_LAYERS, GDN_WIDTH, D_MODEL), GDN_WIDTH),
        "kv_norm": gain(ks[11], (D_MODEL,)),
        "w_kv": nrm(ks[12], (D_MODEL, 2 * SB_WIDTH), D_MODEL),
        "k_norm": gain(ks[13], (SB_HEAD_DIM,)),
        "sb_w_q": nrm(ks[14], (N_B_LAYERS, D_MODEL, SB_WIDTH), D_MODEL),
        "sb_q_norm": gain(ks[15], (N_B_LAYERS, SB_HEAD_DIM)),
        "sb_w_out": nrm(ks[16], (N_B_LAYERS, SB_WIDTH, D_MODEL), SB_WIDTH),
        "ffn_w_in": nrm(ks[17], (DEPTH, D_MODEL, 2 * FFN_HIDDEN), D_MODEL),
        "ffn_w_out": nrm(ks[18], (DEPTH, FFN_HIDDEN, D_MODEL), FFN_HIDDEN),
        "ple_w_proj": nrm(ks[19], (DEPTH, PLE_DIM, D_MODEL), PLE_DIM),
        "ple_w_gate": nrm(ks[20], (DEPTH, D_MODEL, D_MODEL), D_MODEL),
    }

def first_block(x, p, ln_mix, ln_ffn, ln_ple, gdn_w_in, gdn_conv, gdn_a_log, gdn_dt_bias, gdn_norm,
              gdn_w_out, kv_norm, w_kv, k_norm, sb_w_q, sb_q_norm, sb_w_out, ffn_w_in, ffn_w_out,
              ple_w_proj, ple_w_gate):
    h = x
    k_sh, v_sh = None, None
    for i in range(DEPTH):
        hn = rms_norm(h, ln_mix[i])
        if i < N_A_LAYERS:
            h = h + gdn_mixer(hn, gdn_w_in[i], gdn_conv[i], gdn_a_log[i], gdn_dt_bias[i],
                              gdn_norm[i], gdn_w_out[i])
        else:
            j = i - N_A_LAYERS
            h = h + sb_mixer(hn, k_sh, v_sh, sb_w_q[j], sb_q_norm[j], sb_w_out[j])
        h = h + swiglu(rms_norm(h, ln_ffn[i]), ffn_w_in[i], ffn_w_out[i])
        h = h + (p[i] @ ple_w_proj[i]) * jax.nn.sigmoid(rms_norm(h, ln_ple[i]) @ ple_w_gate[i])
        if i == N_A_LAYERS - 1:
            k_sh, v_sh = shared_kv(h, kv_norm, w_kv, k_norm)
    return h


DEPTH_2 = 1

D_FF = 2816
RMS_EPS = 1e-6
N_DIR = 2
D_HYENA = 512
HYENA_ORDER = 2
HYENA_BANDS = 16
HYENA_EMB = 2 * HYENA_BANDS + 1
HYENA_FFN = 64
HYENA_MIN_DECAY = abs(math.log(1e-2)) / 1.5
HYENA_MAX_DECAY = abs(math.log(1e-2)) / 0.3
FILTER_EPS = 1e-6
D_RWKV = 512
RWKV_HEAD = 64
RWKV_HEADS = D_RWKV // RWKV_HEAD
DECAY_LORA = 64
AAA_LORA = 64
GATE_LORA = 160
GN_EPS = 64e-5
N_HY_IN = 3 * D_HYENA
N_RW_IN = 3 * D_RWKV + N_DIR * (DECAY_LORA + AAA_LORA) + GATE_LORA
N_GATE = 2 * D_MODEL
N_IN = N_HY_IN + N_RW_IN + N_GATE


def _rmsnorm(x, g):
    xf = x.astype(jnp.float32)
    y = xf * lax.rsqrt(jnp.mean(xf * xf, axis=-1, keepdims=True) + RMS_EPS)
    return (y * g.astype(jnp.float32)).astype(x.dtype)

def _swiglu(h, w_gu, w_down):
    gate, up = jnp.split(h @ w_gu, 2, axis=-1)
    return (jax.nn.silu(gate) * up) @ w_down

def _centred_conv3(u, w, b):
    up = jnp.pad(u, ((0, 0), (1, 1), (0, 0)))
    return w[0] * up[:, :-2] + w[1] * up[:, 1:-1] + w[2] * up[:, 2:] + b

def _centred_token_shift(u, mu):
    prev = jnp.pad(u, ((0, 0), (1, 0), (0, 0)))[:, :-1]
    nxt = jnp.pad(u, ((0, 0), (0, 1), (0, 0)))[:, 1:]
    return u + mu[0] * (prev - u) + mu[1] * (nxt - u)

def _hyena_filters(L, w1, b1, w2, b2, w3, b3, freq, decay):
    f32 = jnp.float32
    pos = jnp.arange(L, dtype=f32)
    t = (pos / max(L - 1, 1))[:, None]
    ang = (2.0 * math.pi / L) * pos[:, None]
    bands = jnp.linspace(1e-4, HYENA_BANDS - 1, HYENA_BANDS, dtype=f32)[None, :]
    feats = jnp.concatenate([t, jnp.cos(bands * ang), -jnp.sin(bands * ang)], axis=-1)
    fr = freq.astype(f32)
    h = jnp.sin(fr * (feats @ w1.astype(f32) + b1.astype(f32)))
    h = jnp.sin(fr * (h @ w2.astype(f32) + b2.astype(f32)))
    h = h @ w3.astype(f32) + b3.astype(f32)
    h = h.reshape(L, N_DIR, HYENA_ORDER, D_HYENA)
    h = h * jnp.exp(-t[:, :, None, None] * jnp.abs(decay.astype(f32))[None])
    fwd, bwd = h[:, 0], h[:, 1]
    zero = jnp.zeros((1, HYENA_ORDER, D_HYENA), f32)
    k = jnp.concatenate([fwd, zero, jnp.flip(bwd[1:], axis=0)], axis=0)
    k = k * lax.rsqrt(jnp.sum(k * k, axis=0, keepdims=True) + FILTER_EPS)
    return k

def _long_conv(z, k_f, d, L):
    zf = jnp.fft.rfft(z, n=2 * L, axis=1)
    y = jnp.fft.irfft(zf * k_f[None], n=2 * L, axis=1)[:, :L]
    return y + d * z

def _hyena_branch(u, conv_w, conv_b, w1, b1, w2, b2, w3, b3, freq, decay, bias_d, w_o):
    out_dtype = u.dtype
    L = u.shape[1]
    uc = _centred_conv3(u, conv_w, conv_b).astype(jnp.float32)
    x1, x2, v = jnp.split(uc, 3, axis=-1)
    k = _hyena_filters(L, w1, b1, w2, b2, w3, b3, freq, decay)
    k_f = jnp.fft.rfft(k, axis=0)
    d = bias_d.astype(jnp.float32)
    z = x1 * _long_conv(v, k_f[:, 0], d[0], L)
    z = x2 * _long_conv(z, k_f[:, 1], d[1], L)
    return z.astype(out_dtype) @ w_o

def _time_major_pair(fwd, bwd):
    return jnp.moveaxis(jnp.stack([fwd, jnp.flip(bwd, axis=1)], axis=0), 2, 0)

def _rwkv7_step(S, inp):
    r, w, k, v, kk, a = inp
    sa = jnp.einsum('dbhij,dbhj->dbhi', S, -kk)
    S = S * w[..., None, :] + sa[..., None] * (kk * a)[..., None, :] + v[..., None] * k[..., None, :]
    y = jnp.einsum('dbhij,dbhj->dbhi', S, r)
    return S, y

def _rwkv7_branch(u, mu, w0, w2, a0, a2, g2, k_k, k_a, r_k, ln_w, ln_b, w_o):
    out_dtype = u.dtype
    B, L, _ = u.shape
    H, N = RWKV_HEADS, RWKV_HEAD
    f32 = jnp.float32
    u = _centred_token_shift(u, mu).astype(f32)
    splits = [D_RWKV, 2 * D_RWKV, 3 * D_RWKV, 3 * D_RWKV + N_DIR * DECAY_LORA,
              3 * D_RWKV + N_DIR * (DECAY_LORA + AAA_LORA)]
    r, k, v, wd, ad, gd = jnp.split(u, splits, axis=-1)
    wd = wd.reshape(B, L, N_DIR, DECAY_LORA)
    ad = ad.reshape(B, L, N_DIR, AAA_LORA)
    w = -jax.nn.softplus(-(w0 + jnp.einsum('bldr,drc->bldc', jnp.tanh(wd), w2))) - 0.5
    decay = jnp.exp(-jnp.exp(w))
    a = jax.nn.sigmoid(a0 + jnp.einsum('bldr,drc->bldc', ad, a2))
    g = jax.nn.sigmoid(gd) @ g2
    kk = (k * k_k).reshape(B, L, H, N)
    kk = kk / jnp.maximum(jnp.sqrt(jnp.sum(kk * kk, axis=-1, keepdims=True)), 1e-12)
    k_dir = k[:, :, None, :] * (1.0 + (a - 1.0) * k_a)

    def heads(t):
        return t.reshape(t.shape[:-1] + (H, N))

    r_h, v_h = heads(r), heads(v)
    decay_h, a_h, k_h = heads(decay), heads(a), heads(k_dir)
    seq = (_time_major_pair(r_h, r_h),
           _time_major_pair(decay_h[:, :, 0], decay_h[:, :, 1]),
           _time_major_pair(k_h[:, :, 0], k_h[:, :, 1]),
           _time_major_pair(v_h, v_h),
           _time_major_pair(kk, kk),
           _time_major_pair(a_h[:, :, 0], a_h[:, :, 1]))
    S0 = jnp.zeros((N_DIR, B, H, N, N), f32)
    _, ys = lax.scan(_rwkv7_step, S0, seq)
    y = jnp.moveaxis(ys[:, 0] + jnp.flip(ys[:, 1], axis=0), 0, 1)
    mean = jnp.mean(y, axis=-1, keepdims=True)
    var = jnp.mean(jnp.square(y - mean), axis=-1, keepdims=True)
    y = ((y - mean) * lax.rsqrt(var + GN_EPS)).reshape(B, L, D_RWKV) * ln_w + ln_b
    bonus = jnp.sum(r_h[:, :, None] * k_h * r_k, axis=-1, keepdims=True)
    y = y + (jnp.sum(bonus, axis=2) * v_h).reshape(B, L, D_RWKV)
    y = y * g
    return y.astype(out_dtype) @ w_o

def second_inputs(seed: int = 0) -> dict:
    key = jax.random.key(seed)
    ks = jax.random.split(key, 35)
    f32 = jnp.float32

    def nrm(i, shape, scale):
        return scale * jax.random.normal(ks[i], shape, f32)

    hy_decay_base = jnp.linspace(HYENA_MIN_DECAY, HYENA_MAX_DECAY, D_HYENA, dtype=f32)
    rw_w0_base = jnp.linspace(-6.0, -1.0, D_RWKV, dtype=f32)
    return {
        "x": nrm(0, (BATCH, SEQ, D_MODEL), 1.0),
        "ffn1_norm": 1.0 + nrm(1, (D_MODEL,), 0.05),
        "ffn1_w_gu": nrm(2, (D_MODEL, 2 * D_FF), D_MODEL ** -0.5),
        "ffn1_w_down": nrm(3, (D_FF, D_MODEL), D_FF ** -0.5),
        "mix_norm": 1.0 + nrm(4, (D_MODEL,), 0.05),
        "w_in": nrm(5, (D_MODEL, N_IN), D_MODEL ** -0.5),
        "hy_conv_w": nrm(6, (3, N_HY_IN), 3 ** -0.5),
        "hy_conv_b": nrm(7, (N_HY_IN,), 0.02),
        "hy_ffn_w1": nrm(8, (HYENA_EMB, HYENA_FFN), HYENA_EMB ** -0.5),
        "hy_ffn_b1": nrm(9, (HYENA_FFN,), 0.1),
        "hy_ffn_w2": nrm(10, (HYENA_FFN, HYENA_FFN), HYENA_FFN ** -0.5),
        "hy_ffn_b2": nrm(11, (HYENA_FFN,), 0.1),
        "hy_ffn_w3": nrm(12, (HYENA_FFN, N_DIR * HYENA_ORDER * D_HYENA), HYENA_FFN ** -0.5),
        "hy_ffn_b3": nrm(13, (N_DIR * HYENA_ORDER * D_HYENA,), 0.1),
        "hy_sin_freq": 1.0 + nrm(14, (HYENA_FFN,), 0.1),
        "hy_decay": hy_decay_base + nrm(15, (N_DIR, HYENA_ORDER, D_HYENA), 0.1),
        "hy_bias_d": nrm(16, (HYENA_ORDER, D_HYENA), 0.5),
        "hy_out": nrm(17, (D_HYENA, D_MODEL), D_HYENA ** -0.5),
        "rw_mu": jax.random.uniform(ks[18], (2, N_RW_IN), f32, 0.0, 0.5),
        "rw_w0": rw_w0_base + nrm(19, (N_DIR, D_RWKV), 0.1),
        "rw_w2": nrm(20, (N_DIR, DECAY_LORA, D_RWKV), 0.1),
        "rw_a0": nrm(21, (N_DIR, D_RWKV), 0.3),
        "rw_a2": nrm(22, (N_DIR, AAA_LORA, D_RWKV), 0.1),
        "rw_g2": nrm(23, (GATE_LORA, D_RWKV), GATE_LORA ** -0.5),
        "rw_k_k": 0.85 + nrm(24, (D_RWKV,), 0.05),
        "rw_k_a": 1.0 + nrm(25, (D_RWKV,), 0.05),
        "rw_r_k": nrm(26, (RWKV_HEADS, RWKV_HEAD), 0.1),
        "rw_ln_w": 1.0 + nrm(27, (D_RWKV,), 0.05),
        "rw_ln_b": nrm(28, (D_RWKV,), 0.02),
        "rw_out": nrm(29, (D_RWKV, D_MODEL), D_RWKV ** -0.5),
        "w_out": nrm(30, (D_MODEL, D_MODEL), D_MODEL ** -0.5),
        "ffn2_norm": 1.0 + nrm(31, (D_MODEL,), 0.05),
        "ffn2_w_gu": nrm(32, (D_MODEL, 2 * D_FF), D_MODEL ** -0.5),
        "ffn2_w_down": nrm(33, (D_FF, D_MODEL), D_FF ** -0.5),
        "final_norm": 1.0 + nrm(34, (D_MODEL,), 0.05),
    }

def second_block(x, ffn1_norm, ffn1_w_gu, ffn1_w_down, mix_norm, w_in, hy_conv_w, hy_conv_b,
              hy_ffn_w1, hy_ffn_b1, hy_ffn_w2, hy_ffn_b2, hy_ffn_w3, hy_ffn_b3, hy_sin_freq,
              hy_decay, hy_bias_d, hy_out, rw_mu, rw_w0, rw_w2, rw_a0, rw_a2, rw_g2, rw_k_k,
              rw_k_a, rw_r_k, rw_ln_w, rw_ln_b, rw_out, w_out, ffn2_norm, ffn2_w_gu,
              ffn2_w_down, final_norm):
    split_at = [N_HY_IN, N_HY_IN + N_RW_IN, N_HY_IN + N_RW_IN + D_MODEL]
    for _ in range(DEPTH_2):
        x = x + 0.5 * _swiglu(_rmsnorm(x, ffn1_norm), ffn1_w_gu, ffn1_w_down)
        h = _rmsnorm(x, mix_norm)
        u_hy, u_rw, g_hy, g_rw = jnp.split(h @ w_in, split_at, axis=-1)
        y_hy = _hyena_branch(u_hy, hy_conv_w, hy_conv_b, hy_ffn_w1, hy_ffn_b1, hy_ffn_w2,
                             hy_ffn_b2, hy_ffn_w3, hy_ffn_b3, hy_sin_freq, hy_decay,
                             hy_bias_d, hy_out)
        y_rw = _rwkv7_branch(u_rw, rw_mu, rw_w0, rw_w2, rw_a0, rw_a2, rw_g2, rw_k_k, rw_k_a,
                             rw_r_k, rw_ln_w, rw_ln_b, rw_out)
        merged = jax.nn.sigmoid(g_hy) * y_hy + jax.nn.sigmoid(g_rw) * y_rw
        x = x + merged @ w_out
        x = x + 0.5 * _swiglu(_rmsnorm(x, ffn2_norm), ffn2_w_gu, ffn2_w_down)
    return _rmsnorm(x, final_norm)


def setup_inputs(seed=0):
    out = dict(first_inputs(seed))
    for name, value in second_inputs(seed + 1).items():
        if name != "x":
            out[name + "_2"] = value
    return out


def reference(
    x, p, ln_mix, ln_ffn, ln_ple, gdn_w_in, gdn_conv, gdn_a_log, gdn_dt_bias, gdn_norm,
    gdn_w_out, kv_norm, w_kv, k_norm, sb_w_q, sb_q_norm, sb_w_out, ffn_w_in, ffn_w_out,
    ple_w_proj, ple_w_gate, ffn1_norm_2, ffn1_w_gu_2, ffn1_w_down_2, mix_norm_2, w_in_2,
    hy_conv_w_2, hy_conv_b_2, hy_ffn_w1_2, hy_ffn_b1_2, hy_ffn_w2_2, hy_ffn_b2_2, hy_ffn_w3_2,
    hy_ffn_b3_2, hy_sin_freq_2, hy_decay_2, hy_bias_d_2, hy_out_2, rw_mu_2, rw_w0_2, rw_w2_2,
    rw_a0_2, rw_a2_2, rw_g2_2, rw_k_k_2, rw_k_a_2, rw_r_k_2, rw_ln_w_2, rw_ln_b_2, rw_out_2,
    w_out_2, ffn2_norm_2, ffn2_w_gu_2, ffn2_w_down_2, final_norm_2,
):
    x = first_block(
        x, p, ln_mix, ln_ffn, ln_ple, gdn_w_in, gdn_conv, gdn_a_log, gdn_dt_bias, gdn_norm,
        gdn_w_out, kv_norm, w_kv, k_norm, sb_w_q, sb_q_norm, sb_w_out, ffn_w_in, ffn_w_out,
        ple_w_proj, ple_w_gate,
    )
    return second_block(
        x, ffn1_norm_2, ffn1_w_gu_2, ffn1_w_down_2, mix_norm_2, w_in_2, hy_conv_w_2,
        hy_conv_b_2, hy_ffn_w1_2, hy_ffn_b1_2, hy_ffn_w2_2, hy_ffn_b2_2, hy_ffn_w3_2,
        hy_ffn_b3_2, hy_sin_freq_2, hy_decay_2, hy_bias_d_2, hy_out_2, rw_mu_2, rw_w0_2,
        rw_w2_2, rw_a0_2, rw_a2_2, rw_g2_2, rw_k_k_2, rw_k_a_2, rw_r_k_2, rw_ln_w_2, rw_ln_b_2,
        rw_out_2, w_out_2, ffn2_norm_2, ffn2_w_gu_2, ffn2_w_down_2, final_norm_2,
    )


_drawn_inputs = setup_inputs


def setup_inputs(seed=0):
    import zlib

    import numpy as np

    out = dict(_drawn_inputs(seed))
    spreads = {}
    factors = {'ln_ffn': 2.996,
     'ln_ple': 33.27,
     'gdn_norm': 3.526,
     'kv_norm': 4.689,
     'k_norm': 8.0,
     'sb_q_norm': 8.0,
     'ffn1_norm_2': 3.922,
     'rw_w2_2': 5.85,
     'rw_a0_2': 3.274,
     'rw_k_k_2': 175.245,
     'rw_k_a_2': 21.95,
     'rw_ln_w_2': 39.335,
     'rw_ln_b_2': 64.0,
     'ffn2_norm_2': 5.167,
     'hy_conv_b_2': 26.103,
     'hy_ffn_b1_2': 3.421,
     'hy_ffn_b2_2': 2.826,
     'hy_sin_freq_2': 5.809,
     'hy_ffn_b3_2': 3.948,
     'hy_decay_2': 4.111}
    for name, (base, spread) in spreads.items():
        noise = np.random.default_rng([zlib.crc32(name.encode()), seed]).standard_normal(out[name].shape)
        drawn = base * np.exp(spread * noise) if base else spread * noise
        out[name] = __import__('jax').numpy.asarray(drawn.astype(out[name].dtype))
    for name, factor in factors.items():
        out[name] = (out[name] * factor).astype(out[name].dtype)
    return out
```

```python
import numpy as np
from contextlib import ExitStack

import concourse.bass as bass
from concourse import mybir

ALU = mybir.AluOpType
ACT = mybir.ActivationFunctionType
AX = mybir.AxisListType
F32 = mybir.dt.float32
F32R = mybir.dt.float32r

P = 128
T = 512
DM = 1024
KD = DM // P
HEADS = 8
HID = 2816
KH = HID // P
EPS = 1e-6
WK, WN = 8, 256
WT = WK * WN
DR = 512
C7 = 64
SCALE = P ** -0.5


def weight_plan():
    plan = []

    def block(name, r0, rows, c0, cols):
        plan.append((name, [(r0 + k * P, c0, k, 0, P, cols) for k in range(rows // P)]))

    def columns(name, c0, cols, rows=DM):
        for c in range(c0, c0 + cols, WN):
            block(name, 0, rows, c, min(WN, c0 + cols - c))

    def ffn(w_in, w_out):
        for g in range(HID // WN):
            block(w_in, 0, DM, g * WN, WN)
            block(w_in, 0, DM, HID + g * WN, WN)
        for c in range(0, DM, WN):
            for r in range(0, HID, WK * P):
                block(w_out, r, min(WK * P, HID - r), c, WN)

    def ple(i):
        for c in range(0, DM, WN):
            block(f"ple_w_proj.{i}", 0, 256, c, WN)
            block(f"ple_w_gate.{i}", 0, DM, c, WN)

    columns("gdn_w_in.0", 0, 4 * DM)
    columns("gdn_w_out.0", 0, DM)
    ffn("ffn_w_in.0", "ffn_w_out.0")
    ple(0)
    columns("w_kv", 0, 2 * DM)
    columns("sb_w_q.0", 0, DM)
    columns("sb_w_out.0", 0, DM)
    ffn("ffn_w_in.1", "ffn_w_out.1")
    ple(1)
    ffn("ffn1_w_gu_2", "ffn1_w_down_2")
    columns("w_in_2", 0, 3 * DR)
    columns("w_in_2", 3 * DR, 3 * DR)
    columns("w_in_2", 6 * DR, 256)
    columns("w_in_2", 6 * DR + 256, 160)
    columns("w_in_2", 6 * DR + 416, 2 * DM)
    for c in range(0, DM, WN):
        plan.append(("hy_out_2|rw_out_2", [(k * P, c, k, 0, P, WN) for k in range(DR // P)]
                     + [(k * P, c, DR // P + k, 1, P, WN) for k in range(DR // P)]))
    columns("w_out_2", 0, DM)
    ffn("ffn2_w_gu_2", "ffn2_w_down_2")
    return plan


N_WT = len(weight_plan())

VECTORS = [("ln_mix.0", 8), ("ln_mix.1", 8), ("ln_ffn.0", 8), ("ln_ffn.1", 8), ("ln_ple.0", 8), ("ln_ple.1", 8),
           ("kv_norm", 8), ("ffn1_norm_2", 8), ("mix_norm_2", 8), ("ffn2_norm_2", 8), ("final_norm_2", 8),
           ("gdn_norm.0", 1), ("k_norm", 1), ("sb_q_norm.0", 1),
           ("gdn_conv.0.0", 24), ("gdn_conv.0.1", 24), ("gdn_conv.0.2", 24), ("gdn_conv.0.3", 24),
           ("hy_conv_w_2.0", 12), ("hy_conv_w_2.1", 12), ("hy_conv_w_2.2", 12), ("hy_conv_b_2", 12),
           ("hy_bias_d_2.0", 4), ("hy_bias_d_2.1", 4),
           ("rw_mu_2.0", 16), ("rw_mu_2.1", 16),
           ("rw_w0_2.0", 4), ("rw_w0_2.1", 4), ("rw_a0_2.0", 4), ("rw_a0_2.1", 4),
           ("rw_k_k_2", 4), ("rw_k_a_2", 4), ("rw_r_k_2", 4), ("rw_ln_w_2", 4), ("rw_ln_b_2", 4)]
VCOL = {}
for _name, _n in VECTORS:
    VCOL[_name] = sum(n for _, n in VECTORS[:len(VCOL)])
N_VEC = sum(n for _, n in VECTORS)


class Steps:

    def __init__(self, sem, names):
        self.sem, self.names, self.next = sem, list(names), 0
        assert len(set(self.names)) == len(self.names)

    def start(self, engine):
        engine.sem_inc(self.sem, len(self.names))

    def done(self, step):
        assert self.names[self.next] == step, (self.names[self.next], step)
        self.next = (self.next + 1) % len(self.names)
        return self.sem, 1

    def at(self, step, iteration=0):
        return self.sem, iteration * len(self.names) + (len(self.names) + self.names.index(step) + 1)


class Chip:
    pass


def allocate(nc, ctx, io):
    c = Chip()
    c.nc, c.io, c.scopes = nc, io, [ctx]

    def sb(name, shape, dt=F32):
        return c.scopes[-1].enter_context(nc.sbuf_tensor(name, shape, dt))

    def sem(name):
        return ctx.enter_context(nc.semaphore(name))

    c.sb = sb
    c.wraw = sb("wraw", [P, 2, WT])
    c.whi = sb("whi", [P, 2, WT], F32R)
    c.wlo = sb("wlo", [P, 2, WT], F32R)
    c.h = sb("h", [P, KD, T])
    c.vec = sb("vec", [P, N_VEC])
    c.ident = sb("ident", [P, P])
    c.ones = sb("ones", [P, P])
    c.eps = sb("eps", [P, 1])
    c.ps = ctx.enter_context(nc.psum_tensor("ps", [P, 8, T], F32))
    c.raw_loaded = [sem("raw_loaded_even"), sem("raw_loaded_odd")]
    c.hi_ready, c.lo_ready, c.tile_done = sem("hi_ready"), sem("lo_ready"), sem("tile_done")
    c.tile, c.stage = 0, 0
    return c


class scope:

    def __init__(self, c):
        self.c = c

    def __enter__(self):
        self.c.scopes.append(ExitStack())
        return self.c.sb

    def __exit__(self, *a):
        self.c.scopes.pop().close()


def steps(c, name, names):
    c.stage += 1
    return Steps(c.scopes[-1].enter_context(c.nc.semaphore(f"{name}_{c.stage}")), names)


def vcol(c, name, k=0, n=1):
    at = VCOL[name] + k
    return c.vec[:, at:at + n]


def ring_load(c, sp, j, t, known):
    if known is None or known + 4 < N_WT:
        sp.wait_ge(c.lo_ready, j + 3)
        sp.dma_start(c.wraw[:, t, :], c.io["weights"][j + 4]).then_inc(c.raw_loaded[t], 16)


def ring_hi(c, act, j, half, t, known):
    act.wait_ge(c.tile_done, j + 1)
    if known is None or known + 2 < N_WT:
        act.wait_ge(c.raw_loaded[t], half * 16 + 32)
        c.nc.scalar.activation(c.whi[:, t, :], c.wraw[:, t, :], ACT.Copy).then_inc(c.hi_ready, 1)


def ring_lo(c, dve, j, t, known):
    if known is None or known + 2 < N_WT:
        dve.wait_ge(c.hi_ready, j + 3)
        c.nc.vector.tensor_tensor(c.wlo[:, t, :], c.wraw[:, t, :], c.whi[:, t, :].bitcast(F32),
                                  ALU.subtract).then_inc(c.lo_ready, 1)
    else:
        dve.wait_ge(c.tile_done, j + 1)


def simple(groups, ks=KD):
    return [[(q, True, True, [(k, k) for k in range(ks)])] for q in range(groups)]


def dense(c, iters, body, x_of, act_evac, dve_evac, act_steps, dve_steps, frees, tokens_out=False):
    nc, ps = c.nc, c.ps
    u, n_groups = len(body), 1 + max(part[0] for tile in body for part in tile)
    base = c.tile
    assert base % 2 == 0 and u % 2 == 0 and n_groups % 2 == 0
    loops = iters
    while loops > 0 and base + loops * u + 4 > N_WT:
        loops -= 1
    if loops < 2:
        loops = 0

    def run(e, emit):
        if loops:
            with e.Fori(0, loops) as i:
                for r in range(u):
                    emit(e, i, r, i * u + (base + r), i * (u // 2) + (base + r) // 2, None)
        for i in range(loops, iters):
            for r in range(u):
                j = base + i * u + r
                emit(e, i, r, j, j // 2, j)

    def closed(r):
        return [q for q, _, closes, _ in body[r] if closes]

    with nc.Block() as block:
        @block.sync
        def _(sp):
            run(sp, lambda e, i, r, j, half, known: ring_load(c, e, j, r % 2, known))

        @block.scalar
        def _(act):
            if act_steps:
                act_steps.start(act)

            def emit(e, i, r, j, half, known):
                ring_hi(c, e, j, half, r % 2, known)
                for q in closed(r):
                    act_evac(e, i, q)
            run(act, emit)

        @block.vector
        def _(dve):
            if dve_steps:
                dve_steps.start(dve)

            def emit(e, i, r, j, half, known):
                ring_lo(c, e, j, r % 2, known)
                for q in closed(r):
                    dve_evac(e, i, q)
            run(dve, emit)

        @block.tensor
        def _(pe):
            def emit(e, i, r, j, half, known):
                t = r % 2
                e.wait_ge(c.lo_ready, j + 1)
                for q, opens, closes, ks in body[r]:
                    if opens:
                        before, of = (q - 2, i) if q >= 2 else (q - 2 + n_groups, i - 1)
                        e.wait_ge(*frees[before][0].at(frees[before][1], of))
                    pair = ps[:, 2 * (q % 2):2 * (q % 2) + 2, :]
                    if tokens_out:
                        pair = pair.rearrange("p b (a n) -> p (b a) n", n=WN)
                    for m in range(T // P if tokens_out else WN // P):
                        for n, (kw, kx) in enumerate(ks):
                            for wa, xa in ((0, 0), (0, 1), (1, 0)):
                                w = (c.whi, c.wlo)[wa]
                                x = x_of(q, kx)[xa]
                                if tokens_out:
                                    a, b = x[:, m * P:(m + 1) * P], w[:, t, kw * WN:(kw + 1) * WN]
                                else:
                                    a, b = w[:, t, kw * WN + m * P:kw * WN + (m + 1) * P], x
                                last = nc.tensor.matmul(pair[:, m, :], a, b, start=opens and n == 0 and wa + xa == 0,
                                                        stop=closes and n == len(ks) - 1 and wa == 1)
                last.then_inc(c.tile_done, 1)
            run(pe, emit)
    c.tile += iters * u


def prologue(c, x_in):
    nc, io = c.nc, c.io
    with scope(c):
        const_loaded = c.scopes[-1].enter_context(nc.semaphore("const_loaded"))
        with nc.Block() as block:
            @block.sync
            def _(sp):
                for t in range(2):
                    sp.dma_start(c.wraw[:, t, :], io["weights"][t]).then_inc(c.raw_loaded[t], 16)
                sp.dma_start(c.h[:, :, :], x_in).then_inc(const_loaded, 16)
                sp.dma_start(c.vec[:, :], io["vectors"]).then_inc(const_loaded, 16)
                sp.dma_start(c.ident[:, :], io["identity"]).then_inc(const_loaded, 16)
                for t in range(2):
                    sp.wait_ge(c.lo_ready, t + 1)
                    sp.dma_start(c.wraw[:, t, :], io["weights"][t + 2]).then_inc(c.raw_loaded[t], 16)
                sp.wait_ge(const_loaded, 48)

            @block.scalar
            def _(act):
                for t in range(2):
                    act.wait_ge(c.raw_loaded[t], 16)
                    nc.scalar.activation(c.whi[:, t, :], c.wraw[:, t, :], ACT.Copy).then_inc(c.hi_ready, 1)

            @block.vector
            def _(dve):
                nc.vector.memset(c.ones[:, :], 1.0)
                nc.vector.memset(c.eps[:, :], EPS)
                for t in range(2):
                    dve.wait_ge(c.hi_ready, t + 1)
                    nc.vector.tensor_tensor(c.wlo[:, t, :], c.wraw[:, t, :], c.whi[:, t, :].bitcast(F32),
                                            ALU.subtract).then_inc(c.lo_ready, 1)


def norm(c, name, gains, outs, keep=None, after=None):
    nc, h, ps = c.nc, c.h, c.ps
    n_out = len(gains)
    with scope(c) as sb:
        sq = sb(f"{name}_sq", [P, KD, T])
        total = sb(f"{name}_total", [P, T])
        rstd = sb(f"{name}_rstd", [P, T])
        xf = keep if keep is not None else sq
        A = steps(c, f"{name}_act", ["square", "log", "rstd"]
                  + [f"hi{o}{k}" for o in range(len(outs)) for k in range(KD)])
        V = steps(c, f"{name}_dve", ["total"] + [f"{w}{o}{k}" for o in range(n_out)
                                                 for w in (("x", "lo") if outs else ("x",)) for k in range(KD)])
        E = steps(c, f"{name}_pe", ["sum"])
        with nc.Block() as block:
            @block.scalar
            def _(act):
                A.start(act)
                nc.scalar.activation(sq[:, :, :], h[:, :, :], ACT.Square).then_inc(*A.done("square"))
                act.wait_ge(*E.at("sum"))
                nc.scalar.activation(rstd[:, :], ps[:, 4, :], ACT.Ln, bias=c.eps[:, :], scale=1.0 / DM)\
                    .then_inc(*A.done("log"))
                act.wait_ge(*A.at("log"))
                nc.scalar.activation(rstd[:, :], rstd[:, :], ACT.Exp, scale=-0.5).then_inc(*A.done("rstd"))
                if outs:
                    for o in range(n_out):
                        for k in range(KD):
                            act.wait_ge(*V.at(f"x{o}{k}"))
                            nc.scalar.activation(outs[o][0][:, k, :], xf[:, k, :], ACT.Copy)\
                                .then_inc(*A.done(f"hi{o}{k}"))

            @block.vector
            def _(dve):
                V.start(dve)
                dve.wait_ge(*A.at("square"))
                nc.vector.tensor_reduce(total[:, :], sq[:, :, :].rearrange("p k t -> p t k"), AX.X, ALU.add)\
                    .then_inc(*V.done("total"))
                dve.wait_ge(*A.at("rstd"))
                for o in range(n_out):
                    for k in range(KD):
                        if o > 0:
                            dve.wait_ge(*V.at(f"lo{o - 1}{k}"))
                        nc.vector.scalar_tensor_tensor(xf[:, k, :], h[:, k, :], vcol(c, gains[o], k), rstd[:, :],
                                                       ALU.mult, ALU.mult).then_inc(*V.done(f"x{o}{k}"))
                    for k in range(KD):
                        if not outs:
                            continue
                        dve.wait_ge(*A.at(f"hi{o}{k}"))
                        nc.vector.tensor_tensor(outs[o][1][:, k, :], xf[:, k, :], outs[o][0][:, k, :].bitcast(F32),
                                                ALU.subtract).then_inc(*V.done(f"lo{o}{k}"))

            @block.tensor
            def _(pe):
                E.start(pe)
                pe.wait_ge(*V.at("total"))
                nc.tensor.matmul(ps[:, 4, :], c.ones[:, :], total[:, :], start=True, stop=True)\
                    .then_inc(*E.done("sum"))
                if after:
                    pe.wait_ge(*V.at(f"x0{KD - 1}"))
                    after(pe, xf)


def residual(c, name, iters, body, x_of, scale=1.0):
    nc, h, ps = c.nc, c.h, c.ps
    V = steps(c, f"{name}_dve", ["h0", "h1"])

    def dve_evac(dve, i, q):
        at = i * 4 + 2 * q
        pair = ps[:, 2 * (q % 2):2 * (q % 2) + 2, :]
        nc.vector.scalar_tensor_tensor(h[:, ds(at, 2), :], pair, scale, h[:, ds(at, 2), :],
                                       ALU.mult, ALU.add).then_inc(*V.done(f"h{q}"))

    dense(c, iters, body, x_of, lambda act, i, q: None, dve_evac, None, V, [(V, "h0"), (V, "h1")])


def ds(at, n):
    return slice(at, at + n) if isinstance(at, int) else bass.ds(at, n)


def swiglu(c, name, gain, scale=1.0):
    nc, ps = c.nc, c.ps
    with scope(c) as sb:
        xh, xl = sb(f"{name}_xh", [P, KD, T], F32R), sb(f"{name}_xl", [P, KD, T], F32R)
        norm(c, f"{name}_n", [gain], [(xh, xl)])
        uh, ul = sb(f"{name}_uh", [P, KH, T], F32R), sb(f"{name}_ul", [P, KH, T], F32R)
        with scope(c) as sb2:
            gate = sb2(f"{name}_gate", [P, 2, T])
            unit = sb2(f"{name}_unit", [P, 2, T])
            A = steps(c, f"{name}_act", ["gate", "hi"])
            V = steps(c, f"{name}_dve", ["unit", "lo"])

            def act_evac(act, i, q):
                if q == 0:
                    act.wait_ge(*V.at("unit", i - 1))
                    nc.scalar.activation(gate[:, :, :], ps[:, 0:2, :], ACT.Silu).then_inc(*A.done("gate"))
                    return
                act.wait_ge(*V.at("unit", i))
                nc.scalar.activation(uh[:, ds(i * 2, 2), :], unit[:, :, :], ACT.Copy).then_inc(*A.done("hi"))

            def dve_evac(dve, i, q):
                if q == 0:
                    return
                dve.wait_ge(*A.at("gate", i))
                dve.wait_ge(*V.at("lo", i - 1))
                nc.vector.tensor_tensor(unit[:, :, :], gate[:, :, :], ps[:, 2:4, :], ALU.mult)\
                    .then_inc(*V.done("unit"))
                dve.wait_ge(*A.at("hi", i))
                nc.vector.tensor_tensor(ul[:, ds(i * 2, 2), :], unit[:, :, :], uh[:, ds(i * 2, 2), :].bitcast(F32),
                                        ALU.subtract).then_inc(*V.done("lo"))

            dense(c, HID // WN, simple(2), lambda q, k: (xh[:, k, :], xl[:, k, :]), act_evac, dve_evac,
                  A, V, [(A, "gate"), (V, "unit")])
        down = []
        for q in range(2):
            for k0 in range(0, KH, WK):
                ks = range(k0, min(k0 + WK, KH))
                down.append([(q, k0 == 0, k0 + WK >= KH, [(k - k0, k) for k in ks])])
        residual(c, f"{name}_down", DM // WN // 2, down, lambda q, k: (uh[:, k, :], ul[:, k, :]), scale)


def group_pair(c, q):
    return c.ps[:, 2 * (q % 2):2 * (q % 2) + 2, :]


def gated_delta(c):
    nc, ps, io = c.nc, c.ps, c.io
    NC = T // P
    with scope(c) as sb:
        gate = sb("gdn_gate", [P, HEADS, T])
        G8 = sb("gdn_G8", [HEADS, T])
        beta8 = sb("gdn_beta8", [HEADS, T])
        xh = sb("gdn_xh", [P, KD, T], F32R)
        xl = sb("gdn_xl", [P, KD, T], F32R)
        with scope(c) as sb2:
            wab = sb2("gdn_wab", [P, KD, 2 * HEADS])
            neg_a = sb2("gdn_neg_a", [HEADS, 2])
            small = sb2("gdn_small", [HEADS, 4, T])
            loaded = c.scopes[-1].enter_context(nc.semaphore("gdn_small_loaded"))
            ab = steps(c, "gdn_ab_pe", ["a", "b"])

            def after(pe, xf):
                ab.start(pe)
                pe.wait_ge(loaded, 32)
                for n in range(2):
                    for k in range(KD):
                        last = nc.tensor.matmul(ps[0:HEADS, 5 + n, :], wab[:, k, n * HEADS:(n + 1) * HEADS],
                                                xf[:, k, :], start=k == 0, stop=k == KD - 1)
                    last.then_inc(*ab.done("ab"[n]))

            with nc.Block() as block:
                @block.gpsimd
                def _(pool):
                    pool.dma_start(wab[:, :, :], io["gdn_w_ab"]).then_inc(loaded, 16)
                    pool.dma_start(neg_a[:, :], io["gdn_ab"]).then_inc(loaded, 16)
            norm(c, "gdn_n", ["ln_mix.0"], [(xh, xl)], after=after)
            A = steps(c, "gdn_gates_act", ["ea", "abs", "exp", "log", "beta"])
            V = steps(c, "gdn_gates_dve", ["x", "sp", "na", "g"] + [f"G{n}" for n in range(NC)])
            with nc.Block() as block:
                @block.vector
                def _(dve):
                    V.start(dve)
                    nc.vector.tensor_scalar(small[:, 0, :], ps[0:HEADS, 5, :], neg_a[:, 1:2], None, ALU.add)\
                        .then_inc(*V.done("x"))
                    dve.wait_ge(*A.at("log"))
                    nc.vector.scalar_tensor_tensor(small[:, 2, :], small[:, 0, :], 0.0, small[:, 1, :],
                                                   ALU.max, ALU.add).then_inc(*V.done("sp"))
                    nc.vector.tensor_scalar(neg_a[:, 0:1], neg_a[:, 0:1], -1.0, None, ALU.mult)\
                        .then_inc(*V.done("na"))
                    dve.wait_ge(*V.at("na"))
                    nc.vector.tensor_scalar(small[:, 3, :], small[:, 2, :], neg_a[:, 0:1], None, ALU.mult)\
                        .then_inc(*V.done("g"))
                    dve.wait_ge(*V.at("g"))
                    for n in range(NC):
                        nc.vector.tensor_tensor_scan(G8[:, n * P:(n + 1) * P], c.ones[0:HEADS, :],
                                                     small[:, 3, n * P:(n + 1) * P], 0.0, ALU.mult, ALU.add)\
                            .then_inc(*V.done(f"G{n}"))

                @block.scalar
                def _(act):
                    A.start(act)
                    nc.scalar.activation(neg_a[:, 0:1], neg_a[:, 0:1], ACT.Exp).then_inc(*A.done("ea"))
                    act.wait_ge(*V.at("x"))
                    nc.scalar.activation(small[:, 1, :], small[:, 0, :], ACT.Abs).then_inc(*A.done("abs"))
                    act.wait_ge(*A.at("abs"))
                    nc.scalar.activation(small[:, 1, :], small[:, 1, :], ACT.Exp, scale=-1.0).then_inc(*A.done("exp"))
                    act.wait_ge(*A.at("exp"))
                    nc.scalar.activation(small[:, 1, :], small[:, 1, :], ACT.Ln, bias=c.ones[0:HEADS, 0:1])\
                        .then_inc(*A.done("log"))
                    nc.scalar.activation(beta8[:, :], ps[0:HEADS, 6, :], ACT.Sigmoid).then_inc(*A.done("beta"))

        qkv = sb("gdn_qkv", [P, 3 * HEADS, T])
        with scope(c) as sb2:
            padded = sb2("gdn_padded", [P, 2, 2, 3 + T])
            conv = sb2("gdn_conv_out", [P, 2, 2, T])
            taps = range(4)
            A = steps(c, "gdn_qkv_act", [f"{w}{q}" for q in range(2) for w in ("padded", "silu")])
            V = steps(c, "gdn_qkv_dve", [f"conv{q}{w}" for q in range(2) for w in taps])
            with nc.Block() as block:
                @block.vector
                def _(dve):
                    nc.vector.memset(padded[:, :, :, 0:3], 0.0)

            def act_evac(act, i, q):
                act.wait_ge(*V.at(f"conv{q}3", i - 1))
                nc.scalar.activation(padded[:, q, :, 3:], group_pair(c, q), ACT.Copy).then_inc(*A.done(f"padded{q}"))
                act.wait_ge(*V.at(f"conv{q}3", i))
                nc.scalar.activation(qkv[:, ds(i * 4 + 2 * q, 2), :], conv[:, q, :, :], ACT.Silu)\
                    .then_inc(*A.done(f"silu{q}"))

            def dve_evac(dve, i, q):
                dve.wait_ge(*A.at(f"silu{q}", i - 1))
                dve.wait_ge(*A.at(f"padded{q}", i))
                for w in taps:
                    if w:
                        dve.wait_ge(*V.at(f"conv{q}{w - 1}", i))
                    for m in range(2):
                        col = i * 4 + (2 * q + m)
                        at = VCOL[f"gdn_conv.0.{w}"] + col
                        scalar = c.vec[:, ds(at, 1)]
                        src, dst = padded[:, q, m, w:w + T], conv[:, q, m, :]
                        if w == 0:
                            last = nc.vector.tensor_scalar(dst, src, scalar, None, ALU.mult)
                        else:
                            last = nc.vector.scalar_tensor_tensor(dst, src, scalar, dst, ALU.mult, ALU.add)
                    last.then_inc(*V.done(f"conv{q}{w}"))

            dense(c, 6, simple(2), lambda q, k: (xh[:, k, :], xl[:, k, :]), act_evac, dve_evac, A, V,
                  [(A, "padded0"), (A, "padded1")])
        A = steps(c, "gdn_gate_act", ["gate0", "gate1"])

        def gate_evac(act, i, q):
            nc.scalar.activation(gate[:, ds(i * 4 + 2 * q, 2), :], group_pair(c, q), ACT.Silu)\
                .then_inc(*A.done(f"gate{q}"))
        dense(c, 2, simple(2), lambda q, k: (xh[:, k, :], xl[:, k, :]), gate_evac, lambda dve, i, q: None, A, None,
              [(A, "gate0"), (A, "gate1")])
        gdn_core(c, qkv, gate, G8, beta8, xh, xl)
        residual(c, "gdn_out", 2, simple(2), lambda q, k: (xh[:, k, :], xl[:, k, :]))


def doubling(n):
    size = 2
    while size < n:
        yield size
        size *= 2


def gdn_core(c, qkv, gate, G8, beta8, oh, ol):
    nc, ps, io = c.nc, c.ps, c.io
    NC = T // P
    levels = list(doubling(P))
    NL = len(levels)
    with scope(c) as sb:
        mask = sb("gdn_mask", [P, 2 + NL, P])
        gcol = sb("gdn_gcol", [P, NC, HEADS])
        b = {n: sb(f"gdn_{n}", [P, T]) for n in "kn qn grow D kb eg ekd vb kd AT X sq".split()}
        b["attT"], b["XT"], b["Y"] = b["ekd"], b["D"], b["kb"]
        blocks = sb("gdn_blocks", [P, 2, T])
        b["CTa"], b["CTb"] = blocks[:, 0, :], blocks[:, 1, :]
        sel = blocks[0:HEADS, :, :]
        state = sb("gdn_state", [P, P])
        R = sb("gdn_R", [P, P])
        VN = sb("gdn_VN", [P, P])
        rs = sb("gdn_rs", [P, 2, T])

        def ch(buf, n):
            return buf[:, n * P:(n + 1) * P]

        def wide(buf, n0=0, n=NC):
            return buf[:, n0 * P:(n0 + n) * P].rearrange("p (n t) -> p n t", n=n)

        def over(m, n=NC):
            return m[:, None, :].to_broadcast([P, n, P])

        half = NC // 2
        E = steps(c, "gdn_core_pe", ["rows", "norms", "kk", "qk", "turn_v", "turn_kd", "turn_X"]
                  + [f"{w}{l}{a}" for l in range(NL) for a in range(2) for w in ("Y", "Z")]
                  + [f"{w}{n}" for n in range(NC) for w in ("kS", "vn", "o", "dS")] + ["osum"])
        A = steps(c, "gdn_core_act", ["qsq", "ksq", "grow", "log", "rs", "eg", "ekd", "D", "vbt", "kdt", "X"]
                  + [f"Y{l}{a}" for l in range(NL) for a in range(2)]
                  + [f"vn{n}" for n in range(NC)] + ["osq", "olog", "ors", "hi"])
        V = steps(c, "gdn_core_dve", ["gsel", "bsel", "state", "nd", "diff", "masked", "qn", "kn", "vb", "kb", "kg",
                                      "qd", "kd", "AT", "attT", "off", "XT"]
                  + [f"{w}{l}{a}" for l in range(NL) for a in range(2) for w in ("X", "XT")]
                  + [w for n in range(NC) for w in (f"R{n}", f"S{n}")] + ["on", "og", "lo"])
        Q = steps(c, "gdn_core_pool", [f"CT{l}" for l in range(NL)])
        pre = steps(c, "gdn_gcol_pe", ["turn"])
        loaded = c.scopes[-1].enter_context(nc.semaphore("gdn_mask_loaded"))
        with nc.Block() as block:
            @block.sync
            def _(sp):
                sp.dma_start(mask[:, :, :], io["gdn_masks"]).then_inc(loaded, 16)
                sp.wait_ge(loaded, 16)

            @block.tensor
            def _(pe):
                pre.start(pe)
                for n in range(NC):
                    last = nc.tensor.transpose(ps[:, 4, n * HEADS:(n + 1) * HEADS], ch(G8, n),
                                               c.ident[0:HEADS, 0:HEADS])
                last.then_inc(*pre.done("turn"))

            @block.vector
            def _(dve):
                dve.wait_ge(*pre.at("turn"))
                nc.vector.tensor_copy(gcol[:, :, :].rearrange("p n h -> p (n h)"), ps[:, 4, 0:NC * HEADS])

        with nc.Block() as block:
            @block.vector
            def _(dve):
                V.start(dve)
                with dve.Fori(0, HEADS) as i:
                    dve.wait_ge(*V.at("lo", i - 1))
                    pick = c.ident[0:HEADS, ds(i, 1)].to_broadcast([HEADS, T])
                    nc.vector.tensor_tensor(sel[:, 0, :], G8[:, :], pick, ALU.mult).then_inc(*V.done("gsel"))
                    nc.vector.tensor_tensor(sel[:, 1, :], beta8[:, :], pick, ALU.mult).then_inc(*V.done("bsel"))
                    dve.wait_ge(*V.at(f"S{NC - 1}", i - 1))
                    nc.vector.memset(state[:, :], 0.0).then_inc(*V.done("state"))
                    dve.wait_ge(*A.at("grow", i))
                    grow = wide(b["grow"])
                    nc.vector.tensor_tensor(wide(b["ekd"]), grow[:, :, P - 1:P].to_broadcast([P, NC, P]), grow,
                                            ALU.subtract).then_inc(*V.done("nd"))
                    nc.vector.tensor_tensor(wide(b["D"]), grow, gcol[:, :, ds(i, 1)].to_broadcast([P, NC, P]),
                                            ALU.subtract).then_inc(*V.done("diff"))
                    dve.wait_ge(*V.at("diff", i))
                    nc.vector.tensor_tensor(wide(b["D"]), wide(b["D"]), over(mask[:, 0, :]), ALU.add)\
                        .then_inc(*V.done("masked"))
                    dve.wait_ge(*A.at("rs", i))
                    nc.vector.scalar_tensor_tensor(b["qn"][:, :], qkv[:, ds(i, 1), :].rearrange("p a t -> p (a t)"),
                                                   SCALE, rs[:, 0, :], ALU.mult, ALU.mult).then_inc(*V.done("qn"))
                    nc.vector.tensor_tensor(b["kn"][:, :], qkv[:, ds(i + HEADS, 1), :].rearrange("p a t -> p (a t)"),
                                            rs[:, 1, :], ALU.mult).then_inc(*V.done("kn"))
                    dve.wait_ge(*E.at("norms", i))
                    nc.vector.tensor_tensor(b["vb"][:, :],
                                            qkv[:, ds(i + 2 * HEADS, 1), :].rearrange("p a t -> p (a t)"),
                                            ps[:, 5, :], ALU.mult).then_inc(*V.done("vb"))
                    dve.wait_ge(*V.at("kn", i))
                    nc.vector.tensor_tensor(b["kb"][:, :], b["kn"][:, :], ps[:, 5, :], ALU.mult)\
                        .then_inc(*V.done("kb"))
                    dve.wait_ge(*A.at("ekd", i))
                    dve.wait_ge(*V.at("kb", i))
                    nc.vector.tensor_tensor(b["sq"][:, :], b["kb"][:, :], b["eg"][:, :], ALU.mult)\
                        .then_inc(*V.done("kg"))
                    nc.vector.tensor_tensor(b["grow"][:, :], b["qn"][:, :], b["eg"][:, :], ALU.mult)\
                        .then_inc(*V.done("qd"))
                    nc.vector.tensor_tensor(b["kd"][:, :], b["kn"][:, :], b["ekd"][:, :], ALU.mult)\
                        .then_inc(*V.done("kd"))
                    dve.wait_ge(*A.at("D", i))
                    dve.wait_ge(*E.at("kk", i))
                    nc.vector.tensor_tensor(b["AT"][:, :], ps[:, 4, :], b["D"][:, :], ALU.mult)\
                        .then_inc(*V.done("AT"))
                    dve.wait_ge(*E.at("qk", i))
                    dve.wait_ge(*V.at("kd", i))
                    nc.vector.tensor_tensor(b["attT"][:, :], ps[:, 5, :], b["D"][:, :], ALU.mult)\
                        .then_inc(*V.done("attT"))
                    dve.wait_ge(*V.at("attT", i))
                    nc.vector.tensor_tensor(wide(b["XT"]), wide(b["AT"]), over(mask[:, 1, :]), ALU.mult)\
                        .then_inc(*V.done("off"))
                    dve.wait_ge(*V.at("off", i))
                    nc.vector.tensor_tensor(wide(b["XT"]), over(c.ident[:, :]), wide(b["XT"]), ALU.subtract)\
                        .then_inc(*V.done("XT"))
                    for l in range(NL):
                        for a in range(2):
                            s = slice(a * half * P, (a + 1) * half * P)
                            dve.wait_ge(*E.at(f"Z{l}{a}", i))
                            last = l == NL - 1
                            nc.vector.tensor_tensor(b["X"][:, s], b["X"][:, s], ps[:, 4 + a, 0:half * P],
                                                    ALU.subtract).then_inc(*V.done(f"X{l}{a}"))
                            nc.vector.tensor_tensor(b["XT"][:, s], b["XT"][:, s], ps[:, 4 + a, half * P:],
                                                    ALU.subtract).then_inc(*V.done(f"XT{l}{a}"))
                    for n in range(NC):
                        dve.wait_ge(*E.at(f"kS{n}", i))
                        nc.vector.tensor_tensor(R[:, :], ch(b["vb"], n), ps[:, 4, 0:P], ALU.subtract)\
                            .then_inc(*V.done(f"R{n}"))
                        dve.wait_ge(*E.at(f"dS{n}", i))
                        nc.vector.scalar_tensor_tensor(state[:, :], state[:, :],
                                                       b["eg"][:, (n + 1) * P - 1:(n + 1) * P],
                                                       ps[:, 6, 0:P], ALU.mult, ALU.add).then_inc(*V.done(f"S{n}"))
                    dve.wait_ge(*A.at("ors", i))
                    nc.vector.scalar_tensor_tensor(b["CTa"][:, :], ps[:, 7, :], vcol(c, "gdn_norm.0"), rs[:, 0, :],
                                                   ALU.mult, ALU.mult).then_inc(*V.done("on"))
                    dve.wait_ge(*V.at("on", i))
                    nc.vector.tensor_tensor(b["CTa"][:, :], b["CTa"][:, :],
                                            gate[:, ds(i, 1), :].rearrange("p a t -> p (a t)"), ALU.mult)\
                        .then_inc(*V.done("og"))
                    dve.wait_ge(*A.at("hi", i))
                    nc.vector.tensor_tensor(ol[:, ds(i, 1), :].rearrange("p a t -> p (a t)"), b["CTa"][:, :],
                                            oh[:, ds(i, 1), :].rearrange("p a t -> p (a t)").bitcast(F32),
                                            ALU.subtract).then_inc(*V.done("lo"))

            @block.scalar
            def _(act):
                A.start(act)
                with act.Fori(0, HEADS) as i:
                    act.wait_ge(*E.at(f"kS{NC - 1}", i - 1))
                    nc.scalar.activation(b["sq"][:, :], qkv[:, ds(i, 1), :].rearrange("p a t -> p (a t)"),
                                         ACT.Square).then_inc(*A.done("qsq"))
                    act.wait_ge(*V.at("lo", i - 1))
                    nc.scalar.activation(b["X"][:, :], qkv[:, ds(i + HEADS, 1), :].rearrange("p a t -> p (a t)"),
                                         ACT.Square).then_inc(*A.done("ksq"))
                    act.wait_ge(*E.at("norms", i))
                    act.wait_ge(*E.at(f"o{NC - 1}", i - 1))
                    nc.scalar.activation(b["grow"][:, :], ps[:, 4, :], ACT.Copy).then_inc(*A.done("grow"))
                    nc.scalar.activation(rs[:, :, :], ps[:, 6:8, :], ACT.Ln, bias=c.eps[:, :])\
                        .then_inc(*A.done("log"))
                    act.wait_ge(*A.at("log", i))
                    nc.scalar.activation(rs[:, :, :], rs[:, :, :], ACT.Exp, scale=-0.5).then_inc(*A.done("rs"))
                    act.wait_ge(*V.at(f"S{NC - 1}", i - 1))
                    nc.scalar.activation(b["eg"][:, :], ps[:, 4, :], ACT.Exp).then_inc(*A.done("eg"))
                    act.wait_ge(*V.at("nd", i))
                    nc.scalar.activation(b["ekd"][:, :], b["ekd"][:, :], ACT.Exp).then_inc(*A.done("ekd"))
                    act.wait_ge(*V.at("masked", i))
                    nc.scalar.activation(b["D"][:, :], b["D"][:, :], ACT.Exp).then_inc(*A.done("D"))
                    act.wait_ge(*E.at("turn_v", i))
                    nc.scalar.activation(b["vb"][:, :], ps[:, 6, :], ACT.Copy).then_inc(*A.done("vbt"))
                    act.wait_ge(*E.at("turn_kd", i))
                    nc.scalar.activation(b["kd"][:, :], ps[:, 7, :], ACT.Copy).then_inc(*A.done("kdt"))
                    act.wait_ge(*E.at("turn_X", i))
                    nc.scalar.activation(b["X"][:, :], ps[:, 6, :], ACT.Copy).then_inc(*A.done("X"))
                    for l in range(NL):
                        for a in range(2):
                            act.wait_ge(*E.at(f"Y{l}{a}", i))
                            nc.scalar.activation(b["Y"][:, a * half * P:(a + 1) * half * P],
                                                 ps[:, 6 + a, 0:half * P], ACT.Copy).then_inc(*A.done(f"Y{l}{a}"))
                    for n in range(NC):
                        act.wait_ge(*E.at(f"vn{n}", i))
                        nc.scalar.activation(VN[:, :], ps[:, 5, 0:P], ACT.Copy).then_inc(*A.done(f"vn{n}"))
                    act.wait_ge(*E.at(f"o{NC - 1}", i))
                    nc.scalar.activation(b["Y"][:, :], ps[:, 7, :], ACT.Square).then_inc(*A.done("osq"))
                    act.wait_ge(*E.at("osum", i))
                    nc.scalar.activation(rs[:, 0, :], ps[:, 5, :], ACT.Ln, bias=c.eps[:, :], scale=1.0 / P)\
                        .then_inc(*A.done("olog"))
                    act.wait_ge(*A.at("olog", i))
                    nc.scalar.activation(rs[:, 0, :], rs[:, 0, :], ACT.Exp, scale=-0.5).then_inc(*A.done("ors"))
                    act.wait_ge(*V.at("og", i))
                    nc.scalar.activation(oh[:, ds(i, 1), :].rearrange("p a t -> p (a t)"), b["CTa"][:, :], ACT.Copy)\
                        .then_inc(*A.done("hi"))

            @block.gpsimd
            def _(pool):
                Q.start(pool)
                with pool.Fori(0, HEADS) as i:
                    for l in range(NL):
                        ct = b["CTa"] if l % 2 == 0 else b["CTb"]
                        if l == 0:
                            pool.wait_ge(*V.at("lo", i - 1))
                            pool.wait_ge(*V.at("AT", i))
                        if l >= 2:
                            pool.wait_ge(*E.at(f"Y{l - 2}1", i))
                        elif l == 1:
                            pool.wait_ge(*E.at(f"Y{NL - 1 - (NL - 1 + 1) % 2}1", i - 1))
                        nc.gpsimd.tensor_tensor(wide(ct), wide(b["AT"]), over(mask[:, 2 + l, :]), ALU.mult)\
                            .then_inc(*Q.done(f"CT{l}"))

            @block.tensor
            def _(pe):
                E.start(pe)
                with pe.Fori(0, HEADS) as i:
                    pe.wait_ge(*V.at("bsel", i))
                    pe.wait_ge(*V.at("lo", i - 1))
                    nc.tensor.matmul(ps[:, 4, :], c.ones[0:HEADS, :], sel[:, 0, :], start=True, stop=True)
                    nc.tensor.matmul(ps[:, 5, :], c.ones[0:HEADS, :], sel[:, 1, :], start=True, stop=True)\
                        .then_inc(*E.done("rows"))
                    pe.wait_ge(*A.at("ksq", i))
                    nc.tensor.matmul(ps[:, 6, :], c.ones[:, :], b["sq"][:, :], start=True, stop=True)
                    nc.tensor.matmul(ps[:, 7, :], c.ones[:, :], b["X"][:, :], start=True, stop=True)\
                        .then_inc(*E.done("norms"))
                    pe.wait_ge(*V.at("kb", i))
                    pe.wait_ge(*A.at("eg", i))
                    for n in range(NC):
                        last = nc.tensor.matmul(ch(ps[:, 4, :], n), ch(b["kn"], n), ch(b["kb"], n), start=True, stop=True)
                    last.then_inc(*E.done("kk"))
                    for n in range(NC):
                        last = nc.tensor.matmul(ch(ps[:, 5, :], n), ch(b["kn"], n), ch(b["qn"], n), start=True, stop=True)
                    last.then_inc(*E.done("qk"))
                    for n in range(NC):
                        last = nc.tensor.transpose(ch(ps[:, 6, :], n), ch(b["vb"], n), c.ident[:, :])
                    last.then_inc(*E.done("turn_v"))
                    pe.wait_ge(*V.at("kd", i))
                    for n in range(NC):
                        last = nc.tensor.transpose(ch(ps[:, 7, :], n), ch(b["kd"], n), c.ident[:, :])
                    last.then_inc(*E.done("turn_kd"))
                    pe.wait_ge(*V.at("XT", i))
                    pe.wait_ge(*A.at("vbt", i))
                    for n in range(NC):
                        last = nc.tensor.transpose(ch(ps[:, 6, :], n), ch(b["XT"], n), c.ident[:, :])
                    last.then_inc(*E.done("turn_X"))
                    pe.wait_ge(*A.at("X", i))
                    for l in range(NL):
                        ct = b["CTa"] if l % 2 == 0 else b["CTb"]
                        pe.wait_ge(*Q.at(f"CT{l}", i))
                        for a in range(2):
                            if l:
                                pe.wait_ge(*V.at(f"XT{l - 1}{a}", i))
                            for m in range(half):
                                n = a * half + m
                                last = nc.tensor.matmul(ch(ps[:, 6 + a, :], m), ch(ct, n), ch(b["X"], n),
                                                        start=True, stop=True)
                            last.then_inc(*E.done(f"Y{l}{a}"))
                            pe.wait_ge(*A.at(f"Y{l}{a}", i))
                            for m in range(half):
                                n = a * half + m
                                nc.tensor.matmul(ch(ps[:, 4 + a, :], m), ch(b["XT"], n), ch(b["Y"], n),
                                                 start=True, stop=True)
                                last = nc.tensor.matmul(ch(ps[:, 4 + a, :], half + m), ch(b["Y"], n), ch(b["XT"], n),
                                                        start=True, stop=True)
                            last.then_inc(*E.done(f"Z{l}{a}"))
                    for n in range(NC):
                        if n:
                            pe.wait_ge(*V.at(f"S{n - 1}", i))
                        else:
                            pe.wait_ge(*V.at(f"XT{NL - 1}1", i))
                        nc.tensor.matmul(ps[:, 4, 0:P], ch(b["sq"], n), state[:, :], start=True, stop=True)\
                            .then_inc(*E.done(f"kS{n}"))
                        pe.wait_ge(*V.at(f"R{n}", i))
                        nc.tensor.matmul(ps[:, 5, 0:P], ch(b["XT"], n), R[:, :], start=True, stop=True)\
                            .then_inc(*E.done(f"vn{n}"))
                        pe.wait_ge(*A.at(f"vn{n}", i))
                        nc.tensor.matmul(ch(ps[:, 7, :], n), state[:, :], ch(b["grow"], n), start=True, stop=False)
                        nc.tensor.matmul(ch(ps[:, 7, :], n), VN[:, :], ch(b["attT"], n), start=False, stop=True)\
                            .then_inc(*E.done(f"o{n}"))
                        nc.tensor.matmul(ps[:, 6, 0:P], ch(b["kd"], n), VN[:, :], start=True, stop=True)\
                            .then_inc(*E.done(f"dS{n}"))
                    pe.wait_ge(*A.at("osq", i))
                    nc.tensor.matmul(ps[:, 5, :], c.ones[:, :], b["Y"][:, :], start=True, stop=True)\
                        .then_inc(*E.done("osum"))


def per_layer_embedding(c, i_layer):
    nc, ps = c.nc, c.ps
    name = f"ple{i_layer}"
    with scope(c) as sb:
        xh, xl = sb(f"{name}_xh", [P, KD, T], F32R), sb(f"{name}_xl", [P, KD, T], F32R)
        ph, pl = sb(f"{name}_ph", [P, 2, T], F32R), sb(f"{name}_pl", [P, 2, T], F32R)
        praw = sb(f"{name}_p", [P, 2, T])
        sig, prod = sb(f"{name}_sig", [P, 2, T]), sb(f"{name}_prod", [P, 2, T])
        loaded = c.scopes[-1].enter_context(nc.semaphore(f"{name}_p_loaded"))
        S = steps(c, f"{name}_split_act", ["hi"])
        with nc.Block() as block:
            @block.gpsimd
            def _(pool):
                pool.dma_start(praw[:, :, :], c.io["p"][i_layer]).then_inc(loaded, 16)

            @block.scalar
            def _(act):
                S.start(act)
                act.wait_ge(loaded, 16)
                nc.scalar.activation(ph[:, :, :], praw[:, :, :], ACT.Copy).then_inc(*S.done("hi"))

            @block.vector
            def _(dve):
                dve.wait_ge(*S.at("hi"))
                nc.vector.tensor_tensor(pl[:, :, :], praw[:, :, :], ph[:, :, :].bitcast(F32), ALU.subtract)
        norm(c, f"{name}_n", [f"ln_ple.{i_layer}"], [(xh, xl)])
        A = steps(c, f"{name}_act", ["sigmoid"])
        V = steps(c, f"{name}_dve", ["prod", "h"])

        def act_evac(act, i, q):
            if q == 1:
                act.wait_ge(*V.at("prod", i - 1))
                nc.scalar.activation(sig[:, :, :], ps[:, 2:4, :], ACT.Sigmoid).then_inc(*A.done("sigmoid"))

        def dve_evac(dve, i, q):
            if q == 1:
                dve.wait_ge(*A.at("sigmoid", i))
                dve.wait_ge(*V.at("h", i - 1))
                nc.vector.tensor_tensor(prod[:, :, :], ps[:, 0:2, :], sig[:, :, :], ALU.mult).then_inc(*V.done("prod"))
                dve.wait_ge(*V.at("prod", i))
                nc.vector.tensor_tensor(c.h[:, ds(i * 2, 2), :], c.h[:, ds(i * 2, 2), :], prod[:, :, :], ALU.add)\
                    .then_inc(*V.done("h"))

        body = [[(0, True, True, [(0, 0), (1, 1)])], [(1, True, True, [(k, k) for k in range(KD)])]]
        dense(c, DM // WN, body, lambda q, k: (ph[:, k, :], pl[:, k, :]) if q == 0 else (xh[:, k, :], xl[:, k, :]),
              act_evac, dve_evac, A, V, [(V, "prod"), (A, "sigmoid")])


def project(c, name, iters, xs, dst, tokens_out=False, func=ACT.Copy):
    A = steps(c, f"{name}_act", ["copy0", "copy1"])

    def evac(act, i, q):
        if tokens_out:
            to = dst[:, :, ds(i * 2 * WN + q * WN, WN)]
            pair = group_pair(c, q).rearrange("p b (a n) -> p (b a) n", n=WN)
        else:
            to, pair = dst[:, ds(i * 4 + 2 * q, 2), :], group_pair(c, q)
        c.nc.scalar.activation(to, pair, func).then_inc(*A.done(f"copy{q}"))

    dense(c, iters, simple(2), lambda q, k: (xs[0][:, k, :], xs[1][:, k, :]), evac, lambda dve, i, q: None, A, None,
          [(A, "copy0"), (A, "copy1")], tokens_out)


def stick_breaking(c):
    nc = c.nc
    with scope(c) as sb:
        oh, ol = sb("sb_oh", [P, KD, T], F32R), sb("sb_ol", [P, KD, T], F32R)
        k = sb("sb_k", [P, HEADS, T])
        v = sb("sb_v", [P, T // P, DM])
        with scope(c) as sb2:
            qh, ql = sb2("sb_qh", [P, KD, T], F32R), sb2("sb_ql", [P, KD, T], F32R)
            norm(c, "sb_n", ["kv_norm", "ln_mix.1"], [(oh, ol), (qh, ql)])
            project(c, "sb_k", 2, (oh, ol), k)
            project(c, "sb_v", 2, (oh, ol), v, tokens_out=True)
            q = ol[:, :, :].bitcast(F32)
            project(c, "sb_q", 2, (qh, ql), q)
        stick_core(c, k, v, q, oh, ol)
        residual(c, "sb_out", 2, simple(2), lambda q_, k_: (oh[:, k_, :], ol[:, k_, :]))


def stick_core(c, k, v, q, oh, ol):
    nc, ps = c.nc, c.ps
    N = T // P
    off = {0: 512, 2: 896, 1: 1024}
    width = 1280
    z = ps[:, 4:7, :].rearrange("p b t -> p (b t)")
    tail = ps[:, 0:3, :].rearrange("p b t -> p (b t)")
    with scope(c) as sb:
        mats = sb("sb_mats", [P, 3, P])
        qg = sb("sb_qg", [P, 1])
        sqk, rs = sb("sb_sq", [P, 2, T]), sb("sb_rs", [P, 2, T])
        kn, qn = sb("sb_kn", [P, T]), sb("sb_qn", [P, T])
        vt = sb("sb_vt", [P, N, P])
        la, sp, ls, w = (sb(f"sb_{n}", [P, width]) for n in ("la", "sp", "ls", "w"))
        loaded = c.scopes[-1].enter_context(nc.semaphore("sb_mats_loaded"))
        A = steps(c, "sb_act", ["qsq", "ksq", "log", "rs", "abs", "exp", "soft", "w", "hi"])
        V = steps(c, "sb_dve", ["qn", "kn", "sp", "ls", "spm", "lw", "wm", "lo"])
        E = steps(c, "sb_pe", ["norms", "z", "tail", "o"])
        Q = steps(c, "sb_pool", ["v"])
        with nc.Block() as block:
            @block.gpsimd
            def _(pool):
                pool.dma_start(mats[:, :, :], c.io["sb_mats"]).then_inc(loaded, 16)
                pool.wait_ge(loaded, 16)

            @block.vector
            def _(dve):
                nc.vector.tensor_scalar(qg[:, :], vcol(c, "sb_q_norm.0"), SCALE, None, ALU.mult)

        def head(buf, i):
            return buf[:, ds(i, 1), :].rearrange("p a t -> p (a t)")

        def diagonal(buf):
            return buf[:, 0:N * P].rearrange("p (n t) -> p n t", n=N)

        def over(m):
            return m[:, None, :].to_broadcast([P, N, P])

        with nc.Block() as block:
            @block.gpsimd
            def _(pool):
                Q.start(pool)
                with pool.Fori(0, HEADS) as i:
                    pool.wait_ge(*E.at("o", i - 1))
                    nc.gpsimd.tensor_copy(vt[:, :, :], v[:, :, ds(i * P, P)]).then_inc(*Q.done("v"))

            @block.scalar
            def _(act):
                A.start(act)
                with act.Fori(0, HEADS) as i:
                    act.wait_ge(*E.at("norms", i - 1))
                    nc.scalar.activation(sqk[:, 0, :], head(q, i), ACT.Square).then_inc(*A.done("qsq"))
                    nc.scalar.activation(sqk[:, 1, :], head(k, i), ACT.Square).then_inc(*A.done("ksq"))
                    act.wait_ge(*E.at("norms", i))
                    act.wait_ge(*V.at("kn", i - 1))
                    nc.scalar.activation(rs[:, :, :], ps[:, 3:5, :], ACT.Ln, bias=c.eps[:, :], scale=1.0 / P)\
                        .then_inc(*A.done("log"))
                    act.wait_ge(*A.at("log", i))
                    nc.scalar.activation(rs[:, :, :], rs[:, :, :], ACT.Exp, scale=-0.5).then_inc(*A.done("rs"))
                    act.wait_ge(*E.at("z", i))
                    act.wait_ge(*V.at("ls", i - 1))
                    nc.scalar.activation(la[:, :], z[:, 0:width], ACT.Abs).then_inc(*A.done("abs"))
                    act.wait_ge(*A.at("abs", i))
                    nc.scalar.activation(la[:, :], la[:, :], ACT.Exp, scale=-1.0).then_inc(*A.done("exp"))
                    act.wait_ge(*A.at("exp", i))
                    nc.scalar.activation(la[:, :], la[:, :], ACT.Ln, bias=c.ones[:, 0:1]).then_inc(*A.done("soft"))
                    act.wait_ge(*V.at("lw", i))
                    nc.scalar.activation(w[:, :], ls[:, :], ACT.Exp).then_inc(*A.done("w"))
                    act.wait_ge(*E.at("o", i))
                    nc.scalar.activation(head(oh, i), ps[:, 3, :], ACT.Copy).then_inc(*A.done("hi"))

            @block.vector
            def _(dve):
                V.start(dve)
                with dve.Fori(0, HEADS) as i:
                    dve.wait_ge(*A.at("rs", i))
                    nc.vector.scalar_tensor_tensor(qn[:, :], head(q, i), qg[:, :], rs[:, 0, :], ALU.mult, ALU.mult)\
                        .then_inc(*V.done("qn"))
                    nc.vector.scalar_tensor_tensor(kn[:, :], head(k, i), vcol(c, "k_norm"), rs[:, 1, :],
                                                   ALU.mult, ALU.mult).then_inc(*V.done("kn"))
                    dve.wait_ge(*A.at("soft", i))
                    nc.vector.scalar_tensor_tensor(sp[:, :], z[:, 0:width], 0.0, la[:, :], ALU.max, ALU.add)\
                        .then_inc(*V.done("sp"))
                    nc.vector.scalar_tensor_tensor(ls[:, :], z[:, 0:width], 0.0, la[:, :], ALU.min, ALU.subtract)\
                        .then_inc(*V.done("ls"))
                    dve.wait_ge(*V.at("sp", i))
                    nc.vector.tensor_tensor(diagonal(sp), diagonal(sp), over(mats[:, 0, :]), ALU.mult)\
                        .then_inc(*V.done("spm"))
                    dve.wait_ge(*E.at("tail", i))
                    nc.vector.tensor_tensor(ls[:, :], ls[:, :], tail[:, 0:width], ALU.add).then_inc(*V.done("lw"))
                    dve.wait_ge(*A.at("w", i))
                    nc.vector.tensor_tensor(diagonal(w), diagonal(w), over(mats[:, 0, :]), ALU.mult)\
                        .then_inc(*V.done("wm"))
                    dve.wait_ge(*A.at("hi", i))
                    nc.vector.tensor_tensor(head(ol, i), ps[:, 3, :], head(oh, i).bitcast(F32), ALU.subtract)\
                        .then_inc(*V.done("lo"))

            @block.tensor
            def _(pe):
                E.start(pe)
                with pe.Fori(0, HEADS) as i:
                    pe.wait_ge(*A.at("ksq", i))
                    pe.wait_ge(*V.at("lo", i - 1))
                    for n in range(2):
                        last = nc.tensor.matmul(ps[:, 3 + n, :], c.ones[:, :], sqk[:, n, :], start=True, stop=True)
                    last.then_inc(*E.done("norms"))
                    pe.wait_ge(*V.at("kn", i))
                    for j in range(N):
                        last = nc.tensor.matmul(z[:, j * P:(j + 1) * P], kn[:, j * P:(j + 1) * P],
                                                qn[:, j * P:(j + 1) * P], start=True, stop=True)
                        if j < N - 1:
                            last = nc.tensor.matmul(z[:, off[j]:off[j] + T - (j + 1) * P], kn[:, j * P:(j + 1) * P],
                                                    qn[:, (j + 1) * P:], start=True, stop=True)
                    last.then_inc(*E.done("z"))
                    pe.wait_ge(*V.at("spm", i))
                    for j in range(N):
                        last = nc.tensor.matmul(tail[:, j * P:(j + 1) * P], mats[:, 1, :], sp[:, j * P:(j + 1) * P],
                                                start=True, stop=True)
                        if j == N - 1:
                            continue
                        dst = tail[:, off[j]:off[j] + T - (j + 1) * P]
                        nc.tensor.matmul(dst, mats[:, 1, :], sp[:, off[j]:off[j] + T - (j + 1) * P],
                                         start=True, stop=False)
                        for jj in range(j + 1, N):
                            at = (jj - j - 1) * P
                            last = nc.tensor.matmul(dst[:, at:at + P], mats[:, 2, :], sp[:, jj * P:(jj + 1) * P],
                                                    start=False, stop=jj == N - 1)
                            if jj < N - 1:
                                nc.tensor.matmul(dst[:, at + P:], mats[:, 2, :],
                                                 sp[:, off[jj]:off[jj] + T - (jj + 1) * P], start=False, stop=False)
                    last.then_inc(*E.done("tail"))
                    pe.wait_ge(*V.at("wm", i))
                    pe.wait_ge(*Q.at("v", i))
                    for j in range(N):
                        if j < N - 1:
                            nc.tensor.matmul(ps[:, 3, (j + 1) * P:], vt[:, j, :], w[:, off[j]:off[j] + T - (j + 1) * P],
                                             start=j == 0, stop=False, skip_group_check=True)
                        last = nc.tensor.matmul(ps[:, 3, j * P:(j + 1) * P], vt[:, j, :], w[:, j * P:(j + 1) * P],
                                                start=False, stop=True, skip_group_check=True)
                    last.then_inc(*E.done("o"))



def three_taps(c, name, iters, x, dst, before, middle, after, bias=None):
    nc = c.nc
    with scope(c) as sb:
        padded = sb(f"{name}_padded", [P, 2, 2, T + 2])
        A = steps(c, f"{name}_act", ["padded0", "padded1"])
        V = steps(c, f"{name}_dve", [f"{w}{q}" for q in range(2) for w in ("mid", "before", "after")])
        with nc.Block() as block:
            @block.vector
            def _(dve):
                nc.vector.memset(padded[:, :, :, 0:1], 0.0)
                nc.vector.memset(padded[:, :, :, T + 1:], 0.0)

        def act_evac(act, i, q):
            act.wait_ge(*V.at(f"after{q}", i - 1))
            nc.scalar.activation(padded[:, q, :, 1:T + 1], group_pair(c, q), ACT.Copy).then_inc(*A.done(f"padded{q}"))

        def dve_evac(dve, i, q):
            dve.wait_ge(*A.at(f"padded{q}", i))
            for step, at, col in (("mid", 1, middle), ("before", 0, before), ("after", 2, after)):
                if step != "mid":
                    dve.wait_ge(*V.at(f"mid{q}" if step == "before" else f"before{q}", i))
                for m in range(2):
                    k = i * 4 + (2 * q + m)
                    to = dst[:, ds(k, 1), :].rearrange("p a t -> p (a t)")
                    src = padded[:, q, m, at:at + T]
                    if step == "mid":
                        last = nc.vector.tensor_scalar(to, src, col(k), bias(k) if bias else None, ALU.mult,
                                                       *([ALU.add] if bias else []))
                    else:
                        last = nc.vector.scalar_tensor_tensor(to, src, col(k), to, ALU.mult, ALU.add)
                last.then_inc(*V.done(f"{step}{q}"))

        dense(c, iters, simple(2), lambda q, k: (x[0][:, k, :], x[1][:, k, :]), act_evac, dve_evac, A, V,
              [(A, "padded0"), (A, "padded1")])


def vec_at(c, name):
    return lambda k: c.vec[:, ds(k + VCOL[name], 1)]


HY_EMB, HY_FFN = 33, 64
TWO_PI = 2 * np.pi
ROUND = 1.5 * 2 ** 23
PI_A = 6.28125
PI_B = float(np.float32(np.floor((TWO_PI - PI_A) * 2 ** 21) / 2 ** 21))
PI_C = float(np.float32(TWO_PI - PI_A - PI_B))


def hyena(c, u):
    nc, ps, io = c.nc, c.ps, c.io
    N = T // P
    with scope(c) as sb:
        h2 = sb("hy_h2", [HY_FFN + 1, T])
        with scope(c) as sb2:
            feats = sb2("hy_feats", [HY_EMB, T])
            w1, w2 = sb2("hy_w1", [HY_EMB, HY_FFN]), sb2("hy_w2", [HY_FFN, HY_FFN])
            cols = sb2("hy_cols", [HY_FFN, 3])
            arg, turns = sb2("hy_arg", [HY_FFN, T]), sb2("hy_turns", [HY_FFN, T])
            hid = sb2("hy_hid", [HY_FFN, T])
            loaded = c.scopes[-1].enter_context(nc.semaphore("hy_small_loaded"))
            E = steps(c, "hy_mlp_pe", ["product0", "product1"])
            V = steps(c, "hy_mlp_dve", [f"{w}{n}" for n in range(2)
                                        for w in ("arg", "scaled", "turns", "ra", "rb", "rc", "clamped")])
            A = steps(c, "hy_mlp_act", ["sin0", "sin1"])
            with nc.Block() as block:
                @block.sync
                def _(sp):
                    for dst, src in ((feats, "hy_feats"), (w1, "hy_w1"), (w2, "hy_w2"), (cols, "hy_cols")):
                        sp.dma_start(dst[:, :], io[src]).then_inc(loaded, 16)

                @block.tensor
                def _(pe):
                    E.start(pe)
                    pe.wait_ge(loaded, 64)
                    nc.tensor.matmul(ps[0:HY_FFN, 4, :], w1[:, :], feats[:, :], start=True, stop=True)\
                        .then_inc(*E.done("product0"))
                    pe.wait_ge(*A.at("sin0"))
                    nc.tensor.matmul(ps[0:HY_FFN, 5, :], w2[:, :], hid[:, :], start=True, stop=True)\
                        .then_inc(*E.done("product1"))

                @block.vector
                def _(dve):
                    V.start(dve)
                    nc.vector.memset(h2[HY_FFN:HY_FFN + 1, :], 1.0)
                    dve.wait_ge(loaded, 64)
                    for n in range(2):
                        dve.wait_ge(*E.at(f"product{n}"))
                        nc.vector.tensor_scalar(arg[:, :], ps[0:HY_FFN, 4 + n, :], cols[:, n:n + 1], cols[:, 2:3],
                                                ALU.add, ALU.mult).then_inc(*V.done(f"arg{n}"))
                        dve.wait_ge(*V.at(f"arg{n}"))
                        nc.vector.tensor_scalar(turns[:, :], arg[:, :], 1 / TWO_PI, ROUND, ALU.mult, ALU.add)\
                            .then_inc(*V.done(f"scaled{n}"))
                        dve.wait_ge(*V.at(f"scaled{n}"))
                        nc.vector.tensor_scalar(turns[:, :], turns[:, :], ROUND, None, ALU.subtract)\
                            .then_inc(*V.done(f"turns{n}"))
                        before = f"turns{n}"
                        for step, part in (("ra", PI_A), ("rb", PI_B), ("rc", PI_C)):
                            dve.wait_ge(*V.at(before))
                            nc.vector.scalar_tensor_tensor(arg[:, :], turns[:, :], -part, arg[:, :],
                                                           ALU.mult, ALU.add).then_inc(*V.done(f"{step}{n}"))
                            before = f"{step}{n}"
                        dve.wait_ge(*V.at(before))
                        nc.vector.tensor_scalar(arg[:, :], arg[:, :], 3.1415925, -3.1415925, ALU.min, ALU.max)\
                            .then_inc(*V.done(f"clamped{n}"))

                @block.scalar
                def _(act):
                    A.start(act)
                    for n, dst in ((0, hid[:, :]), (1, h2[0:HY_FFN, :])):
                        act.wait_ge(*V.at(f"clamped{n}"))
                        nc.scalar.activation(dst, arg[:, :], ACT.Sin).then_inc(*A.done(f"sin{n}"))

        trig = sb("hy_trig", [P, 4, N, T])
        kp, km = sb("hy_kp", [P, N, T]), sb("hy_km", [P, N, T])
        kre, kim = sb("hy_kre", [P, N, T]), sb("hy_kim", [P, N, T])
        zT = sb("hy_zT", [P, N, T])
        w3 = sb("hy_w3", [HY_FFN + 1, 4 * DR])
        decay = sb("hy_decay", [P, 4 * DR])
        tpos = sb("hy_tpos", [P, N + 1])
        damp = sb("hy_damp", [P, T])
        side = [sb(f"hy_side{d}", [P, T]) for d in range(2)]
        sq = sb("hy_sq", [P, T])
        rsq = sb("hy_rsq", [P, T])
        part = [sb(f"hy_part{n}", [P, T]) for n in range(2)]
        yre, yim = kp, km
        loaded = c.scopes[-1].enter_context(nc.semaphore("hy_trig_loaded"))
        pe_steps = ["h300"]
        for n in range(1, 2 * N):
            pe_steps += [f"h3{n // 2}{n % 2}", f"sum{(n - 1) // 2}{(n - 1) % 2}"]
        E = steps(c, "hy_pe", pe_steps + [f"sum{N - 1}1"] + [f"turn{s}" for s in range(N)]
                  + [f"k{w}{j}" for j in range(N) for w in "ri"]
                  + [f"z{j}" for j in range(N)] + [f"y{m}" for m in range(N)])
        A = steps(c, "hy_act", [f"{w}{p}{d}" for p in range(N) for d in range(2) for w in ("damp", "sq")]
                  + ["log", "rsq"] + [f"zT{s}" for s in range(N)])
        V = steps(c, "hy_dve", [x for p in range(N) for x in (f"side{p}0", f"side{p}1", f"kp{p}", f"km{p}")]
                  + [f"k{w}{j}" for j in range(N) for w in "ri"]
                  + [f"{w}{j}" for j in range(N) for w in ("a", "b", "re", "c", "d", "im")]
                  + [f"{w}{m}" for m in range(N) for w in ("dz", "z")])
        with nc.Block() as block:
            @block.sync
            def _(sp):
                for n in range(4):
                    sp.dma_start(trig[:, n, :, :], io["hy_trig"][n]).then_inc(loaded, 16)
                sp.dma_start(w3[:, :], io["hy_w3"]).then_inc(loaded, 16)
                sp.dma_start(decay[:, :], io["hy_decay"].partition_broadcast(P)).then_inc(loaded, 16)
                sp.dma_start(tpos[:, :], io["hy_tpos"]).then_inc(loaded, 16)
                sp.wait_ge(loaded, 7 * 16)

            @block.scalar
            def _(act):
                act.wait_ge(loaded, 7 * 16)
                nc.scalar.activation(decay[:, :], decay[:, :], ACT.Abs)
        def tile_of(buf, k):
            return buf[:, ds(k, 1), :].rearrange("p a t -> p (a t)")

        with nc.Block() as block:
            @block.tensor
            def _(pe):
                E.start(pe)

                def total(i, p, d):
                    pe.wait_ge(*A.at(f"sq{p}{d}", i))
                    nc.tensor.matmul(ps[:, 2, :], c.ones[:, :], sq[:, :], start=p + d == 0, stop=p + d == N)\
                        .then_inc(*E.done(f"sum{p}{d}"))

                with pe.Fori(0, 2) as i:
                    done = None
                    for p in range(N):
                        for d in range(2):
                            if p:
                                pe.wait_ge(*V.at(f"side{p - 1}{d}", i))
                            else:
                                pe.wait_ge(*V.at(f"z{N - 1}", i - 1))
                            nc.tensor.matmul(ps[:, d, :], h2[:, p * P:(p + 1) * P],
                                             w3[:, ds(i * DR + 2 * d * DR, DR)], start=True, stop=True)\
                                .then_inc(*E.done(f"h3{p}{d}"))
                            if done:
                                total(i, *done)
                            done = (p, d)
                    total(i, *done)
                    for s in range(N):
                        if s >= 2:
                            pe.wait_ge(*A.at(f"zT{s - 2}", i))
                        for m in range(N):
                            last = nc.tensor.transpose(ps[:, 4 + s % 2, m * P:(m + 1) * P],
                                                       u[:, 2 * N + m, s * P:(s + 1) * P], c.ident[:, :])
                        last.then_inc(*E.done(f"turn{s}"))
                    pe.wait_ge(*V.at(f"km{N - 1}", i))
                    for j in range(N):
                        for n, (w, src) in enumerate((("r", kp), ("i", km))):
                            if j:
                                pe.wait_ge(*V.at(f"k{w}{j - 1}", i))
                            for s in range(N):
                                last = nc.tensor.matmul(ps[:, 6 + n, :], trig[:, n, s, j * P:(j + 1) * P],
                                                        src[:, s, :], start=s == 0, stop=s == N - 1)
                            last.then_inc(*E.done(f"k{w}{j}"))
                    pe.wait_ge(*A.at(f"zT{N - 1}", i))
                    for j in range(N):
                        bank = 2 * (j % 2)
                        if j >= 2:
                            pe.wait_ge(*V.at(f"d{j - 2}", i))
                        for n in range(2):
                            for s in range(N):
                                last = nc.tensor.matmul(ps[:, bank + n, :], trig[:, n, s, j * P:(j + 1) * P],
                                                        zT[:, s, :], start=s == 0, stop=s == N - 1)
                        last.then_inc(*E.done(f"z{j}"))
                    pe.wait_ge(*V.at(f"im{N - 1}", i))
                    for m in range(N):
                        if m >= 2:
                            pe.wait_ge(*V.at(f"dz{m - 2}", i))
                        for n, src in enumerate((yre, yim)):
                            for j in range(N):
                                last = nc.tensor.matmul(ps[:, 4 + m % 2, :], src[:, j, m * P:(m + 1) * P],
                                                        trig[:, 2 + n, j, :], start=n + j == 0, stop=n * (j + 1) == N)
                        last.then_inc(*E.done(f"y{m}"))

            @block.scalar
            def _(act):
                A.start(act)
                with act.Fori(0, 2) as i:
                    before = None
                    for p in range(N):
                        for d in range(2):
                            nc.scalar.activation(damp[:, :], decay[:, ds(i * DR + 2 * d * DR, DR)], ACT.Exp,
                                                 scale=tpos[:, p:p + 1]).then_inc(*A.done(f"damp{p}{d}"))
                            act.wait_ge(*V.at(f"side{p}{d}", i))
                            if before:
                                act.wait_ge(*E.at("sum%d%d" % before, i))
                            nc.scalar.activation(sq[:, :], side[d][:, :], ACT.Square).then_inc(*A.done(f"sq{p}{d}"))
                            before = (p, d)
                    act.wait_ge(*E.at(f"sum{N - 1}1", i))
                    nc.scalar.activation(rsq[:, :], ps[:, 2, :], ACT.Ln, bias=c.eps[:, :]).then_inc(*A.done("log"))
                    act.wait_ge(*A.at("log", i))
                    nc.scalar.activation(rsq[:, :], rsq[:, :], ACT.Exp, scale=-0.5).then_inc(*A.done("rsq"))
                    for s in range(N):
                        act.wait_ge(*E.at(f"turn{s}", i))
                        nc.scalar.activation(zT[:, s, :], ps[:, 4 + s % 2, :], ACT.Copy).then_inc(*A.done(f"zT{s}"))

            @block.vector
            def _(dve):
                V.start(dve)
                with dve.Fori(0, 2) as i:
                    for p in range(N):
                        for d in range(2):
                            dve.wait_ge(*A.at(f"damp{p}{d}", i))
                            dve.wait_ge(*E.at(f"h3{p}{d}", i))
                            if p:
                                dve.wait_ge(*A.at(f"sq{p - 1}{d}", i))
                                dve.wait_ge(*V.at(f"km{p - 1}", i))
                            keep = tpos[:, N:N + 1] if (p, d) == (0, 1) else 1.0
                            nc.vector.scalar_tensor_tensor(side[d][:, :], ps[:, d, :], keep, damp[:, :],
                                                           ALU.mult, ALU.mult).then_inc(*V.done(f"side{p}{d}"))
                        dve.wait_ge(*V.at(f"side{p}1", i))
                        nc.vector.tensor_tensor(kp[:, p, :], side[0][:, :], side[1][:, :], ALU.add)\
                            .then_inc(*V.done(f"kp{p}"))
                        nc.vector.tensor_tensor(km[:, p, :], side[1][:, :], side[0][:, :], ALU.subtract)\
                            .then_inc(*V.done(f"km{p}"))
                    dve.wait_ge(*A.at("rsq", i))
                    for j in range(N):
                        for n, (w, dst) in enumerate((("r", kre), ("i", kim))):
                            dve.wait_ge(*E.at(f"k{w}{j}", i))
                            nc.vector.scalar_tensor_tensor(dst[:, j, :], ps[:, 6 + n, :], 1 / T, rsq[:, :],
                                                           ALU.mult, ALU.mult).then_inc(*V.done(f"k{w}{j}"))
                    dve.wait_ge(*V.at(f"ki{N - 1}", i))
                    for j in range(N):
                        zc, zs = ps[:, 2 * (j % 2), :], ps[:, 2 * (j % 2) + 1, :]
                        dve.wait_ge(*E.at(f"z{j}", i))
                        if j:
                            dve.wait_ge(*V.at(f"im{j - 1}", i))
                        nc.vector.tensor_tensor(part[0][:, :], zc, kre[:, j, :], ALU.mult).then_inc(*V.done(f"a{j}"))
                        nc.vector.tensor_tensor(part[1][:, :], zs, kim[:, j, :], ALU.mult).then_inc(*V.done(f"b{j}"))
                        dve.wait_ge(*V.at(f"b{j}", i))
                        nc.vector.tensor_tensor(yre[:, j, :], part[0][:, :], part[1][:, :], ALU.add)\
                            .then_inc(*V.done(f"re{j}"))
                        dve.wait_ge(*V.at(f"re{j}", i))
                        nc.vector.tensor_tensor(part[0][:, :], zs, kre[:, j, :], ALU.mult).then_inc(*V.done(f"c{j}"))
                        nc.vector.tensor_tensor(part[1][:, :], zc, kim[:, j, :], ALU.mult).then_inc(*V.done(f"d{j}"))
                        dve.wait_ge(*V.at(f"d{j}", i))
                        nc.vector.tensor_tensor(yim[:, j, :], part[0][:, :], part[1][:, :], ALU.subtract)\
                            .then_inc(*V.done(f"im{j}"))
                    for m in range(N):
                        dve.wait_ge(*E.at(f"y{m}", i))
                        z = u[:, 2 * N + m, :]
                        nc.vector.scalar_tensor_tensor(z, z, c.vec[:, ds(i * N + VCOL["hy_bias_d_2.0"] + m, 1)],
                                                       ps[:, 4 + m % 2, :], ALU.mult, ALU.add)\
                            .then_inc(*V.done(f"dz{m}"))
                        dve.wait_ge(*V.at(f"dz{m}", i))
                        nc.vector.tensor_tensor(z, z, tile_of(u, i * N + m), ALU.mult).then_inc(*V.done(f"z{m}"))



def shifted(c, x, u):
    nc = c.nc
    with scope(c) as sb:
        mid = sb("rw_mid", [P, 16])
        M = steps(c, "rw_mid_dve", ["sum", "mid"])
        with nc.Block() as block:
            @block.vector
            def _(dve):
                M.start(dve)
                nc.vector.tensor_tensor(mid[:, :], vcol(c, "rw_mu_2.0", 0, 16), vcol(c, "rw_mu_2.1", 0, 16), ALU.add)\
                    .then_inc(*M.done("sum"))
                dve.wait_ge(*M.at("sum"))
                nc.vector.tensor_scalar(mid[:, :], mid[:, :], -1.0, 1.0, ALU.mult, ALU.add).then_inc(*M.done("mid"))
        three_taps(c, "rw_taps", 4, x, u, vec_at(c, "rw_mu_2.0"), lambda k: mid[:, ds(k, 1)], vec_at(c, "rw_mu_2.1"))


NORM_EPS7 = 64e-5
GATE_LORA = 160
RATE = -float(np.exp(-0.5))


def rwkv7(c, u, out):
    nc, ps, io = c.nc, c.ps, c.io
    NCH = T // C7
    HP = DR // P
    levels = list(doubling(C7))
    NL = len(levels)
    with scope(c) as sb:
        lora = sb("rw_lora", [P, 4, DR])
        fix = sb("rw_fix", [P, 4, P])
        mask = sb("rw_mask", [P, 2, 3 + NL, P])
        pair1 = sb("rw_pair1", [P, P])
        resets = sb("rw_resets", [P, T])
        gn_eps = sb("rw_gn_eps", [P, 1])
        prm = sb("rw_prm", [P, 9])
        AR = [sb(f"rw_AR{d}", [P, NCH, 2 * P]) for d in range(2)]
        Bm = [sb(f"rw_B{d}", [P, NCH, P]) for d in range(2)]
        Km = [sb(f"rw_K{d}", [P, NCH, P]) for d in range(2)]
        XT = [sb(f"rw_XT{d}", [P, NCH, P]) for d in range(2)]
        PT = [sb(f"rw_PT{d}", [P, NCH, P]) for d in range(2)]
        MV = [sb(f"rw_MV{d}", [P, NCH, C7]) for d in range(2)]
        LT, X, CT, Y = (sb(f"rw_{n}", [P, 4, P]) for n in ("LT", "X", "CT", "Y"))
        MT, QT = CT, X
        vt = sb("rw_vt", [P, NCH, C7])
        ysum = sb("rw_ysum", [P, NCH, C7])
        half = sb("rw_half", [P, 2, NCH])
        fac = sb("rw_fac", [P, 2, NCH])
        nkk, t1, t2, t3, av = (sb(f"rw_{n}", [P, T]) for n in ("nkk", "t1", "t2", "t3", "av"))
        ksum = sb("rw_ksum", [P, T])
        Y2 = sb("rw_eB", [P, T])
        vcp = LT[:, :, :].rearrange("p n t -> p (n t)")
        tot = sb("rw_tot", [P, 2, NCH])
        Zs = sb("rw_Zs", [P, 2, C7])
        US = sb("rw_US", [P, 2, C7])
        ST = sb("rw_ST", [P, 2, C7])
        S1 = sb("rw_S1", [P, 2, C7])
        st = sb("rw_stats", [P, 3, NCH])
        loaded = c.scopes[-1].enter_context(nc.semaphore("rw_loaded"))

        def chunks(buf):
            return buf[:, :].rearrange("p (n t) -> p n t", n=NCH)

        def both(bank):
            return ps[:, bank:bank + 2, :].rearrange("p b (n t) -> p (b n) t", n=2)

        def cur2(buf, k):
            return buf[:, ds(k, 1), :].rearrange("p a t -> p (a t)")

        def cur(k):
            return cur2(u, k)

        quads = [(d, z) for d in range(2) for z in range(2)]
        e_steps, a_steps, v_steps, q_steps = [], [], [], ["fix", "prm"]
        e_steps += ["kk"] + [f"{w}{d}" for d in range(2) for w in ("w", "a")] + ["vt"]
        for d, z in quads:
            e_steps += [f"{w}{d}{z}" for w in ("BA", "tB", "KA", "tK", "V", "tX")]
            e_steps += [f"{w}{l}{d}{z}{a}" for l in range(NL) for a in range(2) for w in ("Y", "Z")]
        e_steps += [f"{w}{n}" for n in range(NCH) for w in ("z", "U", "dS", "y")] + ["bonus", "g", "turn"]
        a_steps += ["kk2", "norm"]
        for d in range(2):
            a_steps += [f"{w}{d}" for w in ("sw", "sa", "eB", "eR", "eA", "half")]
        a_steps += ["vt"]
        for d, z in quads:
            a_steps += [f"{w}{d}{z}" for w in ("LT", "tB", "tK", "V", "X")]
            a_steps += [f"Y{l}{d}{z}{a}" for l in range(NL) for a in range(2)]
        a_steps += [f"U{n}" for n in range(NCH)] + ["ysq", "ylog", "yrs", "g"]
        v_steps += ["kk", "vcopy", "floor", "inv", "nkk"]
        for d in range(2):
            v_steps += [f"{w}{d}" for w in ("scan", "tot", "u1", "u2", "ka", "b", "kdir", "ks", "B0", "B1", "K0", "K1",
                                            "R0", "R1", "A0", "A1")]
        v_steps += ["fac", "state"]
        for d, z in quads:
            v_steps += [f"{w}{d}{z}" for w in ("PT", "MT", "QT", "ysum", "off", "XT")]
            v_steps += [f"{w}{l}{d}{z}{a}" for l in range(NL) for a in range(2) for w in ("X", "XT")]
        v_steps += [x for n in range(NCH) for x in (f"Z0{n}", f"Z1{n}", f"S1{n}", f"Sf{n}", f"Sb{n}", f"yf{n}", f"yb{n}")]
        v_steps += ["sum", "mean", "centred", "var", "normed", "bonus1", "bonus2", "lnw", "plus", "out"]
        for d, z in quads:
            q_steps += [f"CT{l}{d}{z}" for l in range(NL)]
        E, A = steps(c, "rw_pe", e_steps), steps(c, "rw_act", a_steps)
        V, Q = steps(c, "rw_dve", v_steps), steps(c, "rw_pool", q_steps)
        PRM = [("rw_w0_2.0", 0), ("rw_w0_2.1", 1), ("rw_a0_2.0", 2), ("rw_a0_2.1", 3), ("rw_k_k_2", 4),
               ("rw_k_a_2", 5), ("rw_r_k_2", 6), ("rw_ln_w_2", 7), ("rw_ln_b_2", 8)]
        with nc.Block() as block:
            @block.sync
            def _(sp):
                sp.dma_start(lora[:, :, :], io["rw_lora"]).then_inc(loaded, 16)
                sp.dma_start(mask[:, :, :, :], io["rw_masks"]).then_inc(loaded, 16)
                sp.dma_start(pair1[:, :], io["rw_pair"]).then_inc(loaded, 16)
                sp.dma_start(resets[:, :], io["rw_resets"].partition_broadcast(P)).then_inc(loaded, 16)
                sp.wait_ge(loaded, 64)

            @block.gpsimd
            def _(pool):
                for d in range(2):
                    nc.gpsimd.memset(AR[d][:, :, :], 0.0)
                    nc.gpsimd.memset(Bm[d][:, :, :], 0.0)
                    nc.gpsimd.memset(Km[d][:, :, :], 0.0)
                nc.gpsimd.memset(gn_eps[:, :], NORM_EPS7)

            @block.scalar
            def _(act):
                nc.scalar.activation(u[:, 12, :], u[:, 12, :], ACT.Tanh)
                nc.scalar.activation(u[:, 14:16, :], u[:, 14:16, :], ACT.Sigmoid)

        with nc.Block() as block:
            @block.gpsimd
            def _(pool):
                Q.start(pool)
                with pool.Fori(0, HP) as i:
                    pool.wait_ge(*E.at("g", i - 1))
                    nc.gpsimd.tensor_copy(fix[:, :, :], lora[:, :, ds(i * P, P)]).then_inc(*Q.done("fix"))
                    pool.wait_ge(*V.at("out", i - 1))
                    for name, at in PRM:
                        last = nc.gpsimd.tensor_copy(prm[:, at:at + 1], c.vec[:, ds(i + VCOL[name], 1)])
                    last.then_inc(*Q.done("prm"))
                    for d, z in quads:
                        for l in range(NL):
                            if l == 0:
                                pool.wait_ge(*E.at(f"V{d}{z}", i))
                                pool.wait_ge(*A.at(f"LT{d}{z}", i))
                            else:
                                pool.wait_ge(*E.at(f"Y{l - 1}{d}{z}1", i))
                            nc.gpsimd.tensor_tensor(CT[:, :, :], LT[:, :, :],
                                                    mask[:, d, 3 + l, :][:, None, :].to_broadcast([P, 4, P]),
                                                    ALU.mult).then_inc(*Q.done(f"CT{l}{d}{z}"))

            @block.scalar
            def _(act):
                A.start(act)
                with act.Fori(0, HP) as i:
                    act.wait_ge(*V.at("kk", i))
                    nc.scalar.activation(t2[:, :], t1[:, :], ACT.Square).then_inc(*A.done("kk2"))
                    act.wait_ge(*E.at("kk", i))
                    nc.scalar.activation(t2[:, :], ps[:, 0, :], ACT.Sqrt).then_inc(*A.done("norm"))
                    for d in range(2):
                        act.wait_ge(*E.at(f"a{d}", i))
                        act.wait_ge(*V.at("nkk" if d == 0 else "A10", i))
                        nc.scalar.activation(t1[:, :], ps[:, 1, :], ACT.Sigmoid, bias=prm[:, d:d + 1])\
                            .then_inc(*A.done(f"sw{d}"))
                        nc.scalar.activation(av[:, :], ps[:, 2, :], ACT.Sigmoid, bias=prm[:, 2 + d:3 + d])\
                            .then_inc(*A.done(f"sa{d}"))
                        g1, g2 = (t2, t1) if d == 0 else (t1, t2)
                        s = 1.0 if d == 0 else -1.0
                        act.wait_ge(*V.at(f"u2{d}", i))
                        nc.scalar.activation(Y2[:, :], g1[:, :], ACT.Exp, scale=-s * RATE).then_inc(*A.done(f"eB{d}"))
                        act.wait_ge(*A.at(f"eB{d}", i))
                        nc.scalar.activation(g1[:, :], g1[:, :], ACT.Exp, scale=s * RATE).then_inc(*A.done(f"eR{d}"))
                        nc.scalar.activation(g2[:, :], g2[:, :], ACT.Exp, scale=s * RATE).then_inc(*A.done(f"eA{d}"))
                        nc.scalar.activation(half[:, d, :], tot[:, d, :], ACT.Exp, scale=RATE / 2)\
                            .then_inc(*A.done(f"half{d}"))
                    act.wait_ge(*E.at("vt", i))
                    nc.scalar.activation(vt[:, :, :].rearrange("p n e -> p (n e)"), ps[:, 3, :], ACT.Copy)\
                        .then_inc(*A.done("vt"))
                    for n, (d, z) in enumerate(quads):
                        four = slice(4 * z, 4 * z + 4)
                        if n == 0:
                            act.wait_ge(*V.at("A11", i))
                        act.wait_ge(*E.at(f"BA{d}{z}", i))
                        nc.scalar.activation(LT[:, :, :], both(0)[:, :, 0:P], ACT.Copy).then_inc(*A.done(f"LT{d}{z}"))
                        act.wait_ge(*E.at(f"tB{d}{z}", i))
                        nc.scalar.activation(Bm[d][:, four, :], ps[:, 4, :].rearrange("p (n t) -> p n t", n=4),
                                             ACT.Copy).then_inc(*A.done(f"tB{d}{z}"))
                        act.wait_ge(*E.at(f"tK{d}{z}", i))
                        nc.scalar.activation(Km[d][:, four, :], ps[:, 5, :].rearrange("p (n t) -> p n t", n=4),
                                             ACT.Copy).then_inc(*A.done(f"tK{d}{z}"))
                        act.wait_ge(*E.at(f"V{d}{z}", i))
                        nc.scalar.activation(MV[d][:, four, :],
                                             ps[:, 6, 0:4 * C7].rearrange("p (n e) -> p n e", n=4), ACT.Copy)\
                            .then_inc(*A.done(f"V{d}{z}"))
                        act.wait_ge(*E.at(f"tX{d}{z}", i))
                        nc.scalar.activation(X[:, :, :], ps[:, 7, :].rearrange("p (n t) -> p n t", n=4), ACT.Copy)\
                            .then_inc(*A.done(f"X{d}{z}"))
                        for l in range(NL):
                            for a in range(2):
                                act.wait_ge(*E.at(f"Y{l}{d}{z}{a}", i))
                                nc.scalar.activation(Y[:, 2 * a:2 * a + 2, :],
                                                     ps[:, 4 + a, 0:2 * P].rearrange("p (n t) -> p n t", n=2),
                                                     ACT.Copy).then_inc(*A.done(f"Y{l}{d}{z}{a}"))
                    for n in range(NCH):
                        act.wait_ge(*E.at(f"U{n}", i))
                        nc.scalar.activation(US[:, :, :].rearrange("p d e -> p (d e)"), ps[:, 1, 0:2 * C7], ACT.Copy)\
                            .then_inc(*A.done(f"U{n}"))
                    act.wait_ge(*V.at("centred", i))
                    nc.scalar.activation(t1[:, :], ysum[:, :, :].rearrange("p n e -> p (n e)"), ACT.Square)\
                        .then_inc(*A.done("ysq"))
                    act.wait_ge(*V.at("var", i))
                    nc.scalar.activation(st[:, 1, :], st[:, 1, :], ACT.Ln, bias=gn_eps[:, :], scale=1.0 / C7)\
                        .then_inc(*A.done("ylog"))
                    act.wait_ge(*A.at("ylog", i))
                    nc.scalar.activation(st[:, 2, :], st[:, 1, :], ACT.Exp, scale=-0.5).then_inc(*A.done("yrs"))
                    act.wait_ge(*E.at("g", i))
                    act.wait_ge(*V.at("nkk", i))
                    nc.scalar.activation(nkk[:, :], ps[:, 7, :], ACT.Copy).then_inc(*A.done("g"))

            @block.vector
            def _(dve):
                V.start(dve)
                with dve.Fori(0, HP) as i:
                    r_, k_, v_ = cur(i), cur(i + HP), cur(i + 2 * HP)
                    dve.wait_ge(*Q.at("prm", i))
                    dve.wait_ge(*A.at("ysq", i - 1))
                    nc.vector.tensor_scalar(t1[:, :], k_, prm[:, 4:5], None, ALU.mult).then_inc(*V.done("kk"))
                    nc.vector.tensor_copy(vcp, v_).then_inc(*V.done("vcopy"))
                    dve.wait_ge(*A.at("norm", i))
                    nc.vector.tensor_scalar(t2[:, :], t2[:, :], 1e-12, None, ALU.max).then_inc(*V.done("floor"))
                    dve.wait_ge(*V.at("floor", i))
                    nc.vector.reciprocal(t2[:, :], t2[:, :]).then_inc(*V.done("inv"))
                    dve.wait_ge(*V.at("inv", i))
                    nc.vector.scalar_tensor_tensor(nkk[:, :], t1[:, :], -1.0, t2[:, :], ALU.mult, ALU.mult)\
                        .then_inc(*V.done("nkk"))
                    for d in range(2):
                        dve.wait_ge(*A.at(f"sa{d}", i))
                        if d:
                            dve.wait_ge(*V.at("R10", i))
                        nc.vector.tensor_tensor_scan(t2[:, :], resets[:, :], t1[:, :], 0.0, ALU.mult, ALU.add)\
                            .then_inc(*V.done(f"scan{d}"))
                        dve.wait_ge(*V.at(f"scan{d}", i))
                        if d == 0:
                            dve.wait_ge(*V.at("fac", i - 1))
                        nc.vector.tensor_copy(tot[:, d, :, None], chunks(t2)[:, :, C7 - 1:C7]).then_inc(*V.done(f"tot{d}"))
                        dve.wait_ge(*V.at(f"tot{d}", i))
                        nc.vector.scalar_tensor_tensor(chunks(t2), tot[:, d, :, None].to_broadcast([P, NCH, C7]), -0.5,
                                                       chunks(t2), ALU.mult, ALU.add).then_inc(*V.done(f"u1{d}"))
                        dve.wait_ge(*V.at(f"u1{d}", i))
                        nc.vector.tensor_tensor(t1[:, :], t2[:, :], t1[:, :], ALU.subtract).then_inc(*V.done(f"u2{d}"))
                        nc.vector.tensor_scalar(t3[:, :], av[:, :], -1.0, prm[:, 5:6], ALU.add, ALU.mult)\
                            .then_inc(*V.done(f"ka{d}"))
                        dve.wait_ge(*V.at(f"ka{d}", i))
                        nc.vector.scalar_tensor_tensor(av[:, :], nkk[:, :], -1.0, av[:, :], ALU.mult, ALU.mult)\
                            .then_inc(*V.done(f"b{d}"))
                        nc.vector.scalar_tensor_tensor(t3[:, :], t3[:, :], 1.0, k_, ALU.add, ALU.mult)\
                            .then_inc(*V.done(f"kdir{d}"))
                        dve.wait_ge(*V.at(f"kdir{d}", i))
                        if d == 0:
                            nc.vector.tensor_copy(ksum[:, :], t3[:, :]).then_inc(*V.done("ks0"))
                        else:
                            nc.vector.tensor_tensor(ksum[:, :], ksum[:, :], t3[:, :], ALU.add).then_inc(*V.done("ks1"))
                        dve.wait_ge(*E.at(f"dS{NCH - 1}", i - 1))
                        dve.wait_ge(*A.at(f"eB{d}", i))
                        g1, g2 = (t2, t1) if d == 0 else (t1, t2)
                        for w, dst, x, y, at in (("B", Bm[d], av, Y2, 0), ("K", Km[d], t3, Y2, 0),
                                                 ("R", AR[d], r_, g1, P), ("A", AR[d], nkk, g2, 0)):
                            if w == "R":
                                dve.wait_ge(*A.at(f"eR{d}", i))
                                dve.wait_ge(*E.at(f"y{NCH - 1}", i - 1))
                            if w == "A":
                                dve.wait_ge(*A.at(f"eA{d}", i))
                            x = x if w == "R" else x[:, :]
                            for hh in range(2):
                                rows = slice(hh * C7, (hh + 1) * C7)
                                nc.vector.tensor_tensor(
                                    dst[rows, :, at + hh * C7:at + (hh + 1) * C7],
                                    x[rows].rearrange("p (n t) -> p n t", n=NCH), chunks(y)[rows], ALU.mult)\
                                    .then_inc(*V.done(f"{w}{hh}{d}"))
                    dve.wait_ge(*A.at("half1", i))
                    nc.vector.tensor_tensor(fac[:, 0, 0:NCH - 1], half[:, 0, 0:NCH - 1], half[:, 0, 1:], ALU.mult)
                    nc.vector.tensor_tensor(fac[:, 1, 1:], half[:, 1, 1:], half[:, 1, 0:NCH - 1], ALU.mult)\
                        .then_inc(*V.done("fac"))
                    nc.vector.memset(ST[:, :, :], 0.0).then_inc(*V.done("state"))
                    for d, z in quads:
                        four = slice(4 * z, 4 * z + 4)
                        strict = mask[:, d, 0, :][:, None, :].to_broadcast([P, 4, P])
                        incl = mask[:, d, 1, :][:, None, :].to_broadcast([P, 4, P])
                        first2 = mask[:, d, 2, :][:, None, :].to_broadcast([P, 4, P])
                        dve.wait_ge(*A.at(f"LT{d}{z}", i))
                        nc.vector.tensor_tensor(PT[d][:, four, :], both(0)[:, :, P:], incl, ALU.mult)\
                            .then_inc(*V.done(f"PT{d}{z}"))
                        dve.wait_ge(*E.at(f"KA{d}{z}", i))
                        if (d, z) != (0, 0):
                            dve.wait_ge(*V.at("XT%d%d%d1" % (NL - 1, *((d, 0) if z else (d - 1, 1))), i))
                        nc.vector.tensor_tensor(MT[:, :, :], both(2)[:, :, 0:P], strict, ALU.mult)\
                            .then_inc(*V.done(f"MT{d}{z}"))
                        nc.vector.tensor_tensor(QT[:, :, :], both(2)[:, :, P:], incl, ALU.mult)\
                            .then_inc(*V.done(f"QT{d}{z}"))
                        dve.wait_ge(*A.at(f"V{d}{z}", i))
                        qv = ps[:, 6, 4 * C7:8 * C7].rearrange("p (n e) -> p n e", n=4)
                        if d == 0:
                            nc.vector.tensor_copy(ysum[:, four, :], qv).then_inc(*V.done(f"ysum{d}{z}"))
                        else:
                            nc.vector.tensor_tensor(ysum[:, four, :], ysum[:, four, :], qv, ALU.add)\
                                .then_inc(*V.done(f"ysum{d}{z}"))
                        dve.wait_ge(*A.at(f"LT{d}{z}", i))
                        xt = XT[d][:, four, :]
                        nc.vector.tensor_tensor(xt, LT[:, :, :], first2, ALU.mult).then_inc(*V.done(f"off{d}{z}"))
                        dve.wait_ge(*V.at(f"off{d}{z}", i))
                        nc.vector.tensor_tensor(xt, xt, c.ident[:, None, :].to_broadcast([P, 4, P]), ALU.add)\
                            .then_inc(*V.done(f"XT{d}{z}"))
                        for l in range(NL):
                            for a in range(2):
                                dve.wait_ge(*E.at(f"Z{l}{d}{z}{a}", i))
                                two = slice(2 * a, 2 * a + 2)
                                zz = ps[:, 6 + a, :].rearrange("p (w n t) -> p w n t", w=2, n=2)
                                nc.vector.tensor_tensor(X[:, two, :], X[:, two, :], zz[:, 0], ALU.add)\
                                    .then_inc(*V.done(f"X{l}{d}{z}{a}"))
                                xa = XT[d][:, 4 * z + 2 * a:4 * z + 2 * a + 2, :]
                                nc.vector.tensor_tensor(xa, xa, zz[:, 1], ALU.add)\
                                    .then_inc(*V.done(f"XT{l}{d}{z}{a}"))
                    for n in range(NCH):
                        at = (n, NCH - 1 - n)
                        dve.wait_ge(*E.at(f"z{n}", i))
                        for d in range(2):
                            nc.vector.tensor_tensor(Zs[:, d, :], MV[d][:, at[d], :], ps[:, 0, d * C7:(d + 1) * C7],
                                                    ALU.add).then_inc(*V.done(f"Z{d}{n}"))
                        dve.wait_ge(*E.at(f"dS{n}", i))
                        nc.vector.tensor_tensor(S1[:, :, :], ST[:, :, :], ps[:, 2:4, 0:C7], ALU.add)\
                            .then_inc(*V.done(f"S1{n}"))
                        dve.wait_ge(*V.at(f"S1{n}", i))
                        dve.wait_ge(*E.at(f"y{n}", i))
                        for d in range(2):
                            f = fac[:, d, at[d]:at[d] + 1] if n < NCH - 1 else 0.0
                            nc.vector.tensor_scalar(ST[:, d, :], S1[:, d, :], f, None, ALU.mult)\
                                .then_inc(*V.done(f"S{'fb'[d]}{n}"))
                        for d in range(2):
                            nc.vector.tensor_tensor(ysum[:, at[d], :], ysum[:, at[d], :], ps[:, 4 + d, 0:C7], ALU.add)\
                                .then_inc(*V.done(f"y{'fb'[d]}{n}"))
                            if d == 0:
                                dve.wait_ge(*V.at(f"yf{n}", i))
                    dve.wait_ge(*V.at(f"yb{NCH - 1}", i))
                    nc.vector.tensor_reduce(st[:, 0, :], ysum[:, :, :], AX.X, ALU.add).then_inc(*V.done("sum"))
                    dve.wait_ge(*V.at("sum", i))
                    nc.vector.tensor_scalar(st[:, 0, :], st[:, 0, :], 1.0 / C7, None, ALU.mult)\
                        .then_inc(*V.done("mean"))
                    dve.wait_ge(*V.at("mean", i))
                    nc.vector.tensor_tensor(ysum[:, :, :], ysum[:, :, :],
                                            st[:, 0, :, None].to_broadcast([P, NCH, C7]), ALU.subtract)\
                        .then_inc(*V.done("centred"))
                    dve.wait_ge(*A.at("ysq", i))
                    nc.vector.tensor_reduce(st[:, 1, :], chunks(t1), AX.X, ALU.add).then_inc(*V.done("var"))
                    dve.wait_ge(*A.at("yrs", i))
                    nc.vector.tensor_tensor(ysum[:, :, :], ysum[:, :, :],
                                            st[:, 2, :, None].to_broadcast([P, NCH, C7]), ALU.mult)\
                        .then_inc(*V.done("normed"))
                    nc.vector.scalar_tensor_tensor(t2[:, :], r_, prm[:, 6:7], ksum[:, :], ALU.mult, ALU.mult)\
                        .then_inc(*V.done("bonus1"))
                    dve.wait_ge(*E.at("bonus", i))
                    nc.vector.tensor_tensor(t2[:, :], v_, ps[:, 6, :], ALU.mult).then_inc(*V.done("bonus2"))
                    dve.wait_ge(*E.at("turn", i))
                    nc.vector.tensor_scalar(t3[:, :], ps[:, 5, :], prm[:, 7:8], prm[:, 8:9], ALU.mult, ALU.add)\
                        .then_inc(*V.done("lnw"))
                    dve.wait_ge(*V.at("lnw", i))
                    nc.vector.tensor_tensor(t3[:, :], t3[:, :], t2[:, :], ALU.add).then_inc(*V.done("plus"))
                    dve.wait_ge(*V.at("plus", i))
                    dve.wait_ge(*A.at("g", i))
                    nc.vector.tensor_tensor(cur2(out, i), t3[:, :], nkk[:, :], ALU.mult).then_inc(*V.done("out"))

            @block.tensor
            def _(pe):
                E.start(pe)
                with pe.Fori(0, HP) as i:
                    pe.wait_ge(*V.at("out", i - 1))
                    pe.wait_ge(*V.at("vcopy", i))
                    pe.wait_ge(*A.at("kk2", i))
                    nc.tensor.matmul(ps[:, 0, :], pair1[:, :], t2[:, :], start=True, stop=True).then_inc(*E.done("kk"))
                    for d in range(2):
                        pe.wait_ge(*Q.at("fix", i))
                        if d:
                            pe.wait_ge(*A.at("sa0", i))
                        rows = slice(d * C7, (d + 1) * C7)
                        nc.tensor.matmul(ps[:, 1, :], fix[rows, 0, :], u[rows, 12, :], start=True, stop=True)\
                            .then_inc(*E.done(f"w{d}"))
                        nc.tensor.matmul(ps[:, 2, :], fix[rows, 1, :], u[rows, 13, :], start=True, stop=True)\
                            .then_inc(*E.done(f"a{d}"))
                    for n in range(NCH):
                        for hh in range(2):
                            rows = slice(hh * C7, (hh + 1) * C7)
                            last = nc.tensor.matmul(ps[rows, 3, n * C7:(n + 1) * C7], vcp[rows, n * C7:(n + 1) * C7],
                                                    c.ident[rows, rows], start=True, stop=True)
                    last.then_inc(*E.done("vt"))
                    pe.wait_ge(*V.at("A11", i))
                    for d, z in quads:
                        pe.wait_ge(*A.at("vt", i))
                        prev = {(0, 1): (0, 0), (1, 0): (0, 1), (1, 1): (1, 0)}.get((d, z))
                        if prev:
                            pe.wait_ge(*V.at("XT%d%d%d1" % (NL - 1, *prev), i))
                        for m in range(4):
                            last = nc.tensor.matmul(both(0)[:, m, :], Bm[d][:, 4 * z + m, :], AR[d][:, 4 * z + m, :],
                                                    start=True, stop=True)
                        last.then_inc(*E.done(f"BA{d}{z}"))
                        for m in range(4):
                            last = nc.tensor.transpose(ps[:, 4, m * P:(m + 1) * P], Bm[d][:, 4 * z + m, :], c.ident[:, :])
                        last.then_inc(*E.done(f"tB{d}{z}"))
                        for m in range(4):
                            last = nc.tensor.matmul(both(2)[:, m, :], Km[d][:, 4 * z + m, :], AR[d][:, 4 * z + m, :],
                                                    start=True, stop=True)
                        last.then_inc(*E.done(f"KA{d}{z}"))
                        for m in range(4):
                            last = nc.tensor.transpose(ps[:, 5, m * P:(m + 1) * P], Km[d][:, 4 * z + m, :], c.ident[:, :])
                        last.then_inc(*E.done(f"tK{d}{z}"))
                        pe.wait_ge(*V.at(f"QT{d}{z}", i))
                        for m in range(4):
                            nc.tensor.matmul(ps[:, 6, m * C7:(m + 1) * C7], MT[:, m, :], vt[:, 4 * z + m, :],
                                             start=True, stop=True)
                            last = nc.tensor.matmul(ps[:, 6, (4 + m) * C7:(5 + m) * C7], QT[:, m, :],
                                                    vt[:, 4 * z + m, :], start=True, stop=True)
                        last.then_inc(*E.done(f"V{d}{z}"))
                        pe.wait_ge(*V.at(f"XT{d}{z}", i))
                        for m in range(4):
                            last = nc.tensor.transpose(ps[:, 7, m * P:(m + 1) * P], XT[d][:, 4 * z + m, :], c.ident[:, :])
                        last.then_inc(*E.done(f"tX{d}{z}"))
                        pe.wait_ge(*A.at(f"X{d}{z}", i))
                        for l in range(NL):
                            pe.wait_ge(*Q.at(f"CT{l}{d}{z}", i))
                            for a in range(2):
                                if l:
                                    pe.wait_ge(*V.at(f"XT{l - 1}{d}{z}{a}", i))
                                for m in range(2):
                                    last = nc.tensor.matmul(ps[:, 4 + a, m * P:(m + 1) * P], CT[:, 2 * a + m, :],
                                                            X[:, 2 * a + m, :], start=True, stop=True)
                                last.then_inc(*E.done(f"Y{l}{d}{z}{a}"))
                                pe.wait_ge(*A.at(f"Y{l}{d}{z}{a}", i))
                                for m in range(2):
                                    xt = XT[d][:, 4 * z + 2 * a + m, :]
                                    nc.tensor.matmul(ps[:, 6 + a, m * P:(m + 1) * P], xt, Y[:, 2 * a + m, :],
                                                     start=True, stop=True)
                                    last = nc.tensor.matmul(ps[:, 6 + a, (2 + m) * P:(3 + m) * P], Y[:, 2 * a + m, :],
                                                            xt, start=True, stop=True)
                                last.then_inc(*E.done(f"Z{l}{d}{z}{a}"))
                    pe.wait_ge(*V.at("XT%d111" % (NL - 1), i))
                    for n in range(NCH):
                        at = (n, NCH - 1 - n)
                        if n:
                            pe.wait_ge(*V.at(f"Sb{n - 1}", i))
                        for d in range(2):
                            last = nc.tensor.matmul(ps[:, 0, d * C7:(d + 1) * C7], AR[d][:, at[d], 0:P], ST[:, d, :],
                                                    start=True, stop=True)
                        last.then_inc(*E.done(f"z{n}"))
                        pe.wait_ge(*V.at(f"Z1{n}", i))
                        for d in range(2):
                            last = nc.tensor.matmul(ps[:, 1, d * C7:(d + 1) * C7], XT[d][:, at[d], :], Zs[:, d, :],
                                                    start=True, stop=True)
                        last.then_inc(*E.done(f"U{n}"))
                        pe.wait_ge(*A.at(f"U{n}", i))
                        for d in range(2):
                            nc.tensor.matmul(ps[:, 2 + d, 0:C7], Km[d][:, at[d], :], vt[:, at[d], :],
                                             start=True, stop=False)
                            last = nc.tensor.matmul(ps[:, 2 + d, 0:C7], Bm[d][:, at[d], :], US[:, d, :],
                                                    start=False, stop=True)
                        last.then_inc(*E.done(f"dS{n}"))
                        if n:
                            pe.wait_ge(*V.at(f"yb{n - 1}", i))
                        for d in range(2):
                            nc.tensor.matmul(ps[:, 4 + d, 0:C7], AR[d][:, at[d], P:], ST[:, d, :],
                                             start=True, stop=False)
                            last = nc.tensor.matmul(ps[:, 4 + d, 0:C7], PT[d][:, at[d], :], US[:, d, :],
                                                    start=False, stop=True)
                        last.then_inc(*E.done(f"y{n}"))
                    pe.wait_ge(*V.at("bonus1", i))
                    nc.tensor.matmul(ps[:, 6, :], pair1[:, :], t2[:, :], start=True, stop=True)\
                        .then_inc(*E.done("bonus"))
                    nc.tensor.matmul(ps[:, 7, :], fix[:, 2, :], u[:, 14, :], start=True, stop=False)
                    nc.tensor.matmul(ps[:, 7, :], fix[0:GATE_LORA - P, 3, :], u[0:GATE_LORA - P, 15, :],
                                     start=False, stop=True).then_inc(*E.done("g"))
                    for n in range(NCH):
                        for hh in range(2):
                            rows = slice(hh * C7, (hh + 1) * C7)
                            last = nc.tensor.matmul(ps[rows, 5, n * C7:(n + 1) * C7], ysum[rows, n, :],
                                                    c.ident[rows, rows], start=True, stop=True)
                    last.then_inc(*E.done("turn"))



def split_into(c, name, x, hi, lo):
    A = steps(c, f"{name}_act", ["hi"])
    with c.nc.Block() as block:
        @block.scalar
        def _(act):
            A.start(act)
            c.nc.scalar.activation(hi, x, ACT.Copy).then_inc(*A.done("hi"))

        @block.vector
        def _(dve):
            dve.wait_ge(*A.at("hi"))
            c.nc.vector.tensor_tensor(lo, x, hi.bitcast(F32), ALU.subtract)


def second_mixer(c):
    nc, ps = c.nc, c.ps
    N = DR // P
    with scope(c) as sb:
        hz = sb("hy_z", [P, N, T])
        H = steps(c, "hy_kept_act", [f"kept{m}" for m in range(N)])
        with scope(c) as sb2:
            u = sb2("hy_u", [P, 3 * N, T])
            with scope(c) as sb3:
                xh, xl = sb3("hy_xh", [P, KD, T], F32R), sb3("hy_xl", [P, KD, T], F32R)
                norm(c, "hy_n", ["mix_norm_2"], [(xh, xl)])
                three_taps(c, "hy_taps", 3, (xh, xl), u, vec_at(c, "hy_conv_w_2.0"), vec_at(c, "hy_conv_w_2.1"),
                           vec_at(c, "hy_conv_w_2.2"), vec_at(c, "hy_conv_b_2"))
            hyena(c, u)
            with nc.Block() as block:
                @block.scalar
                def _(act):
                    H.start(act)
                    for m in range(N):
                        nc.scalar.activation(hz[:, m, :], u[:, 2 * N + m, :], ACT.Copy).then_inc(*H.done(f"kept{m}"))
        u = sb("rw_u", [P, 4 * N, T])
        with scope(c) as sb3:
            xh, xl = sb3("rw_xh", [P, KD, T], F32R), sb3("rw_xl", [P, KD, T], F32R)
            norm(c, "rw_n", ["mix_norm_2"], [(xh, xl)])
            shifted(c, (xh, xl), u)
        rwkv7(c, u, u)
        yh, yl = sb("mix_yh", [P, 2 * N, T], F32R), sb("mix_yl", [P, 2 * N, T], F32R)
        split_into(c, "hy_split", hz[:, :, :], yh[:, 0:N, :], yl[:, 0:N, :])
        split_into(c, "rw_split", u[:, 0:N, :], yh[:, N:, :], yl[:, N:, :])
        gates = u
        mh, ml = sb("mix_mh", [P, KD, T], F32R), sb("mix_ml", [P, KD, T], F32R)
        norm(c, "gate_n", ["mix_norm_2"], [(mh, ml)])
        project(c, "mix_gates", 4, (mh, ml), gates, func=ACT.Sigmoid)
        parts = sb("mix_parts", [P, 3, 2, T])
        A = steps(c, "merge_act", ["hi0", "hi1"])
        V = steps(c, "merge_dve", [f"{w}{t}" for t in range(2) for w in ("hyena", "rwkv", "sum", "lo")])

        def act_evac(act, i, q):
            if q % 2:
                t = q // 2
                act.wait_ge(*V.at(f"sum{t}", i))
                nc.scalar.activation(mh[:, ds(i * 4 + 2 * t, 2), :], parts[:, 2, :, :], ACT.Copy)\
                    .then_inc(*A.done(f"hi{t}"))

        def dve_evac(dve, i, q):
            if q % 2:
                t = q // 2
                at = i * 4 + 2 * t
                if t:
                    dve.wait_ge(*V.at("lo0", i))
                else:
                    dve.wait_ge(*V.at("lo1", i - 1))
                nc.vector.tensor_tensor(parts[:, 0, :, :], gates[:, ds(at, 2), :], ps[:, 0:2, :], ALU.mult)\
                    .then_inc(*V.done(f"hyena{t}"))
                nc.vector.tensor_tensor(parts[:, 1, :, :], gates[:, ds(at + KD, 2), :], ps[:, 2:4, :], ALU.mult)\
                    .then_inc(*V.done(f"rwkv{t}"))
                dve.wait_ge(*V.at(f"rwkv{t}", i))
                nc.vector.tensor_tensor(parts[:, 2, :, :], parts[:, 0, :, :], parts[:, 1, :, :], ALU.add)\
                    .then_inc(*V.done(f"sum{t}"))
                dve.wait_ge(*A.at(f"hi{t}", i))
                nc.vector.tensor_tensor(ml[:, ds(at, 2), :], parts[:, 2, :, :], mh[:, ds(at, 2), :].bitcast(F32),
                                        ALU.subtract).then_inc(*V.done(f"lo{t}"))

        body = [[(2 * t + b, True, True, [(b * N + k, b * N + k) for k in range(N)]) for b in range(2)]
                for t in range(2)]
        dense(c, 2, body, lambda q, k: (yh[:, k, :], yl[:, k, :]), act_evac, dve_evac, A, V,
              [(V, f"{w}{t}") for t in range(2) for w in ("hyena", "rwkv")])
        residual(c, "mix_out", 2, simple(2), lambda q, k: (mh[:, k, :], ml[:, k, :]))


def program(nc, io):
    with ExitStack() as ctx:
        c = allocate(nc, ctx, io)
        prologue(c, io["x"])
        gated_delta(c)
        swiglu(c, "ffn0", "ln_ffn.0")
        per_layer_embedding(c, 0)
        stick_breaking(c)
        swiglu(c, "ffn1", "ln_ffn.1")
        per_layer_embedding(c, 1)
        swiglu(c, "ffn2", "ffn1_norm_2", 0.5)
        second_mixer(c)
        swiglu(c, "ffn3", "ffn2_norm_2", 0.5)
        final = c.sb("final", [P, KD, T])
        stored = ctx.enter_context(nc.semaphore("out_stored"))
        norm(c, "final", ["final_norm_2"], [], keep=final)
        with nc.Block() as block:
            @block.sync
            def _(sp):
                sp.dma_start(io["out"], final[:, :, :]).then_inc(stored, 16)
                sp.wait_ge(stored, 16)


def doubling_masks(n, upper=False, copies=1):
    s, t = np.meshgrid(np.arange(n), np.arange(n), indexing="ij")
    out = []
    size = 1
    while size < n:
        new = (s // (2 * size) == t // (2 * size)) & (s // size < t // size)
        out.append(new.T if upper else new)
        size *= 2
    return [np.kron(np.eye(copies), m).astype(np.float32) for m in out]


def hyena_features():
    pos = np.arange(T, dtype=np.float64)
    ang = 2 * np.pi / T * pos
    bands = np.linspace(1e-4, 15, 16)
    rows = [pos / (T - 1)] + [np.cos(b * ang) for b in bands] + [-np.sin(b * ang) for b in bands]
    return np.stack(rows).astype(np.float32)


def hyena_positions():
    t = -(np.arange(T) / (T - 1)).reshape(T // P, P).T
    return np.concatenate([t, (np.arange(P) > 0)[:, None]], 1).astype(np.float32)


def trig_matrices():
    s, j = np.meshgrid(np.arange(T), np.arange(T), indexing="ij")
    a = 2 * np.pi * ((2 * j + 1) * s % (4 * T)) / (4 * T)
    mats = [np.cos(a), np.sin(a), np.cos(a).T, np.sin(a).T]
    return np.stack([m.reshape(T // P, P, T).transpose(1, 0, 2) for m in mats]).astype(np.float32)


def rwkv_lora(w2, a2, g2):
    lora = np.zeros((P, 4, DR), np.float32)
    lora[:, 0], lora[:, 1] = w2.reshape(P, DR), a2.reshape(P, DR)
    lora[:, 2], lora[:g2.shape[0] - P, 3] = g2[:P], g2[P:]
    return lora


def rwkv_masks(upper):
    strict = np.tri(C7, k=-1).T
    strict, full = (strict.T, np.tri(C7)) if upper else (strict, np.tri(C7).T)
    first = [np.kron(np.eye(2), m).astype(np.float32) for m in (strict, full)]
    return np.stack(first + doubling_masks(C7, upper, 2), 1)


def host_arrays(inputs):
    def of(name):
        base, _, i = name.rpartition(".")
        if base:
            return of(base)[int(i)]
        return np.asarray(inputs[name])

    weights = np.zeros((N_WT, P, WK, WN), np.float32)
    for t, (names, parts) in enumerate(weight_plan()):
        mats = [of(n) for n in names.split("|")]
        for r, col, k, which, rows, cols in parts:
            weights[t, :rows, k, :cols] = mats[which][r:r + rows, col:col + cols]
    vectors = np.zeros((P, N_VEC), np.float32)
    for name, n in VECTORS:
        v = of(name).reshape(-1)
        full = np.zeros(n * P, np.float32)
        full[:v.size] = v
        vectors[:, VCOL[name]:VCOL[name] + n] = full.reshape(n, P).T
    return {
        "weights": weights.reshape(N_WT, P, WT),
        "vectors": vectors,
        "gdn_w_ab": np.ascontiguousarray(
            of("gdn_w_in.0")[:, 4 * DM:].reshape(KD, P, 2 * HEADS).transpose(1, 0, 2)),
        "gdn_ab": np.stack([of("gdn_a_log.0"), of("gdn_dt_bias.0")], 1),
        "gdn_masks": np.stack([np.where(np.tri(P).T > 0, 0, -1e30).astype(np.float32)] + doubling_masks(P), 1),
        "sb_mats": np.stack([np.tri(P, k=-1).T, -np.tri(P, k=-1), -np.ones((P, P))], 1).astype(np.float32),
        "hy_feats": hyena_features(),
        "hy_w1": of("hy_ffn_w1_2"), "hy_w2": of("hy_ffn_w2_2"),
        "hy_cols": np.stack([of("hy_ffn_b1_2"), of("hy_ffn_b2_2"), of("hy_sin_freq_2")], 1),
        "hy_w3": np.concatenate([of("hy_ffn_w3_2"), of("hy_ffn_b3_2")[None]]),
        "hy_decay": of("hy_decay_2").reshape(-1),
        "hy_trig": trig_matrices(), "hy_tpos": hyena_positions(),
        "rw_lora": rwkv_lora(of("rw_w2_2"), of("rw_a2_2"), of("rw_g2_2")),
        "rw_masks": np.stack([rwkv_masks(False), rwkv_masks(True)], 1),
        "rw_pair": np.kron(np.eye(2), np.ones((C7, C7))).astype(np.float32),
        "rw_resets": (np.arange(T) % C7 > 0).astype(np.float32),
        "identity": np.eye(P, dtype=np.float32),
        "x": np.ascontiguousarray(of("x")[0].T.reshape(KD, P, T).transpose(1, 0, 2)),
        "p": np.ascontiguousarray(of("p")[:, 0].transpose(0, 2, 1).reshape(2, 2, P, T).transpose(0, 2, 1, 3)),
    }


def kernel(**inputs):
    import concourse.bacc as _bacc
    from concourse.bass_utils import run_bass_kernel_spmd as _run

    nc = _bacc.Bacc("TRN2", target_bir_lowering=False, num_devices=1)
    arrays, io = {}, {}
    for name, a in host_arrays(inputs).items():
        arrays[f"in_{name}"] = np.ascontiguousarray(a)
        io[name] = nc.dram_tensor(f"in_{name}", a.shape, mybir.dt.float32, kind="ExternalInput").ap()
    io["out"] = nc.dram_tensor("out", (P, KD, T), mybir.dt.float32, kind="ExternalOutput").ap()
    program(nc, io)
    got = _run(nc, [arrays], core_ids=[0]).results[0]["out"]
    return np.ascontiguousarray(got.transpose(2, 1, 0).reshape(1, T, DM))
```

```python
import numpy as np
from contextlib import ExitStack

import concourse.bass as bass
from concourse import mybir

ALU = mybir.AluOpType
ACT = mybir.ActivationFunctionType
AX = mybir.AxisListType
F32 = mybir.dt.float32
F32R = mybir.dt.float32r

P = 128
T = 512
DM = 1024
KD = DM // P
HEADS = 8
HID = 2816
KH = HID // P
EPS = 1e-6
WK, WN = 8, 256
WT = WK * WN
DR = 512
C7 = 64
SCALE = P ** -0.5


def weight_plan():
    plan = []

    def block(name, r0, rows, c0, cols):
        plan.append((name, [(r0 + k * P, c0, k, 0, P, cols) for k in range(rows // P)]))

    def columns(name, c0, cols, rows=DM):
        for c in range(c0, c0 + cols, WN):
            block(name, 0, rows, c, min(WN, c0 + cols - c))

    def ffn(w_in, w_out):
        for g in range(HID // WN):
            block(w_in, 0, DM, g * WN, WN)
            block(w_in, 0, DM, HID + g * WN, WN)
        for c in range(0, DM, WN):
            for r in range(0, HID, WK * P):
                block(w_out, r, min(WK * P, HID - r), c, WN)

    def ple(i):
        for c in range(0, DM, WN):
            block(f"ple_w_proj.{i}", 0, 256, c, WN)
            block(f"ple_w_gate.{i}", 0, DM, c, WN)

    columns("gdn_w_in.0", 0, 4 * DM)
    columns("gdn_w_out.0", 0, DM)
    ffn("ffn_w_in.0", "ffn_w_out.0")
    ple(0)
    columns("w_kv", 0, 2 * DM)
    columns("sb_w_q.0", 0, DM)
    columns("sb_w_out.0", 0, DM)
    ffn("ffn_w_in.1", "ffn_w_out.1")
    ple(1)
    ffn("ffn1_w_gu_2", "ffn1_w_down_2")
    columns("w_in_2", 0, 3 * DR)
    columns("w_in_2", 3 * DR, 3 * DR)
    columns("w_in_2", 6 * DR, 256)
    columns("w_in_2", 6 * DR + 256, 160)
    columns("w_in_2", 6 * DR + 416, 2 * DM)
    for c in range(0, DM, WN):
        plan.append(("hy_out_2|rw_out_2", [(k * P, c, k, 0, P, WN) for k in range(DR // P)]
                     + [(k * P, c, DR // P + k, 1, P, WN) for k in range(DR // P)]))
    columns("w_out_2", 0, DM)
    ffn("ffn2_w_gu_2", "ffn2_w_down_2")
    return plan


N_WT = len(weight_plan())

VECTORS = [("ln_mix.0", 8), ("ln_mix.1", 8), ("ln_ffn.0", 8), ("ln_ffn.1", 8), ("ln_ple.0", 8), ("ln_ple.1", 8),
           ("kv_norm", 8), ("ffn1_norm_2", 8), ("mix_norm_2", 8), ("ffn2_norm_2", 8), ("final_norm_2", 8),
           ("gdn_norm.0", 1), ("k_norm", 1), ("sb_q_norm.0", 1),
           ("gdn_conv.0.0", 24), ("gdn_conv.0.1", 24), ("gdn_conv.0.2", 24), ("gdn_conv.0.3", 24),
           ("hy_conv_w_2.0", 12), ("hy_conv_w_2.1", 12), ("hy_conv_w_2.2", 12), ("hy_conv_b_2", 12),
           ("hy_bias_d_2.0", 4), ("hy_bias_d_2.1", 4),
           ("rw_mu_2.0", 16), ("rw_mu_2.1", 16),
           ("rw_w0_2.0", 4), ("rw_w0_2.1", 4), ("rw_a0_2.0", 4), ("rw_a0_2.1", 4),
           ("rw_k_k_2", 4), ("rw_k_a_2", 4), ("rw_r_k_2", 4), ("rw_ln_w_2", 4), ("rw_ln_b_2", 4)]
VCOL = {}
for _name, _n in VECTORS:
    VCOL[_name] = sum(n for _, n in VECTORS[:len(VCOL)])
N_VEC = sum(n for _, n in VECTORS)


LOG_EXP = "natural_log_exp_and_others"


class Steps:

    def __init__(self, sem, names):
        self.sem, self.names, self.next = sem, list(names), 0
        assert len(set(self.names)) == len(self.names)

    def start(self, engine):
        engine.sem_inc(self.sem, len(self.names))

    def done(self, step):
        assert self.names[self.next] == step, (self.names[self.next], step)
        self.next = (self.next + 1) % len(self.names)
        return self.sem, 1

    def at(self, step, iteration=0):
        return self.sem, iteration * len(self.names) + (len(self.names) + self.names.index(step) + 1)


class Chip:
    pass


def allocate(nc, ctx, io):
    c = Chip()
    c.nc, c.io, c.scopes = nc, io, [ctx]

    def sb(name, shape, dt=F32):
        return c.scopes[-1].enter_context(nc.sbuf_tensor(name, shape, dt))

    def sem(name):
        return ctx.enter_context(nc.semaphore(name))

    c.sb = sb
    c.wraw = sb("wraw", [P, 2, WT])
    c.whi = sb("whi", [P, 2, WT], F32R)
    c.wlo = sb("wlo", [P, 2, WT], F32R)
    c.h = sb("h", [P, KD, T])
    c.vec = sb("vec", [P, N_VEC])
    c.ident = sb("ident", [P, P])
    c.ones = sb("ones", [P, P])
    c.eps = sb("eps", [P, 1])
    c.ps = ctx.enter_context(nc.psum_tensor("ps", [P, 8, T], F32))
    c.raw_loaded = [sem("raw_loaded_even"), sem("raw_loaded_odd")]
    c.hi_ready, c.lo_ready, c.tile_done = sem("hi_ready"), sem("lo_ready"), sem("tile_done")
    c.tile, c.stage = 0, 0
    return c


class scope:

    def __init__(self, c):
        self.c = c

    def __enter__(self):
        self.c.scopes.append(ExitStack())
        return self.c.sb

    def __exit__(self, *a):
        self.c.scopes.pop().close()


def steps(c, name, names):
    c.stage += 1
    return Steps(c.scopes[-1].enter_context(c.nc.semaphore(f"{name}_{c.stage}")), names)


def vcol(c, name, k=0, n=1):
    at = VCOL[name] + k
    return c.vec[:, at:at + n]


def ring_load(c, sp, j, t, known):
    if known is None or known + 4 < N_WT:
        sp.wait_ge(c.lo_ready, j + 3)
        sp.dma_start(c.wraw[:, t, :], c.io["weights"][j + 4]).then_inc(c.raw_loaded[t], 16)


def ring_hi(c, act, j, half, t, known):
    act.wait_ge(c.tile_done, j + 1)
    if known is None or known + 2 < N_WT:
        act.wait_ge(c.raw_loaded[t], half * 16 + 32)
        c.nc.scalar.activation(c.whi[:, t, :], c.wraw[:, t, :], ACT.Copy).then_inc(c.hi_ready, 1)


def ring_lo(c, dve, j, t, known):
    if known is None or known + 2 < N_WT:
        dve.wait_ge(c.hi_ready, j + 3)
        c.nc.vector.tensor_tensor(c.wlo[:, t, :], c.wraw[:, t, :], c.whi[:, t, :].bitcast(F32),
                                  ALU.subtract).then_inc(c.lo_ready, 1)
    else:
        dve.wait_ge(c.tile_done, j + 1)


def simple(groups, ks=KD):
    return [[(q, True, True, [(k, k) for k in range(ks)])] for q in range(groups)]


def dense(c, iters, body, x_of, act_evac, dve_evac, act_steps, dve_steps, frees, tokens_out=False):
    nc, ps = c.nc, c.ps
    u, n_groups = len(body), 1 + max(part[0] for tile in body for part in tile)
    base = c.tile
    assert base % 2 == 0 and u % 2 == 0 and n_groups % 2 == 0
    loops = iters
    while loops > 0 and base + loops * u + 4 > N_WT:
        loops -= 1
    if loops < 2:
        loops = 0

    def run(e, emit):
        if loops:
            with e.Fori(0, loops) as i:
                for r in range(u):
                    emit(e, i, r, i * u + (base + r), i * (u // 2) + (base + r) // 2, None)
        for i in range(loops, iters):
            for r in range(u):
                j = base + i * u + r
                emit(e, i, r, j, j // 2, j)

    def closed(r):
        return [q for q, _, closes, _ in body[r] if closes]

    with nc.Block() as block:
        @block.sync
        def _(sp):
            run(sp, lambda e, i, r, j, half, known: ring_load(c, e, j, r % 2, known))

        @block.scalar
        def _(act):
            if act_steps:
                act_steps.start(act)

            def emit(e, i, r, j, half, known):
                ring_hi(c, e, j, half, r % 2, known)
                for q in closed(r):
                    act_evac(e, i, q)
            run(act, emit)

        @block.vector
        def _(dve):
            if dve_steps:
                dve_steps.start(dve)

            def emit(e, i, r, j, half, known):
                ring_lo(c, e, j, r % 2, known)
                for q in closed(r):
                    dve_evac(e, i, q)
            run(dve, emit)

        @block.tensor
        def _(pe):
            def emit(e, i, r, j, half, known):
                t = r % 2
                e.wait_ge(c.lo_ready, j + 1)
                for q, opens, closes, ks in body[r]:
                    if opens:
                        before, of = (q - 2, i) if q >= 2 else (q - 2 + n_groups, i - 1)
                        e.wait_ge(*frees[before][0].at(frees[before][1], of))
                    pair = ps[:, 2 * (q % 2):2 * (q % 2) + 2, :]
                    if tokens_out:
                        pair = pair.rearrange("p b (a n) -> p (b a) n", n=WN)
                    for m in range(T // P if tokens_out else WN // P):
                        for n, (kw, kx) in enumerate(ks):
                            for wa, xa in ((0, 0), (0, 1), (1, 0)):
                                w = (c.whi, c.wlo)[wa]
                                x = x_of(q, kx)[xa]
                                if tokens_out:
                                    a, b = x[:, m * P:(m + 1) * P], w[:, t, kw * WN:(kw + 1) * WN]
                                else:
                                    a, b = w[:, t, kw * WN + m * P:kw * WN + (m + 1) * P], x
                                last = nc.tensor.matmul(pair[:, m, :], a, b, start=opens and n == 0 and wa + xa == 0,
                                                        stop=closes and n == len(ks) - 1 and wa == 1)
                last.then_inc(c.tile_done, 1)
            run(pe, emit)
    c.tile += iters * u


def prologue(c, x_in):
    nc, io = c.nc, c.io
    with scope(c):
        const_loaded = c.scopes[-1].enter_context(nc.semaphore("const_loaded"))
        with nc.Block() as block:
            @block.sync
            def _(sp):
                for t in range(2):
                    sp.dma_start(c.wraw[:, t, :], io["weights"][t]).then_inc(c.raw_loaded[t], 16)
                sp.dma_start(c.h[:, :, :], x_in).then_inc(const_loaded, 16)
                sp.dma_start(c.vec[:, :], io["vectors"]).then_inc(const_loaded, 16)
                sp.dma_start(c.ident[:, :], io["identity"]).then_inc(const_loaded, 16)
                for t in range(2):
                    sp.wait_ge(c.lo_ready, t + 1)
                    sp.dma_start(c.wraw[:, t, :], io["weights"][t + 2]).then_inc(c.raw_loaded[t], 16)
                sp.wait_ge(const_loaded, 48)

            @block.scalar
            def _(act):
                for t in range(2):
                    act.wait_ge(c.raw_loaded[t], 16)
                    nc.scalar.activation(c.whi[:, t, :], c.wraw[:, t, :], ACT.Copy).then_inc(c.hi_ready, 1)

            @block.vector
            def _(dve):
                nc.vector.memset(c.ones[:, :], 1.0)
                nc.vector.memset(c.eps[:, :], EPS)
                for t in range(2):
                    dve.wait_ge(c.hi_ready, t + 1)
                    nc.vector.tensor_tensor(c.wlo[:, t, :], c.wraw[:, t, :], c.whi[:, t, :].bitcast(F32),
                                            ALU.subtract).then_inc(c.lo_ready, 1)


def norm(c, name, gains, outs, keep=None, after=None):
    nc, h, ps = c.nc, c.h, c.ps
    n_out = len(gains)
    with scope(c) as sb:
        sq = sb(f"{name}_sq", [P, KD, T])
        total = sb(f"{name}_total", [P, 2, T])
        rstd = sb(f"{name}_rstd", [P, T])
        xf = keep if keep is not None else sq
        A = steps(c, f"{name}_act", ["square0", "square1", "log", "rstd"]
                  + [f"hi{o}{k}" for o in range(len(outs)) for k in range(KD)])
        on_pool = (1, 3, 5, 7) if outs else ()
        V = steps(c, f"{name}_dve", ["total0", "total1"] + [
            x for o in range(n_out) for x in [f"x{o}{k}" for k in range(KD)]
            + [f"lo{o}{k}" for k in range(KD) if outs and k not in on_pool]])
        Q = steps(c, f"{name}_pool", [f"lo{o}{k}" for o in range(n_out) for k in on_pool])
        E = steps(c, f"{name}_pe", ["sum"])
        with nc.Block() as block:
            @block.scalar
            def _(act):
                A.start(act)
                nc.scalar.preload_act_table_set(LOG_EXP)
                for n in range(2):
                    s = slice(n * KD // 2, (n + 1) * KD // 2)
                    nc.scalar.activation(sq[:, s, :], h[:, s, :], ACT.Square).then_inc(*A.done(f"square{n}"))
                act.wait_ge(*E.at("sum"))
                nc.scalar.activation(rstd[:, :], ps[:, 4, :], ACT.Ln, bias=c.eps[:, :], scale=1.0 / DM)\
                    .then_inc(*A.done("log"))
                act.wait_ge(*A.at("log"))
                nc.scalar.activation(rstd[:, :], rstd[:, :], ACT.Exp, scale=-0.5).then_inc(*A.done("rstd"))
                if outs:
                    for o in range(n_out):
                        for k in range(KD):
                            act.wait_ge(*V.at(f"x{o}{k}"))
                            nc.scalar.activation(outs[o][0][:, k, :], xf[:, k, :], ACT.Copy)\
                                .then_inc(*A.done(f"hi{o}{k}"))

            @block.vector
            def _(dve):
                V.start(dve)
                for n in range(2):
                    dve.wait_ge(*A.at(f"square{n}"))
                    s = slice(n * KD // 2, (n + 1) * KD // 2)
                    nc.vector.tensor_reduce(total[:, n, :], sq[:, s, :].rearrange("p k t -> p t k"), AX.X, ALU.add)\
                        .then_inc(*V.done(f"total{n}"))
                dve.wait_ge(*A.at("rstd"))
                for o in range(n_out):
                    for k in range(KD):
                        if o > 0:
                            dve.wait_ge(*(Q if k in on_pool else V).at(f"lo{o - 1}{k}"))
                        nc.vector.scalar_tensor_tensor(xf[:, k, :], h[:, k, :], vcol(c, gains[o], k), rstd[:, :],
                                                       ALU.mult, ALU.mult).then_inc(*V.done(f"x{o}{k}"))
                    for k in range(KD):
                        if not outs or k in on_pool:
                            continue
                        dve.wait_ge(*A.at(f"hi{o}{k}"))
                        nc.vector.tensor_tensor(outs[o][1][:, k, :], xf[:, k, :], outs[o][0][:, k, :].bitcast(F32),
                                                ALU.subtract).then_inc(*V.done(f"lo{o}{k}"))

            @block.gpsimd
            def _(pool):
                if on_pool:
                    Q.start(pool)
                for o in range(n_out):
                    for k in on_pool:
                        pool.wait_ge(*A.at(f"hi{o}{k}"))
                        nc.gpsimd.tensor_tensor(outs[o][1][:, k, :], xf[:, k, :], outs[o][0][:, k, :].bitcast(F32),
                                                ALU.subtract).then_inc(*Q.done(f"lo{o}{k}"))

            @block.tensor
            def _(pe):
                E.start(pe)
                for n in range(2):
                    pe.wait_ge(*V.at(f"total{n}"))
                    last = nc.tensor.matmul(ps[:, 4, :], c.ones[:, :], total[:, n, :], start=n == 0, stop=n == 1)
                last.then_inc(*E.done("sum"))
                if after:
                    pe.wait_ge(*V.at(f"x0{KD - 1}"))
                    after(pe, xf)


def residual(c, name, iters, body, x_of, scale=1.0):
    nc, h, ps = c.nc, c.h, c.ps
    V = steps(c, f"{name}_dve", ["h0", "h1"])

    def dve_evac(dve, i, q):
        at = i * 4 + 2 * q
        pair = ps[:, 2 * (q % 2):2 * (q % 2) + 2, :]
        nc.vector.scalar_tensor_tensor(h[:, ds(at, 2), :], pair, scale, h[:, ds(at, 2), :],
                                       ALU.mult, ALU.add).then_inc(*V.done(f"h{q}"))

    dense(c, iters, body, x_of, lambda act, i, q: None, dve_evac, None, V, [(V, "h0"), (V, "h1")])


def ds(at, n):
    return slice(at, at + n) if isinstance(at, int) else bass.ds(at, n)


def swiglu(c, name, gain, scale=1.0):
    nc, ps = c.nc, c.ps
    with scope(c) as sb:
        xh, xl = sb(f"{name}_xh", [P, KD, T], F32R), sb(f"{name}_xl", [P, KD, T], F32R)
        norm(c, f"{name}_n", [gain], [(xh, xl)])
        uh, ul = sb(f"{name}_uh", [P, KH, T], F32R), sb(f"{name}_ul", [P, KH, T], F32R)
        with scope(c) as sb2:
            gate = sb2(f"{name}_gate", [P, 2, T])
            unit = sb2(f"{name}_unit", [P, 2, T])
            A = steps(c, f"{name}_act", ["gate", "hi"])
            V = steps(c, f"{name}_dve", ["unit", "lo"])

            def act_evac(act, i, q):
                if q == 0:
                    act.wait_ge(*V.at("unit", i - 1))
                    nc.scalar.activation(gate[:, :, :], ps[:, 0:2, :], ACT.Silu).then_inc(*A.done("gate"))
                    return
                act.wait_ge(*V.at("unit", i))
                nc.scalar.activation(uh[:, ds(i * 2, 2), :], unit[:, :, :], ACT.Copy).then_inc(*A.done("hi"))

            def dve_evac(dve, i, q):
                if q == 0:
                    return
                dve.wait_ge(*A.at("gate", i))
                dve.wait_ge(*V.at("lo", i - 1))
                nc.vector.tensor_tensor(unit[:, :, :], gate[:, :, :], ps[:, 2:4, :], ALU.mult)\
                    .then_inc(*V.done("unit"))
                dve.wait_ge(*A.at("hi", i))
                nc.vector.tensor_tensor(ul[:, ds(i * 2, 2), :], unit[:, :, :], uh[:, ds(i * 2, 2), :].bitcast(F32),
                                        ALU.subtract).then_inc(*V.done("lo"))

            dense(c, HID // WN, simple(2), lambda q, k: (xh[:, k, :], xl[:, k, :]), act_evac, dve_evac,
                  A, V, [(A, "gate"), (V, "unit")])
        down = []
        for q in range(2):
            for k0 in range(0, KH, WK):
                ks = range(k0, min(k0 + WK, KH))
                down.append([(q, k0 == 0, k0 + WK >= KH, [(k - k0, k) for k in ks])])
        residual(c, f"{name}_down", DM // WN // 2, down, lambda q, k: (uh[:, k, :], ul[:, k, :]), scale)


def group_pair(c, q):
    return c.ps[:, 2 * (q % 2):2 * (q % 2) + 2, :]


def gated_delta(c):
    nc, ps, io = c.nc, c.ps, c.io
    NC = T // P
    with scope(c) as sb:
        gate = sb("gdn_gate", [P, HEADS, T])
        G8 = sb("gdn_G8", [HEADS, T])
        beta8 = sb("gdn_beta8", [HEADS, T])
        xh = sb("gdn_xh", [P, KD, T], F32R)
        xl = sb("gdn_xl", [P, KD, T], F32R)
        with scope(c) as sb2:
            wab = sb2("gdn_wab", [P, KD, 2 * HEADS])
            neg_a = sb2("gdn_neg_a", [HEADS, 2])
            small = sb2("gdn_small", [HEADS, 4, T])
            loaded = c.scopes[-1].enter_context(nc.semaphore("gdn_small_loaded"))
            ab = steps(c, "gdn_ab_pe", ["a", "b"])

            def after(pe, xf):
                ab.start(pe)
                pe.wait_ge(loaded, 32)
                for n in range(2):
                    for k in range(KD):
                        last = nc.tensor.matmul(ps[0:HEADS, 5 + n, :], wab[:, k, n * HEADS:(n + 1) * HEADS],
                                                xf[:, k, :], start=k == 0, stop=k == KD - 1)
                    last.then_inc(*ab.done("ab"[n]))

            with nc.Block() as block:
                @block.gpsimd
                def _(pool):
                    pool.dma_start(wab[:, :, :], io["gdn_w_ab"]).then_inc(loaded, 16)
                    pool.dma_start(neg_a[:, :], io["gdn_ab"]).then_inc(loaded, 16)
            norm(c, "gdn_n", ["ln_mix.0"], [(xh, xl)], after=after)
            A = steps(c, "gdn_gates_act", ["ea", "abs", "exp", "log", "beta"])
            V = steps(c, "gdn_gates_dve", ["x", "sp", "na", "g"] + [f"G{n}" for n in range(NC)])
            with nc.Block() as block:
                @block.vector
                def _(dve):
                    V.start(dve)
                    nc.vector.tensor_scalar(small[:, 0, :], ps[0:HEADS, 5, :], neg_a[:, 1:2], None, ALU.add)\
                        .then_inc(*V.done("x"))
                    dve.wait_ge(*A.at("log"))
                    nc.vector.scalar_tensor_tensor(small[:, 2, :], small[:, 0, :], 0.0, small[:, 1, :],
                                                   ALU.max, ALU.add).then_inc(*V.done("sp"))
                    nc.vector.tensor_scalar(neg_a[:, 0:1], neg_a[:, 0:1], -1.0, None, ALU.mult)\
                        .then_inc(*V.done("na"))
                    dve.wait_ge(*V.at("na"))
                    nc.vector.tensor_scalar(small[:, 3, :], small[:, 2, :], neg_a[:, 0:1], None, ALU.mult)\
                        .then_inc(*V.done("g"))
                    dve.wait_ge(*V.at("g"))
                    for n in range(NC):
                        nc.vector.tensor_tensor_scan(G8[:, n * P:(n + 1) * P], c.ones[0:HEADS, :],
                                                     small[:, 3, n * P:(n + 1) * P], 0.0, ALU.mult, ALU.add)\
                            .then_inc(*V.done(f"G{n}"))

                @block.scalar
                def _(act):
                    A.start(act)
                    nc.scalar.activation(neg_a[:, 0:1], neg_a[:, 0:1], ACT.Exp).then_inc(*A.done("ea"))
                    act.wait_ge(*V.at("x"))
                    nc.scalar.activation(small[:, 1, :], small[:, 0, :], ACT.Abs).then_inc(*A.done("abs"))
                    act.wait_ge(*A.at("abs"))
                    nc.scalar.activation(small[:, 1, :], small[:, 1, :], ACT.Exp, scale=-1.0).then_inc(*A.done("exp"))
                    act.wait_ge(*A.at("exp"))
                    nc.scalar.activation(small[:, 1, :], small[:, 1, :], ACT.Ln, bias=c.ones[0:HEADS, 0:1])\
                        .then_inc(*A.done("log"))
                    nc.scalar.activation(beta8[:, :], ps[0:HEADS, 6, :], ACT.Sigmoid).then_inc(*A.done("beta"))

        qkv = sb("gdn_qkv", [P, 3 * HEADS, T])
        with scope(c) as sb2:
            padded = sb2("gdn_padded", [P, 2, 2, 3 + T])
            conv = sb2("gdn_conv_out", [P, 2, 2, T])
            taps = range(4)
            A = steps(c, "gdn_qkv_act", [f"{w}{q}" for q in range(2) for w in ("padded", "silu")])
            V = steps(c, "gdn_qkv_dve", [f"conv{q}{w}" for q in range(2) for w in taps])
            with nc.Block() as block:
                @block.vector
                def _(dve):
                    nc.vector.memset(padded[:, :, :, 0:3], 0.0)

            def act_evac(act, i, q):
                act.wait_ge(*V.at(f"conv{q}3", i - 1))
                nc.scalar.activation(padded[:, q, :, 3:], group_pair(c, q), ACT.Copy).then_inc(*A.done(f"padded{q}"))
                act.wait_ge(*V.at(f"conv{q}3", i))
                nc.scalar.activation(qkv[:, ds(i * 4 + 2 * q, 2), :], conv[:, q, :, :], ACT.Silu)\
                    .then_inc(*A.done(f"silu{q}"))

            def dve_evac(dve, i, q):
                dve.wait_ge(*A.at(f"silu{q}", i - 1))
                dve.wait_ge(*A.at(f"padded{q}", i))
                for w in taps:
                    if w:
                        dve.wait_ge(*V.at(f"conv{q}{w - 1}", i))
                    for m in range(2):
                        col = i * 4 + (2 * q + m)
                        at = VCOL[f"gdn_conv.0.{w}"] + col
                        scalar = c.vec[:, ds(at, 1)]
                        src, dst = padded[:, q, m, w:w + T], conv[:, q, m, :]
                        if w == 0:
                            last = nc.vector.tensor_scalar(dst, src, scalar, None, ALU.mult)
                        else:
                            last = nc.vector.scalar_tensor_tensor(dst, src, scalar, dst, ALU.mult, ALU.add)
                    last.then_inc(*V.done(f"conv{q}{w}"))

            dense(c, 6, simple(2), lambda q, k: (xh[:, k, :], xl[:, k, :]), act_evac, dve_evac, A, V,
                  [(A, "padded0"), (A, "padded1")])
        A = steps(c, "gdn_gate_act", ["gate0", "gate1"])

        def gate_evac(act, i, q):
            nc.scalar.activation(gate[:, ds(i * 4 + 2 * q, 2), :], group_pair(c, q), ACT.Silu)\
                .then_inc(*A.done(f"gate{q}"))
        dense(c, 2, simple(2), lambda q, k: (xh[:, k, :], xl[:, k, :]), gate_evac, lambda dve, i, q: None, A, None,
              [(A, "gate0"), (A, "gate1")])
        gdn_core(c, qkv, gate, G8, beta8, xh, xl)
        residual(c, "gdn_out", 2, simple(2), lambda q, k: (xh[:, k, :], xl[:, k, :]))


def doubling(n):
    size = 2
    while size < n:
        yield size
        size *= 2


def gdn_core(c, qkv, gate, G8, beta8, oh, ol):
    nc, ps, io = c.nc, c.ps, c.io
    NC = T // P
    levels = list(doubling(P))
    NL = len(levels)
    with scope(c) as sb:
        mask = sb("gdn_mask", [P, 2 + NL, P])
        gcol = sb("gdn_gcol", [P, NC, HEADS])
        b = {n: sb(f"gdn_{n}", [P, T]) for n in "kn qn grow D kb eg ekd vb kd AT X sq".split()}
        b["attT"], b["XT"], b["Y"] = b["ekd"], b["D"], b["kb"]
        blocks = sb("gdn_blocks", [P, 2, T])
        b["CTa"], b["CTb"] = blocks[:, 0, :], blocks[:, 1, :]
        sel = (sb("gdn_sel", [HEADS, T])[:, :], b["CTb"][0:HEADS, :])
        squares = (b["X"][:, :], b["AT"][:, :])
        state = sb("gdn_state", [P, P])
        R = sb("gdn_R", [P, P])
        VN = sb("gdn_VN", [P, P])
        rs = sb("gdn_rs", [P, 2, T])
        rso = rs[:, 0, :]

        def ch(buf, n):
            return buf[:, n * P:(n + 1) * P]

        def wide(buf, n0=0, n=NC):
            return buf[:, n0 * P:(n0 + n) * P].rearrange("p (n t) -> p n t", n=n)

        def over(m, n=NC):
            return m[:, None, :].to_broadcast([P, n, P])

        half = NC // 2
        En, An, Vn = (steps(c, f"gdn_next_{e}", n) for e, n in (("pe", ["rows", "norms"]), ("act", ["qsq", "ksq"]),
                                                               ("dve", ["gsel", "bsel"])))
        E = steps(c, "gdn_core_pe", ["kk", "qk", "turn_v", "turn_kd", "turn_X"]
                  + [f"{w}{l}{a}" for l in range(NL) for w in ("Y", "Z") for a in range(2)]
                  + [f"{w}{n}" for n in range(NC) for w in ("kS", "vn", "dS", "o")] + ["osum"])
        A = steps(c, "gdn_core_act", ["grow", "log", "rs", "eg", "ekd", "D", "vbt", "kdt", "X"]
                  + [f"Y{l}{a}" for l in range(NL) for a in range(2)]
                  + [f"vn{n}" for n in range(NC)] + ["osq", "olog", "ors", "hi"])
        V = steps(c, "gdn_core_dve", ["state", "nd", "diff", "masked", "qn", "kn", "vb", "kb", "kg",
                                      "qd", "kd", "AT", "attT", "off", "XT"]
                  + [f"{w}{l}{a}" for l in range(NL) for a in range(2)
                     for w in (("X", "XT") if l < NL - 1 else ("XT",))]
                  + [w for n in range(NC) for w in (f"R{n}", f"S{n}")] + ["on", "og", "lo"])
        Q = steps(c, "gdn_core_pool", [f"CT{l}" for l in range(NL)])
        pre = steps(c, "gdn_gcol_pe", ["turn"])
        loaded = c.scopes[-1].enter_context(nc.semaphore("gdn_mask_loaded"))
        with nc.Block() as block:
            @block.sync
            def _(sp):
                sp.dma_start(mask[:, :, :], io["gdn_masks"]).then_inc(loaded, 16)
                sp.wait_ge(loaded, 16)

            @block.tensor
            def _(pe):
                pre.start(pe)
                for n in range(NC):
                    last = nc.tensor.transpose(ps[:, 4, n * HEADS:(n + 1) * HEADS], ch(G8, n),
                                               c.ident[0:HEADS, 0:HEADS])
                last.then_inc(*pre.done("turn"))

            @block.vector
            def _(dve):
                dve.wait_ge(*pre.at("turn"))
                nc.vector.tensor_copy(gcol[:, :, :].rearrange("p n h -> p (n h)"), ps[:, 4, 0:NC * HEADS])

        with nc.Block() as block:
            @block.vector
            def _(dve):
                def select(i, n):
                    at = slice(i, i + 1) if isinstance(i, int) else ds(i, 1)
                    if n == 0:
                        dve.wait_ge(*En.at("rows", i - 1))
                    nc.vector.tensor_tensor(sel[n], (G8, beta8)[n][:, :],
                                            c.ident[0:HEADS, at].to_broadcast([HEADS, T]), ALU.mult)\
                        .then_inc(*Vn.done(("gsel", "bsel")[n]))

                V.start(dve)
                Vn.start(dve)
                select(0, 0)
                select(0, 1)
                with dve.Fori(0, HEADS) as i:
                    dve.wait_ge(*V.at(f"S{NC - 1}", i - 1))
                    nc.vector.memset(state[:, :], 0.0).then_inc(*V.done("state"))
                    dve.wait_ge(*A.at("grow", i))
                    grow = wide(b["grow"])
                    nc.vector.tensor_tensor(wide(b["ekd"]), grow[:, :, P - 1:P].to_broadcast([P, NC, P]), grow,
                                            ALU.subtract).then_inc(*V.done("nd"))
                    nc.vector.tensor_tensor(wide(b["D"]), grow, gcol[:, :, ds(i, 1)].to_broadcast([P, NC, P]),
                                            ALU.subtract).then_inc(*V.done("diff"))
                    dve.wait_ge(*V.at("diff", i))
                    nc.vector.tensor_tensor(wide(b["D"]), wide(b["D"]), over(mask[:, 0, :]), ALU.add)\
                        .then_inc(*V.done("masked"))
                    dve.wait_ge(*A.at("rs", i))
                    nc.vector.scalar_tensor_tensor(b["qn"][:, :], qkv[:, ds(i, 1), :].rearrange("p a t -> p (a t)"),
                                                   SCALE, rs[:, 0, :], ALU.mult, ALU.mult).then_inc(*V.done("qn"))
                    nc.vector.tensor_tensor(b["kn"][:, :], qkv[:, ds(i + HEADS, 1), :].rearrange("p a t -> p (a t)"),
                                            rs[:, 1, :], ALU.mult).then_inc(*V.done("kn"))
                    dve.wait_ge(*A.at("eg", i))
                    nc.vector.tensor_tensor(b["vb"][:, :],
                                            qkv[:, ds(i + 2 * HEADS, 1), :].rearrange("p a t -> p (a t)"),
                                            ps[:, 1, :], ALU.mult).then_inc(*V.done("vb"))
                    dve.wait_ge(*V.at("kn", i))
                    nc.vector.tensor_tensor(b["kb"][:, :], b["kn"][:, :], ps[:, 1, :], ALU.mult)\
                        .then_inc(*V.done("kb"))
                    dve.wait_ge(*A.at("ekd", i))
                    dve.wait_ge(*V.at("kb", i))
                    nc.vector.tensor_tensor(b["sq"][:, :], b["kb"][:, :], b["eg"][:, :], ALU.mult)\
                        .then_inc(*V.done("kg"))
                    nc.vector.tensor_tensor(b["grow"][:, :], b["qn"][:, :], b["eg"][:, :], ALU.mult)\
                        .then_inc(*V.done("qd"))
                    nc.vector.tensor_tensor(b["kd"][:, :], b["kn"][:, :], b["ekd"][:, :], ALU.mult)\
                        .then_inc(*V.done("kd"))
                    dve.wait_ge(*A.at("D", i))
                    dve.wait_ge(*E.at("kk", i))
                    nc.vector.tensor_tensor(b["AT"][:, :], ps[:, 4, :], b["D"][:, :], ALU.mult)\
                        .then_inc(*V.done("AT"))
                    dve.wait_ge(*E.at("qk", i))
                    dve.wait_ge(*V.at("kd", i))
                    nc.vector.tensor_tensor(b["attT"][:, :], ps[:, 5, :], b["D"][:, :], ALU.mult)\
                        .then_inc(*V.done("attT"))
                    dve.wait_ge(*V.at("attT", i))
                    nc.vector.tensor_tensor(wide(b["XT"]), wide(b["AT"]), over(mask[:, 1, :]), ALU.mult)\
                        .then_inc(*V.done("off"))
                    dve.wait_ge(*V.at("off", i))
                    nc.vector.tensor_tensor(wide(b["XT"]), over(c.ident[:, :]), wide(b["XT"]), ALU.subtract)\
                        .then_inc(*V.done("XT"))
                    for l in range(NL):
                        for a in range(2):
                            s = slice(a * half * P, (a + 1) * half * P)
                            dve.wait_ge(*E.at(f"Z{l}{a}", i))
                            if l < NL - 1:
                                nc.vector.tensor_tensor(b["X"][:, s], b["X"][:, s], ps[:, 4 + a, 0:half * P],
                                                        ALU.subtract).then_inc(*V.done(f"X{l}{a}"))
                            nc.vector.tensor_tensor(b["XT"][:, s], b["XT"][:, s], ps[:, 4 + a, half * P:],
                                                    ALU.subtract).then_inc(*V.done(f"XT{l}{a}"))
                    for n in range(NC):
                        dve.wait_ge(*E.at(f"kS{n}", i))
                        nc.vector.tensor_tensor(R[:, :], ch(b["vb"], n), ps[:, 4, 0:P], ALU.subtract)\
                            .then_inc(*V.done(f"R{n}"))
                        dve.wait_ge(*E.at(f"dS{n}", i))
                        nc.vector.scalar_tensor_tensor(state[:, :], state[:, :],
                                                       b["eg"][:, (n + 1) * P - 1:(n + 1) * P],
                                                       ps[:, 6, 0:P], ALU.mult, ALU.add).then_inc(*V.done(f"S{n}"))
                        if n < 2:
                            select(i + 1, n)
                    dve.wait_ge(*A.at("ors", i))
                    nc.vector.scalar_tensor_tensor(b["CTa"][:, :], ps[:, 7, :], vcol(c, "gdn_norm.0"), rso,
                                                   ALU.mult, ALU.mult).then_inc(*V.done("on"))
                    dve.wait_ge(*V.at("on", i))
                    nc.vector.tensor_tensor(b["CTa"][:, :], b["CTa"][:, :],
                                            gate[:, ds(i, 1), :].rearrange("p a t -> p (a t)"), ALU.mult)\
                        .then_inc(*V.done("og"))
                    dve.wait_ge(*A.at("hi", i))
                    nc.vector.tensor_tensor(ol[:, ds(i, 1), :].rearrange("p a t -> p (a t)"), b["CTa"][:, :],
                                            oh[:, ds(i, 1), :].rearrange("p a t -> p (a t)").bitcast(F32),
                                            ALU.subtract).then_inc(*V.done("lo"))

            @block.scalar
            def _(act):
                def square(i, n):
                    at = i + n * HEADS
                    src = qkv[:, at, :] if isinstance(at, int) else qkv[:, ds(at, 1), :].rearrange("p a t -> p (a t)")
                    if n == 0:
                        act.wait_ge(*En.at("norms", i - 1))
                    nc.scalar.activation(squares[n], src, ACT.Square).then_inc(*An.done(("qsq", "ksq")[n]))

                A.start(act)
                An.start(act)
                nc.scalar.preload_act_table_set(LOG_EXP)
                square(0, 0)
                square(0, 1)
                with act.Fori(0, HEADS) as i:
                    act.wait_ge(*En.at("norms", i))
                    act.wait_ge(*E.at(f"o{NC - 1}", i - 1))
                    nc.scalar.activation(b["grow"][:, :], ps[:, 0, :], ACT.Copy).then_inc(*A.done("grow"))
                    nc.scalar.activation(rs[:, :, :], ps[:, 2:4, :], ACT.Ln, bias=c.eps[:, :])\
                        .then_inc(*A.done("log"))
                    act.wait_ge(*A.at("log", i))
                    nc.scalar.activation(rs[:, :, :], rs[:, :, :], ACT.Exp, scale=-0.5).then_inc(*A.done("rs"))
                    act.wait_ge(*V.at(f"S{NC - 1}", i - 1))
                    nc.scalar.activation(b["eg"][:, :], ps[:, 0, :], ACT.Exp).then_inc(*A.done("eg"))
                    act.wait_ge(*V.at("nd", i))
                    nc.scalar.activation(b["ekd"][:, :], b["ekd"][:, :], ACT.Exp).then_inc(*A.done("ekd"))
                    act.wait_ge(*V.at("masked", i))
                    nc.scalar.activation(b["D"][:, :], b["D"][:, :], ACT.Exp).then_inc(*A.done("D"))
                    act.wait_ge(*E.at("turn_v", i))
                    nc.scalar.activation(b["vb"][:, :], ps[:, 6, :], ACT.Copy).then_inc(*A.done("vbt"))
                    act.wait_ge(*E.at("turn_kd", i))
                    nc.scalar.activation(b["kd"][:, :], ps[:, 7, :], ACT.Copy).then_inc(*A.done("kdt"))
                    act.wait_ge(*E.at("turn_X", i))
                    nc.scalar.activation(b["X"][:, :], ps[:, 6, :], ACT.Copy).then_inc(*A.done("X"))
                    for l in range(NL):
                        for a in range(2):
                            act.wait_ge(*E.at(f"Y{l}{a}", i))
                            nc.scalar.activation(b["Y"][:, a * half * P:(a + 1) * half * P],
                                                 ps[:, 6 + a, 0:half * P], ACT.Copy).then_inc(*A.done(f"Y{l}{a}"))
                    for n in range(NC):
                        act.wait_ge(*E.at(f"vn{n}", i))
                        nc.scalar.activation(VN[:, :], ps[:, 5, 0:P], ACT.Copy).then_inc(*A.done(f"vn{n}"))
                        if n < 2:
                            square(i + 1, n)
                    act.wait_ge(*E.at(f"o{NC - 1}", i))
                    nc.scalar.activation(b["Y"][:, :], ps[:, 7, :], ACT.Square).then_inc(*A.done("osq"))
                    act.wait_ge(*E.at("osum", i))
                    nc.scalar.activation(rso, ps[:, 5, :], ACT.Ln, bias=c.eps[:, :], scale=1.0 / P)\
                        .then_inc(*A.done("olog"))
                    act.wait_ge(*A.at("olog", i))
                    nc.scalar.activation(rso, rso, ACT.Exp, scale=-0.5).then_inc(*A.done("ors"))
                    act.wait_ge(*V.at("og", i))
                    nc.scalar.activation(oh[:, ds(i, 1), :].rearrange("p a t -> p (a t)"), b["CTa"][:, :], ACT.Copy)\
                        .then_inc(*A.done("hi"))

            @block.gpsimd
            def _(pool):
                Q.start(pool)
                with pool.Fori(0, HEADS) as i:
                    for l in range(NL):
                        ct = b["CTa"] if l % 2 == 0 else b["CTb"]
                        if l == 0:
                            pool.wait_ge(*V.at("lo", i - 1))
                            pool.wait_ge(*V.at("AT", i))
                        if l >= 2:
                            pool.wait_ge(*E.at(f"Y{l - 2}1", i))
                        elif l == 1:
                            pool.wait_ge(*E.at(f"Y{NL - 1 - (NL - 1 + 1) % 2}1", i - 1))
                        nc.gpsimd.tensor_tensor(wide(ct), wide(b["AT"]), over(mask[:, 2 + l, :]), ALU.mult)\
                            .then_inc(*Q.done(f"CT{l}"))

            @block.tensor
            def _(pe):
                def rows(i):
                    pe.wait_ge(*Vn.at("bsel", i))
                    pe.wait_ge(*V.at("kb", i - 1))
                    nc.tensor.matmul(ps[:, 0, :], c.ones[0:HEADS, :], sel[0], start=True, stop=True)
                    nc.tensor.matmul(ps[:, 1, :], c.ones[0:HEADS, :], sel[1], start=True, stop=True)\
                        .then_inc(*En.done("rows"))

                def norms(i):
                    pe.wait_ge(*An.at("ksq", i))
                    pe.wait_ge(*A.at("log", i - 1))
                    nc.tensor.matmul(ps[:, 2, :], c.ones[:, :], squares[0], start=True, stop=True)
                    nc.tensor.matmul(ps[:, 3, :], c.ones[:, :], squares[1], start=True, stop=True)\
                        .then_inc(*En.done("norms"))

                E.start(pe)
                En.start(pe)
                rows(0)
                norms(0)
                with pe.Fori(0, HEADS) as i:
                    pe.wait_ge(*V.at("kb", i))
                    pe.wait_ge(*V.at("lo", i - 1))
                    for n in range(NC):
                        last = nc.tensor.matmul(ch(ps[:, 4, :], n), ch(b["kn"], n), ch(b["kb"], n), start=True, stop=True)
                    last.then_inc(*E.done("kk"))
                    for n in range(NC):
                        last = nc.tensor.matmul(ch(ps[:, 5, :], n), ch(b["kn"], n), ch(b["qn"], n), start=True, stop=True)
                    last.then_inc(*E.done("qk"))
                    for n in range(NC):
                        last = nc.tensor.transpose(ch(ps[:, 6, :], n), ch(b["vb"], n), c.ident[:, :])
                    last.then_inc(*E.done("turn_v"))
                    pe.wait_ge(*V.at("kd", i))
                    for n in range(NC):
                        last = nc.tensor.transpose(ch(ps[:, 7, :], n), ch(b["kd"], n), c.ident[:, :])
                    last.then_inc(*E.done("turn_kd"))
                    pe.wait_ge(*V.at("XT", i))
                    pe.wait_ge(*A.at("vbt", i))
                    for n in range(NC):
                        last = nc.tensor.transpose(ch(ps[:, 6, :], n), ch(b["XT"], n), c.ident[:, :])
                    last.then_inc(*E.done("turn_X"))
                    pe.wait_ge(*A.at("X", i))
                    for l in range(NL):
                        ct = b["CTa"] if l % 2 == 0 else b["CTb"]
                        pe.wait_ge(*Q.at(f"CT{l}", i))
                        for a in range(2):
                            if l:
                                pe.wait_ge(*V.at(f"X{l - 1}{a}", i))
                            for m in range(half):
                                n = a * half + m
                                last = nc.tensor.matmul(ch(ps[:, 6 + a, :], m), ch(ct, n), ch(b["X"], n),
                                                        start=True, stop=True)
                            last.then_inc(*E.done(f"Y{l}{a}"))
                        for a in range(2):
                            pe.wait_ge(*A.at(f"Y{l}{a}", i))
                            if l:
                                pe.wait_ge(*V.at(f"XT{l - 1}{a}", i))
                            for m in range(half):
                                n = a * half + m
                                if l < NL - 1:
                                    nc.tensor.matmul(ch(ps[:, 4 + a, :], m), ch(b["XT"], n), ch(b["Y"], n),
                                                     start=True, stop=True)
                                last = nc.tensor.matmul(ch(ps[:, 4 + a, :], half + m), ch(b["Y"], n), ch(b["XT"], n),
                                                        start=True, stop=True)
                            last.then_inc(*E.done(f"Z{l}{a}"))
                    for n in range(NC):
                        if n:
                            pe.wait_ge(*V.at(f"S{n - 1}", i))
                        else:
                            pe.wait_ge(*V.at(f"XT{NL - 1}1", i))
                        nc.tensor.matmul(ps[:, 4, 0:P], ch(b["sq"], n), state[:, :], start=True, stop=True)\
                            .then_inc(*E.done(f"kS{n}"))
                        nc.tensor.matmul(ch(ps[:, 7, :], n), state[:, :], ch(b["grow"], n), start=True, stop=False)
                        pe.wait_ge(*V.at(f"R{n}", i))
                        nc.tensor.matmul(ps[:, 5, 0:P], ch(b["XT"], n), R[:, :], start=True, stop=True)\
                            .then_inc(*E.done(f"vn{n}"))
                        pe.wait_ge(*A.at(f"vn{n}", i))
                        nc.tensor.matmul(ps[:, 6, 0:P], ch(b["kd"], n), VN[:, :], start=True, stop=True)\
                            .then_inc(*E.done(f"dS{n}"))
                        nc.tensor.matmul(ch(ps[:, 7, :], n), VN[:, :], ch(b["attT"], n), start=False, stop=True)\
                            .then_inc(*E.done(f"o{n}"))
                    rows(i + 1)
                    pe.wait_ge(*A.at("osq", i))
                    nc.tensor.matmul(ps[:, 5, :], c.ones[:, :], b["Y"][:, :], start=True, stop=True)\
                        .then_inc(*E.done("osum"))
                    norms(i + 1)


def per_layer_embedding(c, i_layer):
    nc, ps = c.nc, c.ps
    name = f"ple{i_layer}"
    with scope(c) as sb:
        xh, xl = sb(f"{name}_xh", [P, KD, T], F32R), sb(f"{name}_xl", [P, KD, T], F32R)
        ph, pl = sb(f"{name}_ph", [P, 2, T], F32R), sb(f"{name}_pl", [P, 2, T], F32R)
        praw = sb(f"{name}_p", [P, 2, T])
        sig, prod = sb(f"{name}_sig", [P, 2, T]), sb(f"{name}_prod", [P, 2, T])
        loaded = c.scopes[-1].enter_context(nc.semaphore(f"{name}_p_loaded"))
        S = steps(c, f"{name}_split_act", ["hi"])
        with nc.Block() as block:
            @block.gpsimd
            def _(pool):
                pool.dma_start(praw[:, :, :], c.io["p"][i_layer]).then_inc(loaded, 16)

            @block.scalar
            def _(act):
                S.start(act)
                act.wait_ge(loaded, 16)
                nc.scalar.activation(ph[:, :, :], praw[:, :, :], ACT.Copy).then_inc(*S.done("hi"))

            @block.vector
            def _(dve):
                dve.wait_ge(*S.at("hi"))
                nc.vector.tensor_tensor(pl[:, :, :], praw[:, :, :], ph[:, :, :].bitcast(F32), ALU.subtract)
        norm(c, f"{name}_n", [f"ln_ple.{i_layer}"], [(xh, xl)])
        A = steps(c, f"{name}_act", ["sigmoid"])
        V = steps(c, f"{name}_dve", ["prod", "h"])

        def act_evac(act, i, q):
            if q == 1:
                act.wait_ge(*V.at("prod", i - 1))
                nc.scalar.activation(sig[:, :, :], ps[:, 2:4, :], ACT.Sigmoid).then_inc(*A.done("sigmoid"))

        def dve_evac(dve, i, q):
            if q == 1:
                dve.wait_ge(*A.at("sigmoid", i))
                dve.wait_ge(*V.at("h", i - 1))
                nc.vector.tensor_tensor(prod[:, :, :], ps[:, 0:2, :], sig[:, :, :], ALU.mult).then_inc(*V.done("prod"))
                dve.wait_ge(*V.at("prod", i))
                nc.vector.tensor_tensor(c.h[:, ds(i * 2, 2), :], c.h[:, ds(i * 2, 2), :], prod[:, :, :], ALU.add)\
                    .then_inc(*V.done("h"))

        body = [[(0, True, True, [(0, 0), (1, 1)])], [(1, True, True, [(k, k) for k in range(KD)])]]
        dense(c, DM // WN, body, lambda q, k: (ph[:, k, :], pl[:, k, :]) if q == 0 else (xh[:, k, :], xl[:, k, :]),
              act_evac, dve_evac, A, V, [(V, "prod"), (A, "sigmoid")])


def project(c, name, iters, xs, dst, tokens_out=False, func=ACT.Copy):
    A = steps(c, f"{name}_act", ["copy0", "copy1"])

    def evac(act, i, q):
        if tokens_out:
            to = dst[:, :, ds(i * 2 * WN + q * WN, WN)]
            pair = group_pair(c, q).rearrange("p b (a n) -> p (b a) n", n=WN)
        else:
            to, pair = dst[:, ds(i * 4 + 2 * q, 2), :], group_pair(c, q)
        c.nc.scalar.activation(to, pair, func).then_inc(*A.done(f"copy{q}"))

    dense(c, iters, simple(2), lambda q, k: (xs[0][:, k, :], xs[1][:, k, :]), evac, lambda dve, i, q: None, A, None,
          [(A, "copy0"), (A, "copy1")], tokens_out)


def stick_breaking(c):
    nc = c.nc
    with scope(c) as sb:
        oh, ol = sb("sb_oh", [P, KD, T], F32R), sb("sb_ol", [P, KD, T], F32R)
        k = sb("sb_k", [P, HEADS, T])
        v = sb("sb_v", [P, T // P, DM])
        with scope(c) as sb2:
            qh, ql = sb2("sb_qh", [P, KD, T], F32R), sb2("sb_ql", [P, KD, T], F32R)
            norm(c, "sb_n", ["kv_norm", "ln_mix.1"], [(oh, ol), (qh, ql)])
            project(c, "sb_k", 2, (oh, ol), k)
            project(c, "sb_v", 2, (oh, ol), v, tokens_out=True)
            q = ol[:, :, :].bitcast(F32)
            project(c, "sb_q", 2, (qh, ql), q)
        stick_core(c, k, v, q, oh, ol)
        residual(c, "sb_out", 2, simple(2), lambda q_, k_: (oh[:, k_, :], ol[:, k_, :]))


def stick_norms(c, k, q):
    nc, ps = c.nc, c.ps
    with scope(c) as sb:
        qg = sb("sb_qg", [P, 1])
        sq, rs = sb("sb_sq", [P, 4, T]), sb("sb_rs", [P, 4, T])
        A = steps(c, "sb_norm_act", [f"{w}{n}" for w in ("sq", "log", "rs") for n in range(2)])
        V = steps(c, "sb_norm_dve", ["q0", "k0", "q1", "k1"])
        E = steps(c, "sb_norm_pe", ["sum0", "sum1"])

        def heads(buf, i):
            return buf[:, ds(i, 1), :].rearrange("p a t -> p (a t)")

        with nc.Block() as block:
            @block.vector
            def _(dve):
                nc.vector.tensor_scalar(qg[:, :], vcol(c, "sb_q_norm.0"), SCALE, None, ALU.mult)

        with nc.Block() as block:
            @block.scalar
            def _(act):
                A.start(act)
                nc.scalar.preload_act_table_set(LOG_EXP)
                with act.Fori(0, HEADS // 2) as i:
                    for n in range(2):
                        act.wait_ge(*E.at(f"sum{n}", i - 1))
                        nc.scalar.activation(sq[:, 2 * n, :], heads(q, 2 * i + n), ACT.Square)
                        nc.scalar.activation(sq[:, 2 * n + 1, :], heads(k, 2 * i + n), ACT.Square)\
                            .then_inc(*A.done(f"sq{n}"))
                    for n in range(2):
                        two = slice(2 * n, 2 * n + 2)
                        act.wait_ge(*E.at(f"sum{n}", i))
                        act.wait_ge(*V.at(f"k{n}", i - 1))
                        nc.scalar.activation(rs[:, two, :], ps[:, two, :], ACT.Ln, bias=c.eps[:, :], scale=1.0 / P)\
                            .then_inc(*A.done(f"log{n}"))
                    for n in range(2):
                        two = slice(2 * n, 2 * n + 2)
                        act.wait_ge(*A.at(f"log{n}", i))
                        nc.scalar.activation(rs[:, two, :], rs[:, two, :], ACT.Exp, scale=-0.5)\
                            .then_inc(*A.done(f"rs{n}"))

            @block.tensor
            def _(pe):
                E.start(pe)
                with pe.Fori(0, HEADS // 2) as i:
                    for n in range(2):
                        pe.wait_ge(*A.at(f"sq{n}", i))
                        pe.wait_ge(*A.at(f"log{n}", i - 1))
                        for m in range(2):
                            last = nc.tensor.matmul(ps[:, 2 * n + m, :], c.ones[:, :], sq[:, 2 * n + m, :],
                                                    start=True, stop=True)
                        last.then_inc(*E.done(f"sum{n}"))

            @block.vector
            def _(dve):
                V.start(dve)
                with dve.Fori(0, HEADS // 2) as i:
                    for n in range(2):
                        dve.wait_ge(*A.at(f"rs{n}", i))
                        for w, x, gain, m in (("q", q, qg[:, :], 0), ("k", k, vcol(c, "k_norm"), 1)):
                            at = heads(x, 2 * i + n)
                            nc.vector.scalar_tensor_tensor(at, at, gain, rs[:, 2 * n + m, :], ALU.mult, ALU.mult)\
                                .then_inc(*V.done(f"{w}{n}"))


def stick_core(c, k, v, q, oh, ol):
    nc, ps = c.nc, c.ps
    N = T // P
    off = {0: 512, 2: 896, 1: 1024}
    width = 1280
    z = ps[:, 4:7, :].rearrange("p b t -> p (b t)")
    tail = ps[:, 0:3, :].rearrange("p b t -> p (b t)")
    stick_norms(c, k, q)
    with scope(c) as sb:
        mats = sb("sb_mats", [P, 3, P])
        kn, qn = sb("sb_kn", [P, T]), sb("sb_qn", [P, T])
        vt = sb("sb_vt", [P, N, P])
        la, sp, ls, w = (sb(f"sb_{n}", [P, width]) for n in ("la", "sp", "ls", "w"))
        loaded = c.scopes[-1].enter_context(nc.semaphore("sb_mats_loaded"))
        Ez, Et, Eo = steps(c, "sb_z_pe", ["z"]), steps(c, "sb_tail_pe", ["tail"]), steps(c, "sb_o_pe", ["o"])
        As, Aw, Ah = steps(c, "sb_soft_act", ["abs", "exp", "soft"]), steps(c, "sb_w_act", ["w"]), steps(c, "sb_hi_act", ["hi"])
        Vs, Vw, Vl = steps(c, "sb_sp_dve", ["sp", "ls", "spm"]), steps(c, "sb_w_dve", ["lw", "wm"]), steps(c, "sb_lo_dve", ["lo"])
        Qk, Qv = steps(c, "sb_k_pool", ["k"]), steps(c, "sb_v_pool", ["v"])
        with nc.Block() as block:
            @block.gpsimd
            def _(pool):
                pool.dma_start(mats[:, :, :], c.io["sb_mats"]).then_inc(loaded, 16)
                pool.wait_ge(loaded, 16)

        def head(buf, i):
            if isinstance(i, int):
                return buf[:, i, :]
            return buf[:, ds(i, 1), :].rearrange("p a t -> p (a t)")

        def diagonal(buf):
            return buf[:, 0:N * P].rearrange("p (n t) -> p n t", n=N)

        def over(m):
            return m[:, None, :].to_broadcast([P, N, P])

        with nc.Block() as block:
            @block.gpsimd
            def _(pool):
                def keys(i):
                    pool.wait_ge(*Ez.at("z", i - 1))
                    nc.gpsimd.tensor_copy(kn[:, :], head(k, i))
                    nc.gpsimd.tensor_copy(qn[:, :], head(q, i)).then_inc(*Qk.done("k"))

                def values(i):
                    pool.wait_ge(*Eo.at("o", i - 1))
                    columns = slice(i * P, (i + 1) * P) if isinstance(i, int) else ds(i * P, P)
                    nc.gpsimd.tensor_copy(vt[:, :, :], v[:, :, columns]).then_inc(*Qv.done("v"))

                for group in (Qk, Qv):
                    group.start(pool)
                keys(0)
                with pool.Fori(0, HEADS - 1) as i:
                    values(i)
                    keys(i + 1)
                values(HEADS - 1)

            @block.scalar
            def _(act):
                def soft(i):
                    act.wait_ge(*Ez.at("z", i))
                    act.wait_ge(*Vs.at("ls", i - 1))
                    nc.scalar.activation(la[:, :], z[:, 0:width], ACT.Abs).then_inc(*As.done("abs"))
                    act.wait_ge(*As.at("abs", i))
                    nc.scalar.activation(la[:, :], la[:, :], ACT.Exp, scale=-1.0).then_inc(*As.done("exp"))
                    act.wait_ge(*As.at("exp", i))
                    nc.scalar.activation(la[:, :], la[:, :], ACT.Ln, bias=c.ones[:, 0:1]).then_inc(*As.done("soft"))

                def weights(i):
                    act.wait_ge(*Vw.at("lw", i))
                    nc.scalar.activation(w[:, :], w[:, :], ACT.Exp).then_inc(*Aw.done("w"))

                def high(i):
                    act.wait_ge(*Eo.at("o", i))
                    nc.scalar.activation(head(oh, i), ps[:, 3, :], ACT.Copy).then_inc(*Ah.done("hi"))

                for group in (As, Aw, Ah):
                    group.start(act)
                nc.scalar.preload_act_table_set(LOG_EXP)
                soft(0)
                with act.Fori(0, HEADS - 1) as i:
                    weights(i)
                    soft(i + 1)
                    high(i)
                weights(HEADS - 1)
                high(HEADS - 1)

            @block.vector
            def _(dve):
                def soft(i):
                    dve.wait_ge(*As.at("soft", i))
                    dve.wait_ge(*Et.at("tail", i - 1))
                    nc.vector.scalar_tensor_tensor(sp[:, :], z[:, 0:width], 0.0, la[:, :], ALU.max, ALU.add)\
                        .then_inc(*Vs.done("sp"))
                    dve.wait_ge(*Vw.at("lw", i - 1))
                    nc.vector.scalar_tensor_tensor(ls[:, :], z[:, 0:width], 0.0, la[:, :], ALU.min, ALU.subtract)\
                        .then_inc(*Vs.done("ls"))
                    dve.wait_ge(*Vs.at("sp", i))
                    nc.vector.tensor_tensor(diagonal(sp), diagonal(sp), over(mats[:, 0, :]), ALU.mult)\
                        .then_inc(*Vs.done("spm"))

                def weights(i):
                    dve.wait_ge(*Et.at("tail", i))
                    dve.wait_ge(*Vs.at("ls", i))
                    dve.wait_ge(*Eo.at("o", i - 1))
                    nc.vector.tensor_tensor(w[:, :], ls[:, :], tail[:, 0:width], ALU.add).then_inc(*Vw.done("lw"))
                    dve.wait_ge(*Aw.at("w", i))
                    nc.vector.tensor_tensor(diagonal(w), diagonal(w), over(mats[:, 0, :]), ALU.mult)\
                        .then_inc(*Vw.done("wm"))

                def low(i):
                    dve.wait_ge(*Ah.at("hi", i))
                    nc.vector.tensor_tensor(head(ol, i), ps[:, 3, :], head(oh, i).bitcast(F32), ALU.subtract)\
                        .then_inc(*Vl.done("lo"))

                for group in (Vs, Vw, Vl):
                    group.start(dve)
                soft(0)
                with dve.Fori(0, HEADS - 1) as i:
                    weights(i)
                    soft(i + 1)
                    low(i)
                weights(HEADS - 1)
                low(HEADS - 1)

            @block.tensor
            def _(pe):
                def scores(i):
                    pe.wait_ge(*Qk.at("k", i))
                    pe.wait_ge(*Vs.at("ls", i - 1))
                    for j in range(N):
                        last = nc.tensor.matmul(z[:, j * P:(j + 1) * P], kn[:, j * P:(j + 1) * P],
                                                qn[:, j * P:(j + 1) * P], start=True, stop=True)
                        if j < N - 1:
                            last = nc.tensor.matmul(z[:, off[j]:off[j] + T - (j + 1) * P], kn[:, j * P:(j + 1) * P],
                                                    qn[:, (j + 1) * P:], start=True, stop=True)
                    last.then_inc(*Ez.done("z"))

                def tails(i):
                    pe.wait_ge(*Vs.at("spm", i))
                    pe.wait_ge(*Vw.at("lw", i - 1))
                    for j in range(N):
                        last = nc.tensor.matmul(tail[:, j * P:(j + 1) * P], mats[:, 1, :], sp[:, j * P:(j + 1) * P],
                                                start=True, stop=True)
                        if j == N - 1:
                            continue
                        dst = tail[:, off[j]:off[j] + T - (j + 1) * P]
                        nc.tensor.matmul(dst, mats[:, 1, :], sp[:, off[j]:off[j] + T - (j + 1) * P],
                                         start=True, stop=False)
                        for jj in range(j + 1, N):
                            at = (jj - j - 1) * P
                            last = nc.tensor.matmul(dst[:, at:at + P], mats[:, 2, :], sp[:, jj * P:(jj + 1) * P],
                                                    start=False, stop=jj == N - 1)
                            if jj < N - 1:
                                nc.tensor.matmul(dst[:, at + P:], mats[:, 2, :],
                                                 sp[:, off[jj]:off[jj] + T - (jj + 1) * P], start=False, stop=False)
                    last.then_inc(*Et.done("tail"))

                def outputs(i):
                    pe.wait_ge(*Vw.at("wm", i))
                    pe.wait_ge(*Qv.at("v", i))
                    pe.wait_ge(*Vl.at("lo", i - 1))
                    for j in range(N):
                        if j < N - 1:
                            nc.tensor.matmul(ps[:, 3, (j + 1) * P:], vt[:, j, :], w[:, off[j]:off[j] + T - (j + 1) * P],
                                             start=j == 0, stop=False, skip_group_check=True)
                        last = nc.tensor.matmul(ps[:, 3, j * P:(j + 1) * P], vt[:, j, :], w[:, j * P:(j + 1) * P],
                                                start=False, stop=True, skip_group_check=True)
                    last.then_inc(*Eo.done("o"))

                for group in (Ez, Et, Eo):
                    group.start(pe)
                scores(0)
                with pe.Fori(0, HEADS - 1) as i:
                    tails(i)
                    scores(i + 1)
                    outputs(i)
                tails(HEADS - 1)
                outputs(HEADS - 1)


def three_taps(c, name, iters, x, dst, before, middle, after, bias=None):
    nc = c.nc
    with scope(c) as sb:
        padded = sb(f"{name}_padded", [P, 2, 2, T + 2])
        A = steps(c, f"{name}_act", ["padded0", "padded1"])
        V = steps(c, f"{name}_dve", [f"{w}{q}" for q in range(2) for w in ("mid", "before", "after")])
        with nc.Block() as block:
            @block.vector
            def _(dve):
                nc.vector.memset(padded[:, :, :, 0:1], 0.0)
                nc.vector.memset(padded[:, :, :, T + 1:], 0.0)

        def act_evac(act, i, q):
            act.wait_ge(*V.at(f"after{q}", i - 1))
            nc.scalar.activation(padded[:, q, :, 1:T + 1], group_pair(c, q), ACT.Copy).then_inc(*A.done(f"padded{q}"))

        def dve_evac(dve, i, q):
            dve.wait_ge(*A.at(f"padded{q}", i))
            for step, at, col in (("mid", 1, middle), ("before", 0, before), ("after", 2, after)):
                if step != "mid":
                    dve.wait_ge(*V.at(f"mid{q}" if step == "before" else f"before{q}", i))
                for m in range(2):
                    k = i * 4 + (2 * q + m)
                    to = dst[:, ds(k, 1), :].rearrange("p a t -> p (a t)")
                    src = padded[:, q, m, at:at + T]
                    if step == "mid":
                        last = nc.vector.tensor_scalar(to, src, col(k), bias(k) if bias else None, ALU.mult,
                                                       *([ALU.add] if bias else []))
                    else:
                        last = nc.vector.scalar_tensor_tensor(to, src, col(k), to, ALU.mult, ALU.add)
                last.then_inc(*V.done(f"{step}{q}"))

        dense(c, iters, simple(2), lambda q, k: (x[0][:, k, :], x[1][:, k, :]), act_evac, dve_evac, A, V,
              [(A, "padded0"), (A, "padded1")])


def vec_at(c, name):
    return lambda k: c.vec[:, ds(k + VCOL[name], 1)]


HY_EMB, HY_FFN = 33, 64
TWO_PI = 2 * np.pi
ROUND = 1.5 * 2 ** 23
PI_A = 6.28125
PI_B = float(np.float32(np.floor((TWO_PI - PI_A) * 2 ** 21) / 2 ** 21))
PI_C = float(np.float32(TWO_PI - PI_A - PI_B))


def hyena(c, u):
    nc, ps, io = c.nc, c.ps, c.io
    N = T // P
    with scope(c) as sb:
        h2 = sb("hy_h2", [HY_FFN + 1, T])
        with scope(c) as sb2:
            feats = sb2("hy_feats", [HY_EMB, T])
            w1, w2 = sb2("hy_w1", [HY_EMB, HY_FFN]), sb2("hy_w2", [HY_FFN, HY_FFN])
            cols = sb2("hy_cols", [HY_FFN, 3])
            arg, turns = sb2("hy_arg", [HY_FFN, T]), sb2("hy_turns", [HY_FFN, T])
            hid = sb2("hy_hid", [HY_FFN, T])
            loaded = c.scopes[-1].enter_context(nc.semaphore("hy_small_loaded"))
            E = steps(c, "hy_mlp_pe", ["product0", "product1"])
            V = steps(c, "hy_mlp_dve", [f"{w}{n}" for n in range(2)
                                        for w in ("arg", "scaled", "turns", "ra", "rb", "rc", "clamped")])
            A = steps(c, "hy_mlp_act", ["sin0", "sin1"])
            with nc.Block() as block:
                @block.sync
                def _(sp):
                    for dst, src in ((feats, "hy_feats"), (w1, "hy_w1"), (w2, "hy_w2"), (cols, "hy_cols")):
                        sp.dma_start(dst[:, :], io[src]).then_inc(loaded, 16)

                @block.tensor
                def _(pe):
                    E.start(pe)
                    pe.wait_ge(loaded, 64)
                    nc.tensor.matmul(ps[0:HY_FFN, 4, :], w1[:, :], feats[:, :], start=True, stop=True)\
                        .then_inc(*E.done("product0"))
                    pe.wait_ge(*A.at("sin0"))
                    nc.tensor.matmul(ps[0:HY_FFN, 5, :], w2[:, :], hid[:, :], start=True, stop=True)\
                        .then_inc(*E.done("product1"))

                @block.vector
                def _(dve):
                    V.start(dve)
                    nc.vector.memset(h2[HY_FFN:HY_FFN + 1, :], 1.0)
                    dve.wait_ge(loaded, 64)
                    for n in range(2):
                        dve.wait_ge(*E.at(f"product{n}"))
                        nc.vector.tensor_scalar(arg[:, :], ps[0:HY_FFN, 4 + n, :], cols[:, n:n + 1], cols[:, 2:3],
                                                ALU.add, ALU.mult).then_inc(*V.done(f"arg{n}"))
                        dve.wait_ge(*V.at(f"arg{n}"))
                        nc.vector.tensor_scalar(turns[:, :], arg[:, :], 1 / TWO_PI, ROUND, ALU.mult, ALU.add)\
                            .then_inc(*V.done(f"scaled{n}"))
                        dve.wait_ge(*V.at(f"scaled{n}"))
                        nc.vector.tensor_scalar(turns[:, :], turns[:, :], ROUND, None, ALU.subtract)\
                            .then_inc(*V.done(f"turns{n}"))
                        before = f"turns{n}"
                        for step, part in (("ra", PI_A), ("rb", PI_B), ("rc", PI_C)):
                            dve.wait_ge(*V.at(before))
                            nc.vector.scalar_tensor_tensor(arg[:, :], turns[:, :], -part, arg[:, :],
                                                           ALU.mult, ALU.add).then_inc(*V.done(f"{step}{n}"))
                            before = f"{step}{n}"
                        dve.wait_ge(*V.at(before))
                        nc.vector.tensor_scalar(arg[:, :], arg[:, :], 3.1415925, -3.1415925, ALU.min, ALU.max)\
                            .then_inc(*V.done(f"clamped{n}"))

                @block.scalar
                def _(act):
                    A.start(act)
                    for n, dst in ((0, hid[:, :]), (1, h2[0:HY_FFN, :])):
                        act.wait_ge(*V.at(f"clamped{n}"))
                        nc.scalar.activation(dst, arg[:, :], ACT.Sin).then_inc(*A.done(f"sin{n}"))

        trig = sb("hy_trig", [P, 4, N, T])
        kp, km = sb("hy_kp", [P, N, T]), sb("hy_km", [P, N, T])
        kre, kim = sb("hy_kre", [P, N, T]), sb("hy_kim", [P, N, T])
        zT = sb("hy_zT", [P, N, T])
        w3 = sb("hy_w3", [HY_FFN + 1, 4 * DR])
        decay = sb("hy_decay", [P, 4 * DR])
        tpos = sb("hy_tpos", [P, N + 1])
        side = [sb(f"hy_side{d}", [P, T]) for d in range(2)]
        sq = sb("hy_sq", [P, T])
        rsq = sb("hy_rsq", [P, T])
        part = [sb(f"hy_part{n}", [P, T]) for n in range(2)]
        damp, squares = part, (sq, rsq)
        yre, yim = kp, km
        loaded = c.scopes[-1].enter_context(nc.semaphore("hy_trig_loaded"))
        pe_steps = ["h300"]
        for n in range(1, 2 * N):
            pe_steps += [f"h3{n // 2}{n % 2}", f"sum{(n - 1) // 2}{(n - 1) % 2}"]
        E = steps(c, "hy_pe", pe_steps + [f"sum{N - 1}1"] + [f"turn{s}" for s in range(N)]
                  + [f"k{w}{j}" for j in range(N) for w in "ri"]
                  + [f"z{j}" for j in range(N)] + [f"y{m}" for m in range(N)])
        A = steps(c, "hy_act", [f"{w}{p}{d}" for p in range(N) for w in ("damp", "sq") for d in range(2)]
                  + ["log", "rsq"] + [f"zT{s}" for s in range(N)])
        V = steps(c, "hy_dve", [x for p in range(N) for x in (f"side{p}0", f"side{p}1", f"kp{p}", f"km{p}")]
                  + [f"k{w}{j}" for j in range(N) for w in "ri"]
                  + [f"{w}{j}" for j in range(N) for w in ("a", "b", "re", "c", "d", "im")]
                  + [f"{w}{m}" for m in range(N) for w in ("dz", "z")])
        with nc.Block() as block:
            @block.sync
            def _(sp):
                for n in range(4):
                    sp.dma_start(trig[:, n, :, :], io["hy_trig"][n]).then_inc(loaded, 16)
                sp.dma_start(w3[:, :], io["hy_w3"]).then_inc(loaded, 16)
                sp.dma_start(decay[:, :], io["hy_decay"].partition_broadcast(P)).then_inc(loaded, 16)
                sp.dma_start(tpos[:, :], io["hy_tpos"]).then_inc(loaded, 16)
                sp.wait_ge(loaded, 7 * 16)

            @block.scalar
            def _(act):
                act.wait_ge(loaded, 7 * 16)
                nc.scalar.activation(decay[:, :], decay[:, :], ACT.Abs)
        def tile_of(buf, k):
            return buf[:, ds(k, 1), :].rearrange("p a t -> p (a t)")

        with nc.Block() as block:
            @block.tensor
            def _(pe):
                E.start(pe)

                def total(i, p, d):
                    pe.wait_ge(*A.at(f"sq{p}{d}", i))
                    nc.tensor.matmul(ps[:, 2, :], c.ones[:, :], squares[d][:, :], start=p + d == 0, stop=p + d == N)\
                        .then_inc(*E.done(f"sum{p}{d}"))

                with pe.Fori(0, 2) as i:
                    done = None
                    for p in range(N):
                        for d in range(2):
                            if p:
                                pe.wait_ge(*V.at(f"side{p - 1}{d}", i))
                            else:
                                pe.wait_ge(*V.at(f"z{N - 1}", i - 1))
                            nc.tensor.matmul(ps[:, d, :], h2[:, p * P:(p + 1) * P],
                                             w3[:, ds(i * DR + 2 * d * DR, DR)], start=True, stop=True)\
                                .then_inc(*E.done(f"h3{p}{d}"))
                            if done:
                                total(i, *done)
                            done = (p, d)
                    total(i, *done)
                    for s in range(N):
                        if s >= 2:
                            pe.wait_ge(*A.at(f"zT{s - 2}", i))
                        for m in range(N):
                            last = nc.tensor.transpose(ps[:, 4 + s % 2, m * P:(m + 1) * P],
                                                       u[:, 2 * N + m, s * P:(s + 1) * P], c.ident[:, :])
                        last.then_inc(*E.done(f"turn{s}"))
                    pe.wait_ge(*V.at(f"km{N - 1}", i))
                    for j in range(N):
                        for n, (w, src) in enumerate((("r", kp), ("i", km))):
                            if j:
                                pe.wait_ge(*V.at(f"k{w}{j - 1}", i))
                            for s in range(N):
                                last = nc.tensor.matmul(ps[:, 6 + n, :], trig[:, n, s, j * P:(j + 1) * P],
                                                        src[:, s, :], start=s == 0, stop=s == N - 1)
                            last.then_inc(*E.done(f"k{w}{j}"))
                    pe.wait_ge(*A.at(f"zT{N - 1}", i))
                    for j in range(N):
                        bank = 2 * (j % 2)
                        if j >= 2:
                            pe.wait_ge(*V.at(f"d{j - 2}", i))
                        for n in range(2):
                            for s in range(N):
                                last = nc.tensor.matmul(ps[:, bank + n, :], trig[:, n, s, j * P:(j + 1) * P],
                                                        zT[:, s, :], start=s == 0, stop=s == N - 1)
                        last.then_inc(*E.done(f"z{j}"))
                    pe.wait_ge(*V.at(f"im{N - 1}", i))
                    for m in range(N):
                        if m >= 2:
                            pe.wait_ge(*V.at(f"dz{m - 2}", i))
                        for n, src in enumerate((yre, yim)):
                            for j in range(N):
                                last = nc.tensor.matmul(ps[:, 4 + m % 2, :], src[:, j, m * P:(m + 1) * P],
                                                        trig[:, 2 + n, j, :], start=n + j == 0, stop=n * (j + 1) == N)
                        last.then_inc(*E.done(f"y{m}"))

            @block.scalar
            def _(act):
                A.start(act)
                nc.scalar.preload_act_table_set(LOG_EXP)
                with act.Fori(0, 2) as i:
                    act.wait_ge(*V.at(f"z{N - 1}", i - 1))
                    for p in range(N):
                        for d in range(2):
                            nc.scalar.activation(damp[d][:, :], decay[:, ds(i * DR + 2 * d * DR, DR)], ACT.Exp,
                                                 scale=tpos[:, p:p + 1]).then_inc(*A.done(f"damp{p}{d}"))
                        for d in range(2):
                            act.wait_ge(*V.at(f"side{p}{d}", i))
                            if p:
                                act.wait_ge(*E.at(f"sum{p - 1}{d}", i))
                            nc.scalar.activation(squares[d][:, :], side[d][:, :], ACT.Square)\
                                .then_inc(*A.done(f"sq{p}{d}"))
                    act.wait_ge(*E.at(f"sum{N - 1}1", i))
                    nc.scalar.activation(rsq[:, :], ps[:, 2, :], ACT.Ln, bias=c.eps[:, :]).then_inc(*A.done("log"))
                    act.wait_ge(*A.at("log", i))
                    nc.scalar.activation(rsq[:, :], rsq[:, :], ACT.Exp, scale=-0.5).then_inc(*A.done("rsq"))
                    for s in range(N):
                        act.wait_ge(*E.at(f"turn{s}", i))
                        nc.scalar.activation(zT[:, s, :], ps[:, 4 + s % 2, :], ACT.Copy).then_inc(*A.done(f"zT{s}"))

            @block.vector
            def _(dve):
                V.start(dve)
                with dve.Fori(0, 2) as i:
                    for p in range(N):
                        for d in range(2):
                            dve.wait_ge(*A.at(f"damp{p}{d}", i))
                            dve.wait_ge(*E.at(f"h3{p}{d}", i))
                            if p:
                                dve.wait_ge(*A.at(f"sq{p - 1}{d}", i))
                                dve.wait_ge(*V.at(f"km{p - 1}", i))
                            keep = tpos[:, N:N + 1] if (p, d) == (0, 1) else 1.0
                            nc.vector.scalar_tensor_tensor(side[d][:, :], ps[:, d, :], keep, damp[d][:, :],
                                                           ALU.mult, ALU.mult).then_inc(*V.done(f"side{p}{d}"))
                        dve.wait_ge(*V.at(f"side{p}1", i))
                        nc.vector.tensor_tensor(kp[:, p, :], side[0][:, :], side[1][:, :], ALU.add)\
                            .then_inc(*V.done(f"kp{p}"))
                        nc.vector.tensor_tensor(km[:, p, :], side[1][:, :], side[0][:, :], ALU.subtract)\
                            .then_inc(*V.done(f"km{p}"))
                    dve.wait_ge(*A.at("rsq", i))
                    for j in range(N):
                        for n, (w, dst) in enumerate((("r", kre), ("i", kim))):
                            dve.wait_ge(*E.at(f"k{w}{j}", i))
                            nc.vector.scalar_tensor_tensor(dst[:, j, :], ps[:, 6 + n, :], 1 / T, rsq[:, :],
                                                           ALU.mult, ALU.mult).then_inc(*V.done(f"k{w}{j}"))
                    dve.wait_ge(*V.at(f"ki{N - 1}", i))
                    for j in range(N):
                        zc, zs = ps[:, 2 * (j % 2), :], ps[:, 2 * (j % 2) + 1, :]
                        dve.wait_ge(*E.at(f"z{j}", i))
                        if j:
                            dve.wait_ge(*V.at(f"im{j - 1}", i))
                        nc.vector.tensor_tensor(part[0][:, :], zc, kre[:, j, :], ALU.mult).then_inc(*V.done(f"a{j}"))
                        nc.vector.tensor_tensor(part[1][:, :], zs, kim[:, j, :], ALU.mult).then_inc(*V.done(f"b{j}"))
                        dve.wait_ge(*V.at(f"b{j}", i))
                        nc.vector.tensor_tensor(yre[:, j, :], part[0][:, :], part[1][:, :], ALU.add)\
                            .then_inc(*V.done(f"re{j}"))
                        dve.wait_ge(*V.at(f"re{j}", i))
                        nc.vector.tensor_tensor(part[0][:, :], zs, kre[:, j, :], ALU.mult).then_inc(*V.done(f"c{j}"))
                        nc.vector.tensor_tensor(part[1][:, :], zc, kim[:, j, :], ALU.mult).then_inc(*V.done(f"d{j}"))
                        dve.wait_ge(*V.at(f"d{j}", i))
                        nc.vector.tensor_tensor(yim[:, j, :], part[0][:, :], part[1][:, :], ALU.subtract)\
                            .then_inc(*V.done(f"im{j}"))
                    for m in range(N):
                        dve.wait_ge(*E.at(f"y{m}", i))
                        z = u[:, 2 * N + m, :]
                        nc.vector.scalar_tensor_tensor(z, z, c.vec[:, ds(i * N + VCOL["hy_bias_d_2.0"] + m, 1)],
                                                       ps[:, 4 + m % 2, :], ALU.mult, ALU.add)\
                            .then_inc(*V.done(f"dz{m}"))
                        dve.wait_ge(*V.at(f"dz{m}", i))
                        nc.vector.tensor_tensor(z, z, tile_of(u, i * N + m), ALU.mult).then_inc(*V.done(f"z{m}"))



def shifted(c, x, u):
    nc = c.nc
    with scope(c) as sb:
        mid = sb("rw_mid", [P, 16])
        M = steps(c, "rw_mid_dve", ["sum", "mid"])
        with nc.Block() as block:
            @block.vector
            def _(dve):
                M.start(dve)
                nc.vector.tensor_tensor(mid[:, :], vcol(c, "rw_mu_2.0", 0, 16), vcol(c, "rw_mu_2.1", 0, 16), ALU.add)\
                    .then_inc(*M.done("sum"))
                dve.wait_ge(*M.at("sum"))
                nc.vector.tensor_scalar(mid[:, :], mid[:, :], -1.0, 1.0, ALU.mult, ALU.add).then_inc(*M.done("mid"))
        three_taps(c, "rw_taps", 4, x, u, vec_at(c, "rw_mu_2.0"), lambda k: mid[:, ds(k, 1)], vec_at(c, "rw_mu_2.1"))


NORM_EPS7 = 64e-5
GATE_LORA = 160
RATE = -float(np.exp(-0.5))


def rwkv7(c, u, out):
    nc, ps, io = c.nc, c.ps, c.io
    NCH = T // C7
    HP = DR // P
    levels = list(doubling(C7))
    NL = len(levels)
    with scope(c) as sb:
        lora = sb("rw_lora", [P, 4, DR])
        fix = sb("rw_fix", [P, 4, P])
        mask = sb("rw_mask", [P, 2, 3 + NL, P])
        pair1 = sb("rw_pair1", [P, P])
        resets = sb("rw_resets", [P, T])
        gn_eps = sb("rw_gn_eps", [P, 1])
        prm = sb("rw_prm", [P, 9])
        AR = [sb(f"rw_AR{d}", [P, NCH, 2 * P]) for d in range(2)]
        Bm = [sb(f"rw_B{d}", [P, NCH, P]) for d in range(2)]
        Km = [sb(f"rw_K{d}", [P, NCH, P]) for d in range(2)]
        XT = [sb(f"rw_XT{d}", [P, NCH, P]) for d in range(2)]
        PT = [sb(f"rw_PT{d}", [P, NCH, P]) for d in range(2)]
        MV = [sb(f"rw_MV{d}", [P, NCH, C7]) for d in range(2)]
        LT, X, CT0, Y = (sb(f"rw_{n}", [P, 4, P]) for n in ("LT", "X", "CT", "Y"))
        vt = sb("rw_vt", [P, NCH, C7])
        ysum = sb("rw_ysum", [P, NCH, C7])
        half = sb("rw_half", [P, 2, NCH])
        fac = sb("rw_fac", [P, 2, NCH])
        nkk, t1, t2, t3, av = (sb(f"rw_{n}", [P, T]) for n in ("nkk", "t1", "t2", "t3", "av"))
        ksum = sb("rw_ksum", [P, T])
        Y2 = sb("rw_eB", [P, T])
        MT, QT, CT1 = (b[:, :].rearrange("p (n t) -> p n t", n=4) for b in (t3, av, t2))
        CTs = (CT0, CT1)
        vcp = LT[:, :, :].rearrange("p n t -> p (n t)")
        tot = sb("rw_tot", [P, 2, NCH])
        Zs = sb("rw_Zs", [P, 2, C7])
        US = sb("rw_US", [P, 2, C7])
        ST = sb("rw_ST", [P, 2, C7])
        S1 = sb("rw_S1", [P, 2, C7])
        st = sb("rw_stats", [P, 3, NCH])
        loaded = c.scopes[-1].enter_context(nc.semaphore("rw_loaded"))

        def chunks(buf):
            return buf[:, :].rearrange("p (n t) -> p n t", n=NCH)

        def both(bank):
            return ps[:, bank:bank + 2, :].rearrange("p b (n t) -> p (b n) t", n=2)

        def cur2(buf, k):
            return buf[:, ds(k, 1), :].rearrange("p a t -> p (a t)")

        def cur(k):
            return cur2(u, k)

        quads = [(d, z) for d in range(2) for z in range(2)]
        e_steps, a_steps, v_steps, q_steps = [], [], [], ["fix", "prm"]
        e_steps += ["kk"] + [f"{w}{d}" for d in range(2) for w in ("w", "a")] + ["vt"]
        for d, z in quads:
            e_steps += [f"{w}{d}{z}" for w in ("BA", "KA", "tB", "tK", "tX", "V")]
            e_steps += [f"{w}{l}{d}{z}{a}" for l in range(NL) for w in ("Y", "Z") for a in range(2)]
        e_steps += [f"{w}{n}" for n in range(NCH) for w in ("z", "U", "dS", "y")] + ["bonus", "g", "turn"]
        a_steps += ["kk2", "log", "norm"]
        for d in range(2):
            a_steps += [f"{w}{d}" for w in ("sw", "sa", "eB", "eR", "eA", "half")]
        a_steps += ["vt"]
        for d, z in quads:
            a_steps += [f"{w}{d}{z}" for w in ("LT", "tB", "tK", "X", "V")]
            a_steps += [f"Y{l}{d}{z}{a}" for l in range(NL) for a in range(2)]
        a_steps += [f"U{n}" for n in range(NCH)] + ["ysq", "ylog", "yrs", "g"]
        v_steps += ["kk", "vcopy", "floor", "nkk"]
        for d in range(2):
            v_steps += [f"{w}{d}" for w in ("scan", "tot", "u1", "u2", "ka", "b", "kdir", "ks", "B0", "B1", "K0", "K1",
                                            "R0", "R1", "A0", "A1")]
        v_steps += ["fac", "state"]
        for d, z in quads:
            v_steps += [f"{w}{d}{z}" for w in ("off", "XT", "PT", "MT", "QT", "ysum")]
            v_steps += [f"{w}{l}{d}{z}{a}" for l in range(NL) for a in range(2)
                        for w in (("X", "XT") if l < NL - 1 else ("XT",))]
        v_steps += [x for n in range(NCH) for x in (f"Z0{n}", f"Z1{n}", f"f0{n}", f"f1{n}", f"Sf{n}", f"Sb{n}", f"yf{n}", f"yb{n}")]
        v_steps += ["sum", "mean", "centred", "var", "normed", "bonus1", "bonus2", "lnw", "plus", "out"]
        for d, z in quads:
            q_steps += [f"CT{l}{d}{z}" for l in range(NL)]
        E, A = steps(c, "rw_pe", e_steps), steps(c, "rw_act", a_steps)
        V, Q = steps(c, "rw_dve", v_steps), steps(c, "rw_pool", q_steps)
        PRM = [("rw_w0_2.0", 0), ("rw_w0_2.1", 1), ("rw_a0_2.0", 2), ("rw_a0_2.1", 3), ("rw_k_k_2", 4),
               ("rw_k_a_2", 5), ("rw_r_k_2", 6), ("rw_ln_w_2", 7), ("rw_ln_b_2", 8)]
        with nc.Block() as block:
            @block.sync
            def _(sp):
                sp.dma_start(lora[:, :, :], io["rw_lora"]).then_inc(loaded, 16)
                sp.dma_start(mask[:, :, :, :], io["rw_masks"]).then_inc(loaded, 16)
                sp.dma_start(pair1[:, :], io["rw_pair"]).then_inc(loaded, 16)
                sp.dma_start(resets[:, :], io["rw_resets"].partition_broadcast(P)).then_inc(loaded, 16)
                sp.wait_ge(loaded, 64)

            @block.gpsimd
            def _(pool):
                for d in range(2):
                    nc.gpsimd.memset(AR[d][:, :, :], 0.0)
                    nc.gpsimd.memset(Bm[d][:, :, :], 0.0)
                    nc.gpsimd.memset(Km[d][:, :, :], 0.0)
                nc.gpsimd.memset(gn_eps[:, :], NORM_EPS7)

            @block.scalar
            def _(act):
                nc.scalar.activation(u[:, 12, :], u[:, 12, :], ACT.Tanh)
                nc.scalar.activation(u[:, 14:16, :], u[:, 14:16, :], ACT.Sigmoid)

        with nc.Block() as block:
            @block.gpsimd
            def _(pool):
                Q.start(pool)
                with pool.Fori(0, HP) as i:
                    pool.wait_ge(*E.at("g", i - 1))
                    nc.gpsimd.tensor_copy(fix[:, :, :], lora[:, :, ds(i * P, P)]).then_inc(*Q.done("fix"))
                    pool.wait_ge(*V.at("out", i - 1))
                    for name, at in PRM:
                        last = nc.gpsimd.tensor_copy(prm[:, at:at + 1], c.vec[:, ds(i + VCOL[name], 1)])
                    last.then_inc(*Q.done("prm"))
                    for q, (d, z) in enumerate(quads):
                        for l in range(NL):
                            if l == 0:
                                pool.wait_ge(*A.at(f"LT{d}{z}", i))
                            if l >= 2:
                                pool.wait_ge(*E.at(f"Y{l - 2}{d}{z}1", i))
                            elif q:
                                pool.wait_ge(*E.at("Y%d%d%d1" % (NL - 2 + l, *quads[q - 1]), i))
                            nc.gpsimd.tensor_tensor(CTs[(q * NL + l) % 2][:, :, :], LT[:, :, :],
                                                    mask[:, d, 3 + l, :][:, None, :].to_broadcast([P, 4, P]),
                                                    ALU.mult).then_inc(*Q.done(f"CT{l}{d}{z}"))

            @block.scalar
            def _(act):
                A.start(act)
                nc.scalar.preload_act_table_set(LOG_EXP)
                with act.Fori(0, HP) as i:
                    act.wait_ge(*V.at("kk", i))
                    nc.scalar.activation(t2[:, :], t1[:, :], ACT.Square).then_inc(*A.done("kk2"))
                    act.wait_ge(*V.at("floor", i))
                    nc.scalar.activation(t2[:, :], t2[:, :], ACT.Ln).then_inc(*A.done("log"))
                    act.wait_ge(*A.at("log", i))
                    nc.scalar.activation(t2[:, :], t2[:, :], ACT.Exp, scale=-0.5).then_inc(*A.done("norm"))
                    for d in range(2):
                        act.wait_ge(*E.at(f"a{d}", i))
                        act.wait_ge(*V.at("nkk" if d == 0 else "A10", i))
                        nc.scalar.activation(t1[:, :], ps[:, 1, :], ACT.Sigmoid, bias=prm[:, d:d + 1])\
                            .then_inc(*A.done(f"sw{d}"))
                        nc.scalar.activation(av[:, :], ps[:, 2, :], ACT.Sigmoid, bias=prm[:, 2 + d:3 + d])\
                            .then_inc(*A.done(f"sa{d}"))
                        g1, g2 = (t2, t1) if d == 0 else (t1, t2)
                        s = 1.0 if d == 0 else -1.0
                        nc.scalar.preload_act_table_set(LOG_EXP)
                        act.wait_ge(*V.at(f"u2{d}", i))
                        nc.scalar.activation(Y2[:, :], g1[:, :], ACT.Exp, scale=-s * RATE).then_inc(*A.done(f"eB{d}"))
                        act.wait_ge(*A.at(f"eB{d}", i))
                        nc.scalar.activation(g1[:, :], g1[:, :], ACT.Exp, scale=s * RATE).then_inc(*A.done(f"eR{d}"))
                        nc.scalar.activation(g2[:, :], g2[:, :], ACT.Exp, scale=s * RATE).then_inc(*A.done(f"eA{d}"))
                        nc.scalar.activation(half[:, d, :], tot[:, d, :], ACT.Exp, scale=RATE / 2)\
                            .then_inc(*A.done(f"half{d}"))
                    act.wait_ge(*E.at("vt", i))
                    nc.scalar.activation(vt[:, :, :].rearrange("p n e -> p (n e)"), ps[:, 3, :], ACT.Copy)\
                        .then_inc(*A.done("vt"))
                    for n, (d, z) in enumerate(quads):
                        four = slice(4 * z, 4 * z + 4)
                        if n == 0:
                            act.wait_ge(*V.at("A11", i))
                        else:
                            act.wait_ge(*Q.at("CT%d%d%d" % (NL - 1, *quads[n - 1]), i))
                        act.wait_ge(*E.at(f"BA{d}{z}", i))
                        nc.scalar.activation(LT[:, :, :], both(0)[:, :, 0:P], ACT.Copy).then_inc(*A.done(f"LT{d}{z}"))
                        act.wait_ge(*E.at(f"tB{d}{z}", i))
                        nc.scalar.activation(Bm[d][:, four, :], ps[:, 4, :].rearrange("p (n t) -> p n t", n=4),
                                             ACT.Copy).then_inc(*A.done(f"tB{d}{z}"))
                        act.wait_ge(*E.at(f"tK{d}{z}", i))
                        nc.scalar.activation(Km[d][:, four, :], ps[:, 5, :].rearrange("p (n t) -> p n t", n=4),
                                             ACT.Copy).then_inc(*A.done(f"tK{d}{z}"))
                        act.wait_ge(*E.at(f"tX{d}{z}", i))
                        nc.scalar.activation(X[:, :, :], ps[:, 7, :].rearrange("p (n t) -> p n t", n=4), ACT.Copy)\
                            .then_inc(*A.done(f"X{d}{z}"))
                        act.wait_ge(*E.at(f"V{d}{z}", i))
                        nc.scalar.activation(MV[d][:, four, :],
                                             ps[:, 6, 0:4 * C7].rearrange("p (n e) -> p n e", n=4), ACT.Copy)\
                            .then_inc(*A.done(f"V{d}{z}"))
                        for l in range(NL):
                            for a in range(2):
                                act.wait_ge(*E.at(f"Y{l}{d}{z}{a}", i))
                                nc.scalar.activation(Y[:, 2 * a:2 * a + 2, :],
                                                     ps[:, 4 + a, 0:2 * P].rearrange("p (n t) -> p n t", n=2),
                                                     ACT.Copy).then_inc(*A.done(f"Y{l}{d}{z}{a}"))
                    for n in range(NCH):
                        act.wait_ge(*E.at(f"U{n}", i))
                        nc.scalar.activation(US[:, :, :].rearrange("p d e -> p (d e)"), ps[:, 1, 0:2 * C7], ACT.Copy)\
                            .then_inc(*A.done(f"U{n}"))
                    act.wait_ge(*V.at("centred", i))
                    nc.scalar.activation(t1[:, :], ysum[:, :, :].rearrange("p n e -> p (n e)"), ACT.Square)\
                        .then_inc(*A.done("ysq"))
                    act.wait_ge(*V.at("var", i))
                    nc.scalar.activation(st[:, 1, :], st[:, 1, :], ACT.Ln, bias=gn_eps[:, :], scale=1.0 / C7)\
                        .then_inc(*A.done("ylog"))
                    act.wait_ge(*A.at("ylog", i))
                    nc.scalar.activation(st[:, 2, :], st[:, 1, :], ACT.Exp, scale=-0.5).then_inc(*A.done("yrs"))
                    act.wait_ge(*E.at("g", i))
                    act.wait_ge(*V.at("nkk", i))
                    nc.scalar.activation(nkk[:, :], ps[:, 7, :], ACT.Copy).then_inc(*A.done("g"))

            @block.vector
            def _(dve):
                V.start(dve)
                with dve.Fori(0, HP) as i:
                    r_, k_, v_ = cur(i), cur(i + HP), cur(i + 2 * HP)
                    dve.wait_ge(*Q.at("prm", i))
                    dve.wait_ge(*A.at("ysq", i - 1))
                    nc.vector.tensor_scalar(t1[:, :], k_, prm[:, 4:5], None, ALU.mult).then_inc(*V.done("kk"))
                    nc.vector.tensor_copy(vcp, v_).then_inc(*V.done("vcopy"))
                    dve.wait_ge(*E.at("kk", i))
                    nc.vector.tensor_scalar(t2[:, :], ps[:, 0, :], 1e-24, None, ALU.max).then_inc(*V.done("floor"))
                    dve.wait_ge(*A.at("norm", i))
                    nc.vector.scalar_tensor_tensor(nkk[:, :], t1[:, :], -1.0, t2[:, :], ALU.mult, ALU.mult)\
                        .then_inc(*V.done("nkk"))
                    for d in range(2):
                        dve.wait_ge(*A.at(f"sa{d}", i))
                        if d:
                            dve.wait_ge(*V.at("R10", i))
                        nc.vector.tensor_tensor_scan(t2[:, :], resets[:, :], t1[:, :], 0.0, ALU.mult, ALU.add)\
                            .then_inc(*V.done(f"scan{d}"))
                        dve.wait_ge(*V.at(f"scan{d}", i))
                        if d == 0:
                            dve.wait_ge(*V.at("fac", i - 1))
                        nc.vector.tensor_copy(tot[:, d, :, None], chunks(t2)[:, :, C7 - 1:C7]).then_inc(*V.done(f"tot{d}"))
                        dve.wait_ge(*V.at(f"tot{d}", i))
                        nc.vector.scalar_tensor_tensor(chunks(t2), tot[:, d, :, None].to_broadcast([P, NCH, C7]), -0.5,
                                                       chunks(t2), ALU.mult, ALU.add).then_inc(*V.done(f"u1{d}"))
                        dve.wait_ge(*V.at(f"u1{d}", i))
                        nc.vector.tensor_tensor(t1[:, :], t2[:, :], t1[:, :], ALU.subtract).then_inc(*V.done(f"u2{d}"))
                        nc.vector.tensor_scalar(t3[:, :], av[:, :], -1.0, prm[:, 5:6], ALU.add, ALU.mult)\
                            .then_inc(*V.done(f"ka{d}"))
                        dve.wait_ge(*V.at(f"ka{d}", i))
                        nc.vector.scalar_tensor_tensor(av[:, :], nkk[:, :], -1.0, av[:, :], ALU.mult, ALU.mult)\
                            .then_inc(*V.done(f"b{d}"))
                        nc.vector.scalar_tensor_tensor(t3[:, :], t3[:, :], 1.0, k_, ALU.add, ALU.mult)\
                            .then_inc(*V.done(f"kdir{d}"))
                        dve.wait_ge(*V.at(f"kdir{d}", i))
                        if d == 0:
                            nc.vector.tensor_copy(ksum[:, :], t3[:, :]).then_inc(*V.done("ks0"))
                        else:
                            nc.vector.tensor_tensor(ksum[:, :], ksum[:, :], t3[:, :], ALU.add).then_inc(*V.done("ks1"))
                        dve.wait_ge(*E.at(f"dS{NCH - 1}", i - 1))
                        dve.wait_ge(*A.at(f"eB{d}", i))
                        g1, g2 = (t2, t1) if d == 0 else (t1, t2)
                        for w, dst, x, y, at in (("B", Bm[d], av, Y2, 0), ("K", Km[d], t3, Y2, 0),
                                                 ("R", AR[d], r_, g1, P), ("A", AR[d], nkk, g2, 0)):
                            if w == "R":
                                dve.wait_ge(*A.at(f"eR{d}", i))
                                dve.wait_ge(*E.at(f"y{NCH - 1}", i - 1))
                            if w == "A":
                                dve.wait_ge(*A.at(f"eA{d}", i))
                            x = x if w == "R" else x[:, :]
                            for hh in range(2):
                                rows = slice(hh * C7, (hh + 1) * C7)
                                nc.vector.tensor_tensor(
                                    dst[rows, :, at + hh * C7:at + (hh + 1) * C7],
                                    x[rows].rearrange("p (n t) -> p n t", n=NCH), chunks(y)[rows], ALU.mult)\
                                    .then_inc(*V.done(f"{w}{hh}{d}"))
                    dve.wait_ge(*A.at("half1", i))
                    nc.vector.tensor_tensor(fac[:, 0, 0:NCH - 1], half[:, 0, 0:NCH - 1], half[:, 0, 1:], ALU.mult)
                    nc.vector.tensor_tensor(fac[:, 1, 1:], half[:, 1, 1:], half[:, 1, 0:NCH - 1], ALU.mult)\
                        .then_inc(*V.done("fac"))
                    nc.vector.memset(ST[:, :, :], 0.0).then_inc(*V.done("state"))
                    for d, z in quads:
                        four = slice(4 * z, 4 * z + 4)
                        strict = mask[:, d, 0, :][:, None, :].to_broadcast([P, 4, P])
                        incl = mask[:, d, 1, :][:, None, :].to_broadcast([P, 4, P])
                        first2 = mask[:, d, 2, :][:, None, :].to_broadcast([P, 4, P])
                        dve.wait_ge(*A.at(f"LT{d}{z}", i))
                        xt = XT[d][:, four, :]
                        nc.vector.tensor_tensor(xt, LT[:, :, :], first2, ALU.mult).then_inc(*V.done(f"off{d}{z}"))
                        dve.wait_ge(*V.at(f"off{d}{z}", i))
                        nc.vector.tensor_tensor(xt, xt, c.ident[:, None, :].to_broadcast([P, 4, P]), ALU.add)\
                            .then_inc(*V.done(f"XT{d}{z}"))
                        nc.vector.tensor_tensor(PT[d][:, four, :], both(0)[:, :, P:], incl, ALU.mult)\
                            .then_inc(*V.done(f"PT{d}{z}"))
                        dve.wait_ge(*E.at(f"KA{d}{z}", i))
                        nc.vector.tensor_tensor(MT, both(2)[:, :, 0:P], strict, ALU.mult)\
                            .then_inc(*V.done(f"MT{d}{z}"))
                        nc.vector.tensor_tensor(QT, both(2)[:, :, P:], incl, ALU.mult)\
                            .then_inc(*V.done(f"QT{d}{z}"))
                        dve.wait_ge(*A.at(f"V{d}{z}", i))
                        qv = ps[:, 6, 4 * C7:8 * C7].rearrange("p (n e) -> p n e", n=4)
                        if d == 0:
                            nc.vector.tensor_copy(ysum[:, four, :], qv).then_inc(*V.done(f"ysum{d}{z}"))
                        else:
                            nc.vector.tensor_tensor(ysum[:, four, :], ysum[:, four, :], qv, ALU.add)\
                                .then_inc(*V.done(f"ysum{d}{z}"))
                        for l in range(NL):
                            for a in range(2):
                                dve.wait_ge(*E.at(f"Z{l}{d}{z}{a}", i))
                                two = slice(2 * a, 2 * a + 2)
                                zz = ps[:, 6 + a, :].rearrange("p (w n t) -> p w n t", w=2, n=2)
                                if l < NL - 1:
                                    nc.vector.tensor_tensor(X[:, two, :], X[:, two, :], zz[:, 0], ALU.add)\
                                        .then_inc(*V.done(f"X{l}{d}{z}{a}"))
                                xa = XT[d][:, 4 * z + 2 * a:4 * z + 2 * a + 2, :]
                                nc.vector.tensor_tensor(xa, xa, zz[:, 1], ALU.add)\
                                    .then_inc(*V.done(f"XT{l}{d}{z}{a}"))
                    for n in range(NCH):
                        at = (n, NCH - 1 - n)
                        if n:
                            dve.wait_ge(*V.at(f"Sb{n - 1}", i))
                        dve.wait_ge(*E.at(f"z{n}", i))
                        for d in range(2):
                            nc.vector.tensor_tensor(Zs[:, d, :], MV[d][:, at[d], :], ps[:, 0, d * C7:(d + 1) * C7],
                                                    ALU.add).then_inc(*V.done(f"Z{d}{n}"))
                        f = [fac[:, d, at[d]:at[d] + 1] if n < NCH - 1 else 0.0 for d in range(2)]
                        for d in range(2):
                            nc.vector.tensor_scalar(S1[:, d, :], ST[:, d, :], f[d], None, ALU.mult)\
                                .then_inc(*V.done(f"f{d}{n}"))
                        dve.wait_ge(*V.at(f"f1{n}", i))
                        dve.wait_ge(*E.at(f"dS{n}", i))
                        for d in range(2):
                            nc.vector.scalar_tensor_tensor(ST[:, d, :], ps[:, 2 + d, 0:C7], f[d], S1[:, d, :],
                                                           ALU.mult, ALU.add).then_inc(*V.done(f"S{'fb'[d]}{n}"))
                        dve.wait_ge(*E.at(f"y{n}", i))
                        for d in range(2):
                            nc.vector.tensor_tensor(ysum[:, at[d], :], ysum[:, at[d], :], ps[:, 4 + d, 0:C7], ALU.add)\
                                .then_inc(*V.done(f"y{'fb'[d]}{n}"))
                            if d == 0:
                                dve.wait_ge(*V.at(f"yf{n}", i))
                    dve.wait_ge(*V.at(f"yb{NCH - 1}", i))
                    nc.vector.tensor_reduce(st[:, 0, :], ysum[:, :, :], AX.X, ALU.add).then_inc(*V.done("sum"))
                    dve.wait_ge(*V.at("sum", i))
                    nc.vector.tensor_scalar(st[:, 0, :], st[:, 0, :], 1.0 / C7, None, ALU.mult)\
                        .then_inc(*V.done("mean"))
                    dve.wait_ge(*V.at("mean", i))
                    nc.vector.tensor_tensor(ysum[:, :, :], ysum[:, :, :],
                                            st[:, 0, :, None].to_broadcast([P, NCH, C7]), ALU.subtract)\
                        .then_inc(*V.done("centred"))
                    dve.wait_ge(*A.at("ysq", i))
                    nc.vector.tensor_reduce(st[:, 1, :], chunks(t1), AX.X, ALU.add).then_inc(*V.done("var"))
                    dve.wait_ge(*A.at("yrs", i))
                    nc.vector.tensor_tensor(ysum[:, :, :], ysum[:, :, :],
                                            st[:, 2, :, None].to_broadcast([P, NCH, C7]), ALU.mult)\
                        .then_inc(*V.done("normed"))
                    nc.vector.scalar_tensor_tensor(t2[:, :], r_, prm[:, 6:7], ksum[:, :], ALU.mult, ALU.mult)\
                        .then_inc(*V.done("bonus1"))
                    dve.wait_ge(*E.at("bonus", i))
                    nc.vector.tensor_tensor(t2[:, :], v_, ps[:, 6, :], ALU.mult).then_inc(*V.done("bonus2"))
                    dve.wait_ge(*E.at("turn", i))
                    nc.vector.tensor_scalar(t3[:, :], ps[:, 5, :], prm[:, 7:8], prm[:, 8:9], ALU.mult, ALU.add)\
                        .then_inc(*V.done("lnw"))
                    dve.wait_ge(*V.at("lnw", i))
                    nc.vector.tensor_tensor(t3[:, :], t3[:, :], t2[:, :], ALU.add).then_inc(*V.done("plus"))
                    dve.wait_ge(*V.at("plus", i))
                    dve.wait_ge(*A.at("g", i))
                    nc.vector.tensor_tensor(cur2(out, i), t3[:, :], nkk[:, :], ALU.mult).then_inc(*V.done("out"))

            @block.tensor
            def _(pe):
                E.start(pe)
                with pe.Fori(0, HP) as i:
                    pe.wait_ge(*V.at("out", i - 1))
                    pe.wait_ge(*V.at("vcopy", i))
                    pe.wait_ge(*A.at("kk2", i))
                    nc.tensor.matmul(ps[:, 0, :], pair1[:, :], t2[:, :], start=True, stop=True).then_inc(*E.done("kk"))
                    for d in range(2):
                        pe.wait_ge(*Q.at("fix", i))
                        if d:
                            pe.wait_ge(*A.at("sa0", i))
                        rows = slice(d * C7, (d + 1) * C7)
                        nc.tensor.matmul(ps[:, 1, :], fix[rows, 0, :], u[rows, 12, :], start=True, stop=True)\
                            .then_inc(*E.done(f"w{d}"))
                        nc.tensor.matmul(ps[:, 2, :], fix[rows, 1, :], u[rows, 13, :], start=True, stop=True)\
                            .then_inc(*E.done(f"a{d}"))
                    for n in range(NCH):
                        for hh in range(2):
                            rows = slice(hh * C7, (hh + 1) * C7)
                            last = nc.tensor.matmul(ps[rows, 3, n * C7:(n + 1) * C7], vcp[rows, n * C7:(n + 1) * C7],
                                                    c.ident[rows, rows], start=True, stop=True)
                    last.then_inc(*E.done("vt"))
                    pe.wait_ge(*V.at("A11", i))
                    pe.wait_ge(*A.at("vt", i))
                    for q, (d, z) in enumerate(quads):
                        for m in range(4):
                            last = nc.tensor.matmul(both(0)[:, m, :], Bm[d][:, 4 * z + m, :], AR[d][:, 4 * z + m, :],
                                                    start=True, stop=True)
                        last.then_inc(*E.done(f"BA{d}{z}"))
                        for m in range(4):
                            last = nc.tensor.matmul(both(2)[:, m, :], Km[d][:, 4 * z + m, :], AR[d][:, 4 * z + m, :],
                                                    start=True, stop=True)
                        last.then_inc(*E.done(f"KA{d}{z}"))
                        for m in range(4):
                            last = nc.tensor.transpose(ps[:, 4, m * P:(m + 1) * P], Bm[d][:, 4 * z + m, :], c.ident[:, :])
                        last.then_inc(*E.done(f"tB{d}{z}"))
                        for m in range(4):
                            last = nc.tensor.transpose(ps[:, 5, m * P:(m + 1) * P], Km[d][:, 4 * z + m, :], c.ident[:, :])
                        last.then_inc(*E.done(f"tK{d}{z}"))
                        pe.wait_ge(*V.at(f"XT{d}{z}", i))
                        for m in range(4):
                            last = nc.tensor.transpose(ps[:, 7, m * P:(m + 1) * P], XT[d][:, 4 * z + m, :], c.ident[:, :])
                        last.then_inc(*E.done(f"tX{d}{z}"))
                        pe.wait_ge(*V.at(f"QT{d}{z}", i))
                        for m in range(4):
                            nc.tensor.matmul(ps[:, 6, m * C7:(m + 1) * C7], MT[:, m, :], vt[:, 4 * z + m, :],
                                             start=True, stop=True)
                            last = nc.tensor.matmul(ps[:, 6, (4 + m) * C7:(5 + m) * C7], QT[:, m, :],
                                                    vt[:, 4 * z + m, :], start=True, stop=True)
                        last.then_inc(*E.done(f"V{d}{z}"))
                        pe.wait_ge(*A.at(f"X{d}{z}", i))
                        for l in range(NL):
                            CT = CTs[(q * NL + l) % 2]
                            pe.wait_ge(*Q.at(f"CT{l}{d}{z}", i))
                            for a in range(2):
                                if l:
                                    pe.wait_ge(*V.at(f"X{l - 1}{d}{z}{a}", i))
                                for m in range(2):
                                    last = nc.tensor.matmul(ps[:, 4 + a, m * P:(m + 1) * P], CT[:, 2 * a + m, :],
                                                            X[:, 2 * a + m, :], start=True, stop=True)
                                last.then_inc(*E.done(f"Y{l}{d}{z}{a}"))
                            if l == 0:
                                pe.wait_ge(*V.at(f"ysum{d}{z}", i))
                            for a in range(2):
                                pe.wait_ge(*A.at(f"Y{l}{d}{z}{a}", i))
                                if l:
                                    pe.wait_ge(*V.at(f"XT{l - 1}{d}{z}{a}", i))
                                for m in range(2):
                                    xt = XT[d][:, 4 * z + 2 * a + m, :]
                                    if l < NL - 1:
                                        nc.tensor.matmul(ps[:, 6 + a, m * P:(m + 1) * P], xt, Y[:, 2 * a + m, :],
                                                         start=True, stop=True)
                                    last = nc.tensor.matmul(ps[:, 6 + a, (2 + m) * P:(3 + m) * P], Y[:, 2 * a + m, :],
                                                            xt, start=True, stop=True)
                                last.then_inc(*E.done(f"Z{l}{d}{z}{a}"))
                    pe.wait_ge(*V.at("XT%d111" % (NL - 1), i))
                    for n in range(NCH):
                        at = (n, NCH - 1 - n)
                        if n:
                            pe.wait_ge(*V.at(f"Sb{n - 1}", i))
                        for d in range(2):
                            last = nc.tensor.matmul(ps[:, 0, d * C7:(d + 1) * C7], AR[d][:, at[d], 0:P], ST[:, d, :],
                                                    start=True, stop=True)
                        last.then_inc(*E.done(f"z{n}"))
                        for d in range(2):
                            nc.tensor.matmul(ps[:, 2 + d, 0:C7], Km[d][:, at[d], :], vt[:, at[d], :],
                                             start=True, stop=False)
                        if n:
                            pe.wait_ge(*V.at(f"yb{n - 1}", i))
                        pe.wait_ge(*V.at(f"Z1{n}", i))
                        for d in range(2):
                            last = nc.tensor.matmul(ps[:, 1, d * C7:(d + 1) * C7], XT[d][:, at[d], :], Zs[:, d, :],
                                                    start=True, stop=True)
                        last.then_inc(*E.done(f"U{n}"))
                        for d in range(2):
                            nc.tensor.matmul(ps[:, 4 + d, 0:C7], AR[d][:, at[d], P:], ST[:, d, :],
                                             start=True, stop=False)
                        pe.wait_ge(*A.at(f"U{n}", i))
                        for d in range(2):
                            last = nc.tensor.matmul(ps[:, 2 + d, 0:C7], Bm[d][:, at[d], :], US[:, d, :],
                                                    start=False, stop=True)
                        last.then_inc(*E.done(f"dS{n}"))
                        for d in range(2):
                            last = nc.tensor.matmul(ps[:, 4 + d, 0:C7], PT[d][:, at[d], :], US[:, d, :],
                                                    start=False, stop=True)
                        last.then_inc(*E.done(f"y{n}"))
                    pe.wait_ge(*V.at("bonus1", i))
                    nc.tensor.matmul(ps[:, 6, :], pair1[:, :], t2[:, :], start=True, stop=True)\
                        .then_inc(*E.done("bonus"))
                    nc.tensor.matmul(ps[:, 7, :], fix[:, 2, :], u[:, 14, :], start=True, stop=False)
                    nc.tensor.matmul(ps[:, 7, :], fix[0:GATE_LORA - P, 3, :], u[0:GATE_LORA - P, 15, :],
                                     start=False, stop=True).then_inc(*E.done("g"))
                    for n in range(NCH):
                        for hh in range(2):
                            rows = slice(hh * C7, (hh + 1) * C7)
                            last = nc.tensor.matmul(ps[rows, 5, n * C7:(n + 1) * C7], ysum[rows, n, :],
                                                    c.ident[rows, rows], start=True, stop=True)
                    last.then_inc(*E.done("turn"))



def split_into(c, name, x, hi, lo):
    A = steps(c, f"{name}_act", ["hi"])
    with c.nc.Block() as block:
        @block.scalar
        def _(act):
            A.start(act)
            c.nc.scalar.activation(hi, x, ACT.Copy).then_inc(*A.done("hi"))

        @block.vector
        def _(dve):
            dve.wait_ge(*A.at("hi"))
            c.nc.vector.tensor_tensor(lo, x, hi.bitcast(F32), ALU.subtract)


def second_mixer(c):
    nc, ps = c.nc, c.ps
    N = DR // P
    with scope(c) as sb:
        hz = sb("hy_z", [P, N, T])
        H = steps(c, "hy_kept_act", [f"kept{m}" for m in range(N)])
        with scope(c) as sb2:
            u = sb2("hy_u", [P, 3 * N, T])
            with scope(c) as sb3:
                xh, xl = sb3("hy_xh", [P, KD, T], F32R), sb3("hy_xl", [P, KD, T], F32R)
                norm(c, "hy_n", ["mix_norm_2"], [(xh, xl)])
                three_taps(c, "hy_taps", 3, (xh, xl), u, vec_at(c, "hy_conv_w_2.0"), vec_at(c, "hy_conv_w_2.1"),
                           vec_at(c, "hy_conv_w_2.2"), vec_at(c, "hy_conv_b_2"))
            hyena(c, u)
            with nc.Block() as block:
                @block.scalar
                def _(act):
                    H.start(act)
                    for m in range(N):
                        nc.scalar.activation(hz[:, m, :], u[:, 2 * N + m, :], ACT.Copy).then_inc(*H.done(f"kept{m}"))
        u = sb("rw_u", [P, 4 * N, T])
        with scope(c) as sb3:
            xh, xl = sb3("rw_xh", [P, KD, T], F32R), sb3("rw_xl", [P, KD, T], F32R)
            norm(c, "rw_n", ["mix_norm_2"], [(xh, xl)])
            shifted(c, (xh, xl), u)
        rwkv7(c, u, u)
        yh, yl = sb("mix_yh", [P, 2 * N, T], F32R), sb("mix_yl", [P, 2 * N, T], F32R)
        split_into(c, "hy_split", hz[:, :, :], yh[:, 0:N, :], yl[:, 0:N, :])
        split_into(c, "rw_split", u[:, 0:N, :], yh[:, N:, :], yl[:, N:, :])
        gates = u
        mh, ml = sb("mix_mh", [P, KD, T], F32R), sb("mix_ml", [P, KD, T], F32R)
        norm(c, "gate_n", ["mix_norm_2"], [(mh, ml)])
        project(c, "mix_gates", 4, (mh, ml), gates, func=ACT.Sigmoid)
        parts = sb("mix_parts", [P, 3, 2, T])
        A = steps(c, "merge_act", ["hi0", "hi1"])
        V = steps(c, "merge_dve", [f"{w}{t}" for t in range(2) for w in ("hyena", "rwkv", "sum", "lo")])

        def act_evac(act, i, q):
            if q % 2:
                t = q // 2
                act.wait_ge(*V.at(f"sum{t}", i))
                nc.scalar.activation(mh[:, ds(i * 4 + 2 * t, 2), :], parts[:, 2, :, :], ACT.Copy)\
                    .then_inc(*A.done(f"hi{t}"))

        def dve_evac(dve, i, q):
            if q % 2:
                t = q // 2
                at = i * 4 + 2 * t
                if t:
                    dve.wait_ge(*V.at("lo0", i))
                else:
                    dve.wait_ge(*V.at("lo1", i - 1))
                nc.vector.tensor_tensor(parts[:, 0, :, :], gates[:, ds(at, 2), :], ps[:, 0:2, :], ALU.mult)\
                    .then_inc(*V.done(f"hyena{t}"))
                nc.vector.tensor_tensor(parts[:, 1, :, :], gates[:, ds(at + KD, 2), :], ps[:, 2:4, :], ALU.mult)\
                    .then_inc(*V.done(f"rwkv{t}"))
                dve.wait_ge(*V.at(f"rwkv{t}", i))
                nc.vector.tensor_tensor(parts[:, 2, :, :], parts[:, 0, :, :], parts[:, 1, :, :], ALU.add)\
                    .then_inc(*V.done(f"sum{t}"))
                dve.wait_ge(*A.at(f"hi{t}", i))
                nc.vector.tensor_tensor(ml[:, ds(at, 2), :], parts[:, 2, :, :], mh[:, ds(at, 2), :].bitcast(F32),
                                        ALU.subtract).then_inc(*V.done(f"lo{t}"))

        body = [[(2 * t + b, True, True, [(b * N + k, b * N + k) for k in range(N)]) for b in range(2)]
                for t in range(2)]
        dense(c, 2, body, lambda q, k: (yh[:, k, :], yl[:, k, :]), act_evac, dve_evac, A, V,
              [(V, f"{w}{t}") for t in range(2) for w in ("hyena", "rwkv")])
        residual(c, "mix_out", 2, simple(2), lambda q, k: (mh[:, k, :], ml[:, k, :]))


def program(nc, io):
    with ExitStack() as ctx:
        c = allocate(nc, ctx, io)
        prologue(c, io["x"])
        gated_delta(c)
        swiglu(c, "ffn0", "ln_ffn.0")
        per_layer_embedding(c, 0)
        stick_breaking(c)
        swiglu(c, "ffn1", "ln_ffn.1")
        per_layer_embedding(c, 1)
        swiglu(c, "ffn2", "ffn1_norm_2", 0.5)
        second_mixer(c)
        swiglu(c, "ffn3", "ffn2_norm_2", 0.5)
        final = c.sb("final", [P, KD, T])
        stored = ctx.enter_context(nc.semaphore("out_stored"))
        norm(c, "final", ["final_norm_2"], [], keep=final)
        with nc.Block() as block:
            @block.sync
            def _(sp):
                sp.dma_start(io["out"], final[:, :, :]).then_inc(stored, 16)
                sp.wait_ge(stored, 16)


def doubling_masks(n, upper=False, copies=1):
    s, t = np.meshgrid(np.arange(n), np.arange(n), indexing="ij")
    out = []
    size = 1
    while size < n:
        new = (s // (2 * size) == t // (2 * size)) & (s // size < t // size)
        out.append(new.T if upper else new)
        size *= 2
    return [np.kron(np.eye(copies), m).astype(np.float32) for m in out]


def hyena_features():
    pos = np.arange(T, dtype=np.float64)
    ang = 2 * np.pi / T * pos
    bands = np.linspace(1e-4, 15, 16)
    rows = [pos / (T - 1)] + [np.cos(b * ang) for b in bands] + [-np.sin(b * ang) for b in bands]
    return np.stack(rows).astype(np.float32)


def hyena_positions():
    t = -(np.arange(T) / (T - 1)).reshape(T // P, P).T
    return np.concatenate([t, (np.arange(P) > 0)[:, None]], 1).astype(np.float32)


def trig_matrices():
    s, j = np.meshgrid(np.arange(T), np.arange(T), indexing="ij")
    a = 2 * np.pi * ((2 * j + 1) * s % (4 * T)) / (4 * T)
    mats = [np.cos(a), np.sin(a), np.cos(a).T, np.sin(a).T]
    return np.stack([m.reshape(T // P, P, T).transpose(1, 0, 2) for m in mats]).astype(np.float32)


def rwkv_lora(w2, a2, g2):
    lora = np.zeros((P, 4, DR), np.float32)
    lora[:, 0], lora[:, 1] = w2.reshape(P, DR), a2.reshape(P, DR)
    lora[:, 2], lora[:g2.shape[0] - P, 3] = g2[:P], g2[P:]
    return lora


def rwkv_masks(upper):
    strict = np.tri(C7, k=-1).T
    strict, full = (strict.T, np.tri(C7)) if upper else (strict, np.tri(C7).T)
    first = [np.kron(np.eye(2), m).astype(np.float32) for m in (strict, full)]
    return np.stack(first + doubling_masks(C7, upper, 2), 1)


def host_arrays(inputs):
    def of(name):
        base, _, i = name.rpartition(".")
        if base:
            return of(base)[int(i)]
        return np.asarray(inputs[name])

    weights = np.zeros((N_WT, P, WK, WN), np.float32)
    for t, (names, parts) in enumerate(weight_plan()):
        mats = [of(n) for n in names.split("|")]
        for r, col, k, which, rows, cols in parts:
            weights[t, :rows, k, :cols] = mats[which][r:r + rows, col:col + cols]
    vectors = np.zeros((P, N_VEC), np.float32)
    for name, n in VECTORS:
        v = of(name).reshape(-1)
        full = np.zeros(n * P, np.float32)
        full[:v.size] = v
        vectors[:, VCOL[name]:VCOL[name] + n] = full.reshape(n, P).T
    return {
        "weights": weights.reshape(N_WT, P, WT),
        "vectors": vectors,
        "gdn_w_ab": np.ascontiguousarray(
            of("gdn_w_in.0")[:, 4 * DM:].reshape(KD, P, 2 * HEADS).transpose(1, 0, 2)),
        "gdn_ab": np.stack([of("gdn_a_log.0"), of("gdn_dt_bias.0")], 1),
        "gdn_masks": np.stack([np.where(np.tri(P).T > 0, 0, -1e30).astype(np.float32)] + doubling_masks(P), 1),
        "sb_mats": np.stack([np.tri(P, k=-1).T, -np.tri(P, k=-1), -np.ones((P, P))], 1).astype(np.float32),
        "hy_feats": hyena_features(),
        "hy_w1": of("hy_ffn_w1_2"), "hy_w2": of("hy_ffn_w2_2"),
        "hy_cols": np.stack([of("hy_ffn_b1_2"), of("hy_ffn_b2_2"), of("hy_sin_freq_2")], 1),
        "hy_w3": np.concatenate([of("hy_ffn_w3_2"), of("hy_ffn_b3_2")[None]]),
        "hy_decay": of("hy_decay_2").reshape(-1),
        "hy_trig": trig_matrices(), "hy_tpos": hyena_positions(),
        "rw_lora": rwkv_lora(of("rw_w2_2"), of("rw_a2_2"), of("rw_g2_2")),
        "rw_masks": np.stack([rwkv_masks(False), rwkv_masks(True)], 1),
        "rw_pair": np.kron(np.eye(2), np.ones((C7, C7))).astype(np.float32),
        "rw_resets": (np.arange(T) % C7 > 0).astype(np.float32),
        "identity": np.eye(P, dtype=np.float32),
        "x": np.ascontiguousarray(of("x")[0].T.reshape(KD, P, T).transpose(1, 0, 2)),
        "p": np.ascontiguousarray(of("p")[:, 0].transpose(0, 2, 1).reshape(2, 2, P, T).transpose(0, 2, 1, 3)),
    }


def kernel(**inputs):
    import concourse.bacc as _bacc
    from concourse.bass_utils import run_bass_kernel_spmd as _run

    nc = _bacc.Bacc("TRN2", target_bir_lowering=False, num_devices=1)
    arrays, io = {}, {}
    for name, a in host_arrays(inputs).items():
        arrays[f"in_{name}"] = np.ascontiguousarray(a)
        io[name] = nc.dram_tensor(f"in_{name}", a.shape, mybir.dt.float32, kind="ExternalInput").ap()
    io["out"] = nc.dram_tensor("out", (P, KD, T), mybir.dt.float32, kind="ExternalOutput").ap()
    program(nc, io)
    got = _run(nc, [arrays], core_ids=[0]).results[0]["out"]
    return np.ascontiguousarray(got.transpose(2, 1, 0).reshape(1, T, DM))
```
